# Optimizing a Trainium2 kernel written in Bass

```python
import jax, jax.numpy as jnp
from jax import lax
import numpy as np

D_MODEL = 1024
BATCH = 1
SEQ = 1024
DEPTH = 2

CHUNK = 64
EXPAND = 2
D_INNER = EXPAND * D_MODEL
POOL_WINDOWS = (2, 4, 8, 16)
N_POOL_GROUPS = len(POOL_WINDOWS)
POOL_GROUP = D_INNER // N_POOL_GROUPS
HGRN_HEAD_DIM = 128
HGRN_HEADS = D_INNER // HGRN_HEAD_DIM
N_MIXERS = 2
N_POOL_LAYERS = (DEPTH + 1) // 2
N_HGRN_LAYERS = DEPTH // 2
EPS = 1e-6


def rms_norm(x, g):
    xf = x.astype(jnp.float32)
    y = xf * lax.rsqrt(jnp.mean(xf * xf, axis=-1, keepdims=True) + EPS)
    return (y * g.astype(jnp.float32)).astype(x.dtype)

def multiscale_pool(v):
    T = v.shape[1]
    vf = v.astype(jnp.float32)
    cs = jnp.cumsum(vf, axis=1)
    pos = jnp.arange(T, dtype=jnp.float32)
    outs = []
    for g, w in enumerate(POOL_WINDOWS):
        lo, hi = g * POOL_GROUP, (g + 1) * POOL_GROUP
        c = cs[..., lo:hi]
        prev = jnp.pad(c[:, :-w], ((0, 0), (w, 0), (0, 0)))
        cnt = jnp.minimum(pos + 1.0, float(w))[None, :, None]
        outs.append((c - prev) / cnt - vf[..., lo:hi])
    return jnp.stack(outs, axis=2).astype(v.dtype)

def pool_mixer(h, w_in, w_grp, scale, w_out):
    B, T, _ = h.shape
    u = h @ w_in
    v, gate = jnp.split(u, 2, axis=-1)
    p = multiscale_pool(v)
    m = jnp.einsum('btgc,gcd->btgd', p, w_grp).reshape(B, T, D_INNER) * scale
    return (m * jax.nn.silu(gate)) @ w_out

def hgrn2_chunk_scan(q, k, v, b):
    _, Bn, H, C, dk = q.shape
    dv = v.shape[-1]
    causal = jnp.tril(jnp.ones((C, C), dtype=bool))

    def step(S, xs):
        qc, kc, vc, bc = xs
        diff = bc[:, :, :, None, :] - bc[:, :, None, :, :]
        diff = jnp.where(causal[None, None, :, :, None], diff, -jnp.inf)
        A = jnp.einsum('bhtd,bhsd,bhtsd->bhts', qc, kc, jnp.exp(diff))
        o = (jnp.einsum('bhts,bhsv->bhtv', A, vc)
             + jnp.einsum('bhtd,bhdv->bhtv', qc * jnp.exp(bc), S))
        b_last = bc[:, :, -1:, :]
        S = (jnp.exp(b_last[:, :, 0, :])[..., None] * S
             + jnp.einsum('bhsd,bhsv->bhdv', kc * jnp.exp(b_last - bc), vc))
        return S, o

    S0 = jnp.zeros((Bn, H, dk, dv), jnp.float32)
    _, o = lax.scan(step, S0, (q, k, v, b))
    return o

def hgrn2_mixer(h, w_in, lb, norm_g, w_out):
    B, T, _ = h.shape
    N = T // CHUNK
    u = h @ w_in
    q, fz, i, gate = jnp.split(u, 4, axis=-1)
    fz = fz.astype(jnp.float32)
    lbf = lb.astype(jnp.float32)
    log_f = jnp.logaddexp(jnp.log(lbf), jnp.log1p(-lbf) + jax.nn.log_sigmoid(fz))
    k = (1.0 - lbf) * jax.nn.sigmoid(-fz)

    def to_chunks(a):
        return a.astype(jnp.float32).reshape(B, N, CHUNK, HGRN_HEADS, HGRN_HEAD_DIM).transpose(1, 0, 3, 2, 4)

    qc, kc, vc, lfc = to_chunks(q), to_chunks(k), to_chunks(i), to_chunks(log_f)
    bc = jnp.cumsum(lfc, axis=3)
    o = hgrn2_chunk_scan(qc, kc, vc, bc)
    o = o.transpose(1, 0, 3, 2, 4).reshape(B, T, HGRN_HEADS, HGRN_HEAD_DIM)
    o = o * lax.rsqrt(jnp.mean(o * o, axis=-1, keepdims=True) + EPS)
    o = (o * norm_g.astype(jnp.float32).reshape(HGRN_HEADS, HGRN_HEAD_DIM)).reshape(B, T, D_INNER)
    o = o.astype(h.dtype)
    return (o * jax.nn.silu(gate)) @ w_out

def first_inputs(seed: int = 0) -> dict:
    key = jax.random.key(seed)
    ks = jax.random.split(key, 12)
    f32 = jnp.float32
    x = jax.random.normal(ks[0], (BATCH, SEQ, D_MODEL), f32)
    norm_g = 1.0 + 0.05 * jax.random.normal(ks[1], (DEPTH, D_MODEL), f32)
    pool_w_in = jax.random.normal(ks[2], (N_POOL_LAYERS, D_MODEL, 2 * D_INNER), f32) * D_MODEL ** -0.5
    pool_w_grp = jax.random.normal(ks[3], (N_POOL_LAYERS, N_POOL_GROUPS, POOL_GROUP, POOL_GROUP), f32) * POOL_GROUP ** -0.5
    pool_scale = 1.0 + 0.1 * jax.random.normal(ks[4], (N_POOL_LAYERS, D_INNER), f32)
    pool_w_out = jax.random.normal(ks[5], (N_POOL_LAYERS, D_INNER, D_MODEL), f32) * D_INNER ** -0.5
    hgrn_w_in = jax.random.normal(ks[6], (N_HGRN_LAYERS, D_MODEL, 4 * D_INNER), f32) * D_MODEL ** -0.5
    hgrn_lower_bounds = 0.5 * jax.random.normal(ks[7], (DEPTH, D_INNER), f32)
    hgrn_norm_g = 1.0 + 0.05 * jax.random.normal(ks[8], (N_HGRN_LAYERS, D_INNER), f32)
    hgrn_w_out = jax.random.normal(ks[9], (N_HGRN_LAYERS, D_INNER, D_MODEL), f32) * D_INNER ** -0.5
    final_g = 1.0 + 0.05 * jax.random.normal(ks[10], (D_MODEL,), f32)
    return {"x": x, "norm_g": norm_g, "pool_w_in": pool_w_in, "pool_w_grp": pool_w_grp,
            "pool_scale": pool_scale, "pool_w_out": pool_w_out, "hgrn_w_in": hgrn_w_in,
            "hgrn_lower_bounds": hgrn_lower_bounds, "hgrn_norm_g": hgrn_norm_g,
            "hgrn_w_out": hgrn_w_out, "final_g": final_g}

def first_block(x, norm_g, pool_w_in, pool_w_grp, pool_scale, pool_w_out, hgrn_w_in,
              hgrn_lower_bounds, hgrn_norm_g, hgrn_w_out, final_g):
    p = jax.nn.softmax(hgrn_lower_bounds.astype(jnp.float32), axis=0)
    lbs = jnp.cumsum(p, axis=0) - p[0:1]
    h = x
    for layer in range(DEPTH):
        hn = rms_norm(h, norm_g[layer])
        j = layer // N_MIXERS
        if layer % N_MIXERS == 0:
            y = pool_mixer(hn, pool_w_in[j], pool_w_grp[j], pool_scale[j], pool_w_out[j])
        else:
            y = hgrn2_mixer(hn, hgrn_w_in[j], lbs[layer], hgrn_norm_g[j], hgrn_w_out[j])
        h = h + y.astype(h.dtype)
    return rms_norm(h, final_g)


DEPTH_2 = 1

N_MEM = 256
HEAD_DIM = 64
ATT_HEADS = 4
ATT_WIDTH = ATT_HEADS * HEAD_DIM
CONV_WIDTH = 384
CONV_KERNEL = 31
CONV_PAD = CONV_KERNEL // 2
RWKV_HEADS = 6
RWKV_WIDTH = RWKV_HEADS * HEAD_DIM
MIX_WIDTH = ATT_WIDTH + CONV_WIDTH + RWKV_WIDTH
DECAY_RANK = 64
ICLR_RANK = 64
GATE_RANK = 128
RWKV_PROJ = 3 * RWKV_WIDTH + 2 * DECAY_RANK + 2 * ICLR_RANK + GATE_RANK
IN_PROJ = ATT_WIDTH + 2 * CONV_WIDTH + RWKV_PROJ
N_EXPERTS = 16
EXPERT_FF = 1024
CAPACITY_FACTOR = 2
NORM_EPS = 1e-6
LN_EPS = 1e-5
GN_EPS = 64e-5
L2_EPS = 1e-12
DECAY_SCALE = 0.606531


def rms_norm_2(x, g):
    xf = x.astype(jnp.float32)
    y = xf * lax.rsqrt(jnp.mean(xf * xf, axis=-1, keepdims=True) + NORM_EPS)
    return (y * g.astype(jnp.float32)).astype(x.dtype)

def memory_cross_attention(q, mem_n, w_mk, w_mv):
    B, S, _ = q.shape
    qh = q.reshape(B, S, ATT_HEADS, HEAD_DIM)
    kh = (mem_n @ w_mk).reshape(B, -1, ATT_HEADS, HEAD_DIM)
    vh = (mem_n @ w_mv).reshape(B, -1, ATT_HEADS, HEAD_DIM)
    s = jnp.einsum('bqhd,bmhd->bhqm', qh, kh).astype(jnp.float32) * (HEAD_DIM ** -0.5)
    pr = jax.nn.softmax(s, axis=-1).astype(vh.dtype)
    o = jnp.einsum('bhqm,bmhd->bqhd', pr, vh)
    return o.reshape(B, S, ATT_WIDTH)

def conformer_conv(pc, conv_w, conv_b, ln_g, ln_b):
    val, gate = jnp.split(pc, 2, axis=-1)
    u = val * jax.nn.sigmoid(gate)
    u = lax.conv_general_dilated(
        u, conv_w[:, None, :].astype(u.dtype), window_strides=(1,),
        padding=[(CONV_PAD, CONV_PAD)], dimension_numbers=('NWC', 'WIO', 'NWC'),
        feature_group_count=CONV_WIDTH) + conv_b.astype(u.dtype)
    uf = u.astype(jnp.float32)
    mu = jnp.mean(uf, axis=-1, keepdims=True)
    var = jnp.mean(jnp.square(uf - mu), axis=-1, keepdims=True)
    uf = (uf - mu) * lax.rsqrt(var + LN_EPS) * ln_g.astype(jnp.float32) + ln_b.astype(jnp.float32)
    return jax.nn.silu(uf).astype(pc.dtype)

def token_shift_centred(p, mu):
    prev = jnp.pad(p, ((0, 0), (1, 0), (0, 0)))[:, :-1]
    nxt = jnp.pad(p, ((0, 0), (0, 1), (0, 0)))[:, 1:]
    return p + mu[0] * (prev - p) + mu[1] * (nxt - p)

def wkv7_scan(r, w, k, v, kk, a, reverse):
    def step(state, inp):
        r_t, w_t, k_t, v_t, kk_t, a_t = inp
        sa = jnp.einsum('bhij,bhj->bhi', state, -kk_t)
        state = (state * w_t[..., None, :]
                 + sa[..., :, None] * (kk_t * a_t)[..., None, :]
                 + v_t[..., :, None] * k_t[..., None, :])
        y_t = jnp.einsum('bhij,bhj->bhi', state, r_t)
        return state, y_t
    S, B, H, N = r.shape
    state0 = jnp.zeros((B, H, N, N), jnp.float32)
    _, ys = lax.scan(step, state0, (r, w, k, v, kk, a), reverse=reverse)
    return ys

def rwkv7_bidirectional(pr, shift_mu, decay_w0, decay_up, iclr_a0, iclr_up, gate_up,
                        k_k, k_a, r_k, lnx_g, lnx_b):
    f32 = jnp.float32
    B, S, _ = pr.shape
    pf = token_shift_centred(pr.astype(f32), shift_mu.astype(f32))
    c0 = 3 * RWKV_WIDTH
    cuts = [RWKV_WIDTH, 2 * RWKV_WIDTH, c0, c0 + DECAY_RANK, c0 + 2 * DECAY_RANK,
            c0 + 2 * DECAY_RANK + ICLR_RANK, c0 + 2 * DECAY_RANK + 2 * ICLR_RANK]
    r, k, v, wdf, wdb, adf, adb, gd = jnp.split(pf, cuts, axis=-1)

    def heads(t):
        return t.reshape(t.shape[:-1] + (RWKV_HEADS, HEAD_DIM))

    def tm(t):
        return jnp.moveaxis(t, 1, 0)

    g = jax.nn.sigmoid(gd) @ gate_up.astype(f32)
    kk = heads(k * k_k.astype(f32))
    kk = kk * lax.rsqrt(jnp.sum(kk * kk, axis=-1, keepdims=True) + L2_EPS)
    r_h, v_h = heads(r), heads(v)
    r_tm, v_tm, kk_tm = tm(r_h), tm(v_h), tm(kk)
    r_k32 = r_k.astype(f32)

    outs, bonuses = [], []
    for d, (wd, ad) in enumerate(((wdf, adf), (wdb, adb))):
        w = jnp.exp(-DECAY_SCALE * jax.nn.sigmoid(
            decay_w0[d].astype(f32) + jnp.tanh(wd) @ decay_up[d].astype(f32)))
        a = jax.nn.sigmoid(iclr_a0[d].astype(f32) + ad @ iclr_up[d].astype(f32))
        k_d = heads(k * (1.0 + (a - 1.0) * k_a.astype(f32)))
        ys = wkv7_scan(r_tm, tm(heads(w)), tm(k_d), v_tm, kk_tm, tm(heads(a)), reverse=(d == 1))
        outs.append(jnp.moveaxis(ys, 0, 1))
        bonuses.append(jnp.sum(r_h * k_d * r_k32, axis=-1, keepdims=True) * v_h)
    y = outs[0] + outs[1]
    mu = jnp.mean(y, axis=-1, keepdims=True)
    var = jnp.mean(jnp.square(y - mu), axis=-1, keepdims=True)
    y = ((y - mu) * lax.rsqrt(var + GN_EPS) * lnx_g.astype(f32).reshape(RWKV_HEADS, HEAD_DIM)
         + lnx_b.astype(f32).reshape(RWKV_HEADS, HEAD_DIM))
    y = (y + bonuses[0] + bonuses[1]).reshape(B, S, RWKV_WIDTH) * g
    return y.astype(pr.dtype)

def expert_choice_ffn(h, w_router, w_gate, w_up, w_down):
    B, S, D = h.shape
    cap = CAPACITY_FACTOR * S // N_EXPERTS
    aff = jax.nn.softmax((h @ w_router).astype(jnp.float32), axis=-1)
    gates, idx = lax.top_k(jnp.swapaxes(aff, 1, 2), cap)
    xe = jax.vmap(lambda hb, ib: hb[ib])(h, idx)
    hid = jax.nn.silu(jnp.einsum('becd,edf->becf', xe, w_gate)) * jnp.einsum('becd,edf->becf', xe, w_up)
    ye = jnp.einsum('becf,efd->becd', hid, w_down) * gates[..., None].astype(h.dtype)
    bidx = jnp.arange(B)[:, None, None]
    return jnp.zeros_like(h).at[bidx, idx].add(ye)

def second_inputs(seed: int = 0) -> dict:
    key = jax.random.key(seed)
    ks = iter(jax.random.split(key, 40))
    L, D = DEPTH_2, D_MODEL

    def nrm(shape, scale):
        return scale * jax.random.normal(next(ks), shape, jnp.float32)

    return {
        "x": nrm((BATCH, SEQ, D), 1.0),
        "mem": nrm((BATCH, N_MEM, D), 1.0),
        "norm_mix_g": 1.0 + nrm((L, D), 0.05),
        "norm_mem_g": 1.0 + nrm((L, D), 0.05),
        "w_in": nrm((L, D, IN_PROJ), D ** -0.5),
        "w_mk": nrm((L, D, ATT_WIDTH), D ** -0.5),
        "w_mv": nrm((L, D, ATT_WIDTH), D ** -0.5),
        "conv_w": nrm((L, CONV_KERNEL, CONV_WIDTH), CONV_KERNEL ** -0.5),
        "conv_b": nrm((L, CONV_WIDTH), 0.01),
        "conv_ln_g": 1.0 + nrm((L, CONV_WIDTH), 0.05),
        "conv_ln_b": nrm((L, CONV_WIDTH), 0.01),
        "shift_mu": jax.random.uniform(next(ks), (L, 2, RWKV_PROJ), jnp.float32, 0.0, 0.5),
        "decay_w0": nrm((L, 2, RWKV_WIDTH), 0.5),
        "decay_up": nrm((L, 2, DECAY_RANK, RWKV_WIDTH), 0.1),
        "iclr_a0": nrm((L, 2, RWKV_WIDTH), 0.5),
        "iclr_up": nrm((L, 2, ICLR_RANK, RWKV_WIDTH), 0.1),
        "gate_up": nrm((L, GATE_RANK, RWKV_WIDTH), GATE_RANK ** -0.5),
        "k_k": 0.85 + nrm((L, RWKV_WIDTH), 0.05),
        "k_a": 1.0 + nrm((L, RWKV_WIDTH), 0.05),
        "r_k": nrm((L, RWKV_HEADS, HEAD_DIM), 0.1),
        "lnx_g": 1.0 + nrm((L, RWKV_WIDTH), 0.05),
        "lnx_b": nrm((L, RWKV_WIDTH), 0.01),
        "w_out": nrm((L, MIX_WIDTH, D), MIX_WIDTH ** -0.5),
        "norm_ffn_g": 1.0 + nrm((L, D), 0.05),
        "w_router": nrm((L, D, N_EXPERTS), D ** -0.5),
        "w_e_gate": nrm((L, N_EXPERTS, D, EXPERT_FF), D ** -0.5),
        "w_e_up": nrm((L, N_EXPERTS, D, EXPERT_FF), D ** -0.5),
        "w_e_down": nrm((L, N_EXPERTS, EXPERT_FF, D), EXPERT_FF ** -0.5),
        "final_norm_g": 1.0 + nrm((D,), 0.05),
    }

def second_block(x, mem, norm_mix_g, norm_mem_g, w_in, w_mk, w_mv, conv_w, conv_b, conv_ln_g,
              conv_ln_b, shift_mu, decay_w0, decay_up, iclr_a0, iclr_up, gate_up, k_k, k_a,
              r_k, lnx_g, lnx_b, w_out, norm_ffn_g, w_router, w_e_gate, w_e_up, w_e_down,
              final_norm_g):
    for l in range(DEPTH_2):
        h = rms_norm_2(x, norm_mix_g[l])
        p = h @ w_in[l]
        q, pc, pr = jnp.split(p, [ATT_WIDTH, ATT_WIDTH + 2 * CONV_WIDTH], axis=-1)
        mem_n = rms_norm_2(mem, norm_mem_g[l])
        o_att = memory_cross_attention(q, mem_n, w_mk[l], w_mv[l])
        o_conv = conformer_conv(pc, conv_w[l], conv_b[l], conv_ln_g[l], conv_ln_b[l])
        o_rwkv = rwkv7_bidirectional(pr, shift_mu[l], decay_w0[l], decay_up[l], iclr_a0[l],
                                     iclr_up[l], gate_up[l], k_k[l], k_a[l], r_k[l],
                                     lnx_g[l], lnx_b[l])
        x = x + jnp.concatenate([o_att, o_conv, o_rwkv], axis=-1) @ w_out[l]
        x = x + expert_choice_ffn(rms_norm_2(x, norm_ffn_g[l]), w_router[l], w_e_gate[l],
                                  w_e_up[l], w_e_down[l])
    return rms_norm_2(x, final_norm_g)


def setup_inputs(seed=0):
    out = dict(first_inputs(seed))
    for name, value in second_inputs(seed + 1).items():
        if name != "x":
            out[name + "_2"] = value
    return out


def reference(
    x, norm_g, pool_w_in, pool_w_grp, pool_scale, pool_w_out, hgrn_w_in, hgrn_lower_bounds,
    hgrn_norm_g, hgrn_w_out, final_g, mem_2, norm_mix_g_2, norm_mem_g_2, w_in_2, w_mk_2, w_mv_2,
    conv_w_2, conv_b_2, conv_ln_g_2, conv_ln_b_2, shift_mu_2, decay_w0_2, decay_up_2, iclr_a0_2,
    iclr_up_2, gate_up_2, k_k_2, k_a_2, r_k_2, lnx_g_2, lnx_b_2, w_out_2, norm_ffn_g_2,
    w_router_2, w_e_gate_2, w_e_up_2, w_e_down_2, final_norm_g_2,
):
    x = first_block(
        x, norm_g, pool_w_in, pool_w_grp, pool_scale, pool_w_out, hgrn_w_in, hgrn_lower_bounds,
        hgrn_norm_g, hgrn_w_out, final_g,
    )
    return second_block(
        x, mem_2, norm_mix_g_2, norm_mem_g_2, w_in_2, w_mk_2, w_mv_2, conv_w_2, conv_b_2,
        conv_ln_g_2, conv_ln_b_2, shift_mu_2, decay_w0_2, decay_up_2, iclr_a0_2, iclr_up_2,
        gate_up_2, k_k_2, k_a_2, r_k_2, lnx_g_2, lnx_b_2, w_out_2, norm_ffn_g_2, w_router_2,
        w_e_gate_2, w_e_up_2, w_e_down_2, final_norm_g_2,
    )


_drawn_inputs = setup_inputs


def setup_inputs(seed=0):
    import zlib

    import numpy as np

    out = dict(_drawn_inputs(seed))
    spreads = {}
    factors = {'norm_mem_g_2': 8.0,
     'conv_b_2': 25.248,
     'conv_ln_b_2': 49.704,
     'k_k_2': 48.552,
     'lnx_g_2': 12.958,
     'lnx_b_2': 61.888,
     'conv_ln_g_2': 8.0,
     'k_a_2': 2.964,
     'norm_ffn_g_2': 6.822}
    for name, (base, spread) in spreads.items():
        noise = np.random.default_rng([zlib.crc32(name.encode()), seed]).standard_normal(out[name].shape)
        drawn = base * np.exp(spread * noise) if base else spread * noise
        out[name] = __import__('jax').numpy.asarray(drawn.astype(out[name].dtype))
    for name, factor in factors.items():
        out[name] = (out[name] * factor).astype(out[name].dtype)
    return out
```

```python
import concourse.bass as bass
from concourse import mybir
import numpy as np

F32 = mybir.dt.float32
U8 = mybir.dt.uint8
U32 = mybir.dt.uint32
ALU = mybir.AluOpType
ACT = mybir.ActivationFunctionType

P = 128
T = 1024
D = 1024
TT = T // P
KD = D // P
DI = 2048
KI = DI // P
G = 4
GT = DI // G // P
WINDOWS = (2, 4, 8, 16)
PADL = 16
HEADS = DI // P
EPS = 1e-6
HALVES = (64, 32, 16, 8, 4)
MEM = 256
AH = 4
CT = 3
CONV_K = 31
CPAD = CONV_K // 2
DECAY_SCALE = 0.606531
RT = 12
NE = 16
CAP = 2 * T // NE
JOINS = (2, 4, 8, 16, 32, 64)
CHUNK_W = 4096

PAR = {}
_at = 0
for _name, _n in (("norm0", KD), ("norm1", KD), ("pool_scale", KI), ("lb0", KI), ("lb1", KI),
                  ("hgrn_g", KI), ("norm_mix", KD), ("norm_mem", KD),
                  ("conv_w", CT * CONV_K), ("conv_b", CT), ("conv_g", CT), ("conv_beta", CT),
                  ("mu_prev", RT), ("mu_next", RT), ("w0", 2 * CT), ("a0", 2 * CT), ("k_k", CT),
                  ("k_a", CT), ("r_k", CT), ("lnx_g", CT), ("lnx_b", CT), ("router", KD * NE)):
    PAR[_name] = (_at, _n)
    _at += _n
PAR_N = _at

CON = {}
_at = 0
for _name, _n in (("ident", P), ("ones", P), ("inv_count", PADL), ("blocks64", P)):
    CON[_name] = (_at, _n)
    _at += _n
CON_N = _at

RWM = {}
_at = 0
for _name, _n in (("rw_mask", 2 * 640), ("join_mask", 6 * 64), ("pair_mask", 2 * P)):
    RWM[_name] = (_at, _n)
    _at += _n
RWM_N = _at


def constants():
    c = np.zeros((P, CON_N), np.float32)
    a, n = CON["ident"]
    c[:, a:a + n] = np.eye(P)
    a, n = CON["ones"]
    c[:, a:a + n] = 1.0
    a, n = CON["inv_count"]
    c[:, a:a + n] = 1.0 / (np.arange(n) + 1)
    r, q = np.arange(P)[:, None], np.arange(P)[None, :]
    a, n = CON["blocks64"]
    c[:, a:a + n] = r // 64 == q // 64
    return c


def rwkv_masks():
    c = np.zeros((P, RWM_N), np.float32)
    r, q = np.arange(P)[:, None], np.arange(P)[None, :]
    a, n = RWM["rw_mask"]
    for d, before in enumerate((r < q, r > q)):
        upto = before | (r == q)
        c[:, a + 640 * d:a + 640 * (d + 1)] = np.concatenate(
            [-1.0 * before, 1.0 * upto, 1.0 * before, 1.0 * upto, -1.0 * before.T], 1)
    a, n = RWM["join_mask"]
    for n, b in enumerate(JOINS):
        first = np.array([j for j in range(P) if j % (2 * b) < b])[None, :]
        c[:, a + 64 * n:a + 64 * (n + 1)] = (r // (2 * b) == first // (2 * b)) & (r % (2 * b) >= b)
    a, n = RWM["pair_mask"]
    c[:, a:a + P] = (r // 2 == q // 2) & (r > q)
    c[:, a + P:a + 2 * P] = (r // 2 == q // 2) & (r < q)
    return c


def level_masks():
    s = np.arange(P)[:, None]
    parts = []
    for h in HALVES:
        t = np.array([t for t in range(P) if t % (2 * h) >= h])[None, :]
        parts.append((s // (2 * h) == t // (2 * h)) & (s % (2 * h) < h))
    t = np.arange(P)[None, :]
    parts.append((s // 4 == t // 4) & (s <= t))
    t = np.arange(T)[None, :] % P
    keep = [np.repeat(t != 0, P, 0), np.repeat(t != P - 1, P, 0)]
    return np.concatenate([np.tile(m, (1, 4)) for m in parts] + keep, 1).astype(np.float32)


class Memory:

    def __init__(self, nc):
        self.nc = nc
        self.stage = []
        sb = nc.alloc_sbuf_tensor
        self.sent = set()
        self.par = sb("sb_par", [P, PAR_N], F32)
        self.con = sb("sb_con", [P, CON_N], F32)
        self.hmask = sb("sb_hmask", [P, 4 * (5 * 64 + P) + 2 * T], U8)
        self.ring = sb("sb_ring", [P, 2, CHUNK_W], F32)
        self.ht = sb("sb_ht", [P, KD, T], F32)
        self.zt = sb("sb_zt", [P, KI, T], F32)
        self.scr_n = 18432
        self.scr = sb("sb_scr", [P, self.scr_n], F32)
        self.carry = sb("sb_carry", [P, TT, 6], F32)
        self.bounds = sb("sb_bounds", [P, 2 * KI], F32)
        self.small = sb("sb_small", [P, 64], F32)
        self.ps = nc.alloc_psum_tensor("ps", [P, 4, 1024], F32)
        self.h = self.scr[:, 0:TT * D].rearrange("p (a n) -> p a n", a=TT)

    def semaphore(self, name):
        s = self.nc.alloc_semaphore(name)
        self.stage.append(s)
        return s

    def stage_end(self):
        self.nc.clear_and_free_semaphores(self.stage)
        self.nc.all_engine_barrier()
        self.stage = []

    def p(self, name):
        a, n = PAR[name]
        return self.par[:, a:a + n]

    def c(self, name):
        a, n = CON[name]
        return self.con[:, a:a + n]


class Weights:

    def __init__(self, nc):
        self.loaded = [nc.alloc_semaphore(f"weights_loaded_{s}") for s in range(2)]
        self.used = nc.alloc_semaphore("weights_used")
        self.sources = []

    def wait(self, eng, n):
        eng.wait_ge(self.loaded[n % 2], 16 * (n // 2 + 1))


def dma_chunk(eng, M, W, n, slot, src):
    if isinstance(n, int):
        if n >= 2:
            eng.wait_ge(W.used, n - 1)
    else:
        eng.wait_ge(W.used, n - 1)
    width = src.shape[-1]
    eng.dma_start(M.ring[:, slot, 0:width], src).then_inc(W.loaded[slot], 16)


def slot_view(M, slot, kt, cols):
    return M.ring[:, slot, 0:kt * cols].rearrange("p (k n) -> p k n", k=kt)


def norm_transpose(nc, M, W, tag, gain, load=None, store=None, prefetch=()):
    sem = M.semaphore
    rows_in = sem(f"{tag}_rows_in")
    rows_out = sem(f"{tag}_rows_out")
    sq = sem(f"{tag}_squares")
    root = sem(f"{tag}_root")
    rstd = sem(f"{tag}_rstd")
    scaled = sem(f"{tag}_scaled")
    turned = sem(f"{tag}_turned")
    copied = sem(f"{tag}_copied")
    junk = M.scr[:, TT * D:TT * D + D]
    ident = M.c("ident")
    with nc.Block() as block:
        @block.sync
        def _(sp):
            if load is not None:
                for t in range(TT):
                    sp.dma_start(M.h[:, t, :], load[t * P:(t + 1) * P, :]).then_inc(rows_in, 16)
            if store is not None:
                for t in range(TT):
                    sp.dma_start(store[t * P:(t + 1) * P, :], M.h[:, t, :]).then_inc(rows_out, 16)
            for n, src in prefetch:
                dma_chunk(sp, M, W, n, n % 2, src)
            if store is not None:
                sp.wait_ge(rows_out, 16 * TT)

        @block.scalar
        def _(act):
            for t in range(TT):
                if load is not None:
                    act.wait_ge(rows_in, 16 * TT)
                if t:
                    act.wait_ge(sq, t)
                nc.scalar.activation(junk, M.h[:, t, :], ACT.Square,
                                     accum_out=M.small[:, t:t + 1]).then_inc(sq, 1)
            act.wait_ge(sq, TT)
            nc.scalar.activation(M.small[:, 8:8 + TT], M.small[:, 0:TT], ACT.Sqrt,
                                 scale=1.0 / D, bias=M.eps).then_inc(root, 1)

        @block.vector
        def _(dve):
            dve.wait_ge(root, 1)
            nc.vector.reciprocal(M.small[:, 16:16 + TT], M.small[:, 8:8 + TT]).then_inc(rstd, 1)
            dve.wait_ge(rstd, 1)
            if store is not None:
                dve.wait_ge(rows_out, 16 * TT)
            for t in range(TT):
                nc.vector.tensor_scalar(M.h[:, t, :], M.h[:, t, :], M.small[:, 16 + t:17 + t], None,
                                        ALU.mult).then_inc(scaled, 1)
            for t in range(TT):
                dve.wait_ge(turned, t + 1)
                nc.vector.tensor_tensor(
                    M.ht[:, :, t * P:(t + 1) * P],
                    M.ps[:, t % 4, :].rearrange("p (k n) -> p k n", k=KD),
                    gain.unsqueeze(2).to_broadcast([P, KD, P]), ALU.mult).then_inc(copied, 1)

        @block.tensor
        def _(pe):
            for t in range(TT):
                pe.wait_ge(scaled, t + 1)
                if t >= 4:
                    pe.wait_ge(copied, t - 3)
                for k in range(KD):
                    last = nc.tensor.transpose(M.ps[:, t % 4, k * P:(k + 1) * P],
                                               M.h[:, t, k * P:(k + 1) * P], ident)
                last.then_inc(turned, 1)


def pool_layer(nc, M, W, n0, w_in, w_grp, prefetch=()):
    sem = M.semaphore
    grp_in = sem("pool_group_weights")
    zeroed = sem("pool_pads_zeroed")
    v_mm, v_cp = sem("pool_values_summed"), sem("pool_values_copied")
    g_mm, g_cp = sem("pool_gates_summed"), sem("pool_gates_copied")
    m_mm, m_cp = sem("pool_mixed_summed"), sem("pool_mixed_copied")
    win = sem("pool_window_step")
    pooled = sem("pool_pooled")
    LW = PADL + T
    cut = [0]

    def scratch(n):
        cut[0] += n
        return M.scr[:, cut[0] - n:cut[0]]

    V = scratch(GT * LW).rearrange("p (a n) -> p a n", a=GT)
    S = [scratch(2 * LW).rearrange("p (a n) -> p a n", a=2) for _ in range(2)]
    PL = scratch(GT * T).rearrange("p (a n) -> p a n", a=GT)
    WG = scratch(4 * 512).rearrange("p (k n) -> p k n", k=4)
    inv_count = M.c("inv_count")
    scale = M.p("pool_scale")
    steps = [0]

    with nc.Block() as block:
        @block.sync
        def _(sp):
            for g in range(G):
                for j in range(2):
                    n = n0 + 2 * g + j
                    dma_chunk(sp, M, W, n, n % 2, w_in[g + 4 * j]) if n not in M.sent else None
                if g:
                    sp.wait_ge(m_mm, GT * g)
                sp.dma_start(WG, w_grp[g].rearrange("p (k n) -> p k n", k=4)).then_inc(grp_in, 16)
            for n, src in prefetch:
                dma_chunk(sp, M, W, n, n % 2, src)

        @block.tensor
        def _(pe):
            unit = 0

            def free(u):
                if u < 4:
                    return
                u -= 4
                g, r = divmod(u, 3 * GT)
                pe.wait_ge((v_cp, g_cp, m_cp)[r // GT], g * GT + r % GT + 1)

            for g in range(G):
                for j, done in ((0, v_mm), (1, g_mm)):
                    n = n0 + 2 * g + j
                    W.wait(pe, n)
                    w = slot_view(M, n % 2, KD, 512)
                    for m in range(GT):
                        free(unit)
                        for half in range(2):
                            for k in range(KD):
                                last = nc.tensor.matmul(
                                    M.ps[:, unit % 4, half * 512:(half + 1) * 512],
                                    lhsT=w[:, k, m * P:(m + 1) * P],
                                    rhs=M.ht[:, k, half * 512:(half + 1) * 512],
                                    start=k == 0, stop=k == KD - 1)
                        last.then_inc(done, 1)
                        unit += 1
                    pe.wait_ge(done, GT * (g + 1))
                    pe.sem_inc(W.used, 1)
                pe.wait_ge(grp_in, 16 * (g + 1))
                pe.wait_ge(pooled, 2 * (g + 1))
                for m in range(GT):
                    free(unit)
                    for half in range(2):
                        for k in range(GT):
                            last = nc.tensor.matmul(
                                M.ps[:, unit % 4, half * 512:(half + 1) * 512],
                                lhsT=WG[:, k, m * P:(m + 1) * P],
                                rhs=PL[:, k, half * 512:(half + 1) * 512],
                                start=k == 0, stop=k == GT - 1)
                    last.then_inc(m_mm, 1)
                    unit += 1

        @block.scalar
        def _(act):
            u = 0
            act.wait_ge(zeroed, 3)
            for g in range(G):
                for m in range(GT):
                    act.wait_ge(v_mm, g * GT + m + 1)
                    if g:
                        act.wait_ge(pooled, 2 * g)
                    nc.scalar.activation(V[:, m, PADL:LW], M.ps[:, u % 4, :], ACT.Copy).then_inc(v_cp, 1)
                    u += 1
                for m in range(GT):
                    act.wait_ge(g_mm, g * GT + m + 1)
                    nc.scalar.activation(M.zt[:, g * GT + m, :], M.ps[:, u % 4, :], ACT.Silu).then_inc(g_cp, 1)
                    u += 1
                u += GT

        @block.vector
        def _(dve):
            nc.vector.memset(V, 0.0).then_inc(zeroed, 1)
            nc.vector.memset(S[0], 0.0).then_inc(zeroed, 1)
            nc.vector.memset(S[1], 0.0).then_inc(zeroed, 1)
            dve.wait_ge(zeroed, 3)

            def step(ins):
                steps[0] += 1
                ins.then_inc(win, 1)
                dve.wait_ge(win, steps[0])

            u = 0
            for g, w in enumerate(WINDOWS):
                for pair in range(2):
                    dve.wait_ge(v_cp, g * GT + 2 * pair + 2)
                    if g:
                        dve.wait_ge(m_mm, GT * g)
                    v = V[:, 2 * pair:2 * pair + 2, :]
                    src, span = v, 1
                    while span < w:
                        dst = S[(span.bit_length() - 1) % 2]
                        step(nc.vector.tensor_tensor(dst[:, :, PADL:LW], src[:, :, PADL:LW],
                                                     src[:, :, PADL - span:LW - span], ALU.add))
                        src, span = dst, 2 * span
                    out = PL[:, 2 * pair:2 * pair + 2, :]
                    step(nc.vector.scalar_tensor_tensor(out, src[:, :, PADL:LW], 1.0 / w, v[:, :, PADL:LW],
                                                        ALU.mult, ALU.subtract))
                    head = src[:, :, PADL:PADL + w]
                    step(nc.vector.tensor_tensor(head, head,
                                                 inv_count[:, 0:w].unsqueeze(1).to_broadcast([P, 2, w]), ALU.mult))
                    nc.vector.tensor_tensor(out[:, :, 0:w], head, v[:, :, PADL:PADL + w],
                                            ALU.subtract).then_inc(pooled, 1)
                    dve.wait_ge(pooled, 2 * g + pair + 1)
                for m in range(GT):
                    dve.wait_ge(m_mm, g * GT + m + 1)
                    dve.wait_ge(g_cp, g * GT + m + 1)
                    z = M.zt[:, g * GT + m, :]
                    nc.vector.scalar_tensor_tensor(
                        z, M.ps[:, (3 * GT * g + 2 * GT + m) % 4, :], scale[:, g * GT + m:g * GT + m + 1], z,
                        ALU.mult, ALU.mult).then_inc(m_cp, 1)


def out_projection(nc, M, W, tag, n0, zt, kt, w_out, residual, prefetch=()):
    sem = M.semaphore
    rows_in = sem(f"{tag}_residual_in")
    summed, added = sem(f"{tag}_summed"), sem(f"{tag}_added")
    cols = CHUNK_W // kt
    chunks = D // cols
    with nc.Block() as block:
        @block.sync
        def _(sp):
            for t in range(TT):
                sp.dma_start(M.h[:, t, :], residual[t * P:(t + 1) * P, :]).then_inc(rows_in, 16)
            for c in range(chunks):
                if n0 + c not in M.sent:
                    dma_chunk(sp, M, W, n0 + c, (n0 + c) % 2, w_out[c])
            for n, src in prefetch:
                dma_chunk(sp, M, W, n, n % 2, src)

        @block.tensor
        def _(pe):
            for c in range(chunks):
                n = n0 + c
                W.wait(pe, n)
                w = slot_view(M, n % 2, kt, cols)
                for t in range(TT):
                    u = c * TT + t
                    if u >= 8:
                        pe.wait_ge(added, u - 7)
                    for k in range(kt):
                        last = nc.tensor.matmul(bank(M, u % 8)[:, 0:cols], lhsT=zt[:, k, t * P:(t + 1) * P],
                                                rhs=w[:, k, :], start=k == 0, stop=k == kt - 1)
                    last.then_inc(summed, 1)
                pe.wait_ge(summed, (c + 1) * TT)
                pe.sem_inc(W.used, 1)

        @block.vector
        def _(dve):
            dve.wait_ge(rows_in, 16 * TT)
            for c in range(chunks):
                for t in range(TT):
                    u = c * TT + t
                    dve.wait_ge(summed, u + 1)
                    h = M.h[:, t, c * cols:(c + 1) * cols]
                    nc.vector.tensor_tensor(h, bank(M, u % 8)[:, 0:cols], h, ALU.add).then_inc(added, 1)


def bank(M, b):
    return M.ps[:, b // 2, (b % 2) * 512:(b % 2) * 512 + 512]


def row_norm(nc, M, tag, gain_row, store, load=None, raw=None, prefetch=()):
    sem = M.semaphore
    gain_in, sq, root, rstd = (sem(f"{tag}_{x}") for x in ("gain_in", "squares", "root", "rstd"))
    done, out, rows_in, raw_out = (sem(f"{tag}_{x}") for x in ("done", "out", "rows_in", "raw_out"))
    junk = M.scr[:, TT * D:TT * D + D]
    gain = M.scr[:, TT * D + D:TT * D + 2 * D]
    with nc.Block() as block:
        @block.sync
        def _(sp):
            sp.dma_start(gain, gain_row.to_broadcast([P, D])).then_inc(gain_in, 16)
            for t in range(TT):
                if load is not None:
                    sp.dma_start(M.h[:, t, :], load[t * P:(t + 1) * P, :]).then_inc(rows_in, 16)
                if raw is not None:
                    sp.dma_start(raw[t * P:(t + 1) * P, :], M.h[:, t, :]).then_inc(raw_out, 16)
            for place, src, arrived in prefetch:
                sp.dma_start(place, src).then_inc(arrived, 16)
            for t in range(TT):
                sp.wait_ge(done, t + 1)
                sp.dma_start(store[t * P:(t + 1) * P, :], M.h[:, t, :]).then_inc(out, 16)
            sp.wait_ge(out, 16 * TT)
            if raw is not None:
                sp.wait_ge(raw_out, 16 * TT)

        @block.scalar
        def _(act):
            if load is not None:
                act.wait_ge(rows_in, 16 * TT)
            for t in range(TT):
                if t:
                    act.wait_ge(sq, t)
                nc.scalar.activation(junk, M.h[:, t, :], ACT.Square,
                                     accum_out=M.small[:, t:t + 1]).then_inc(sq, 1)
            act.wait_ge(sq, TT)
            nc.scalar.activation(M.small[:, 8:8 + TT], M.small[:, 0:TT], ACT.Sqrt,
                                 scale=1.0 / D, bias=M.eps).then_inc(root, 1)

        @block.vector
        def _(dve):
            dve.wait_ge(root, 1)
            nc.vector.reciprocal(M.small[:, 16:16 + TT], M.small[:, 8:8 + TT]).then_inc(rstd, 1)
            dve.wait_ge(rstd, 1)
            dve.wait_ge(gain_in, 16)
            if raw is not None:
                dve.wait_ge(raw_out, 16 * TT)
            for t in range(TT):
                nc.vector.scalar_tensor_tensor(M.h[:, t, :], M.h[:, t, :], M.small[:, 16 + t:17 + t], gain,
                                               ALU.mult, ALU.mult).then_inc(done, 1)


def setup(nc, M, par, con, hmask):
    s, z, m = M.semaphore("setup_in"), M.semaphore("setup_eps"), M.semaphore("setup_masks")
    M.eps = M.small[:, 63:64]
    floats = M.scr[:, 0:hmask.shape[1]]
    with nc.Block() as block:
        @block.sync
        def _(sp):
            sp.dma_start(M.par[:, :], par).then_inc(s, 16)
            sp.dma_start(M.con[:, :], con).then_inc(s, 16)
            sp.dma_start(floats, hmask).then_inc(s, 16)
            sp.wait_ge(s, 48)

        @block.vector
        def _(dve):
            nc.vector.memset(M.eps, EPS).then_inc(z, 1)
            dve.wait_ge(s, 48)
            nc.vector.tensor_copy(M.hmask[:, :], floats).then_inc(m, 1)
            dve.wait_ge(z, 1)
            dve.wait_ge(m, 1)


def lower_bounds(nc, M):
    sem = M.semaphore
    step, ex = sem("bounds_step"), sem("bounds_exp")
    w = M.scr
    top, e0, e1, tot = (w[:, 16 * j:16 * j + 16] for j in range(4))
    M.lb, M.oml = M.bounds[:, 0:KI], M.bounds[:, KI:2 * KI]
    l0, l1 = M.p("lb0"), M.p("lb1")
    with nc.Block() as block:
        @block.scalar
        def _(act):
            act.wait_ge(step, 3)
            nc.scalar.activation(w[:, 16:48], w[:, 16:48], ACT.Exp).then_inc(ex, 1)

        @block.vector
        def _(dve):
            n = [0]

            def link(ins):
                n[0] += 1
                ins.then_inc(step, 1)
                dve.wait_ge(step, n[0])
            tt = nc.vector.tensor_tensor
            link(tt(top, l0, l1, ALU.max))
            link(tt(e0, l0, top, ALU.subtract))
            link(tt(e1, l1, top, ALU.subtract))
            dve.wait_ge(ex, 1)
            link(tt(tot, e0, e1, ALU.add))
            link(nc.vector.reciprocal(tot, tot))
            link(tt(e0, e0, tot, ALU.mult))
            link(tt(e1, e1, tot, ALU.mult))
            link(tt(e1, e0, e1, ALU.add))
            link(tt(M.lb, e1, e0, ALU.subtract))
            link(nc.vector.tensor_scalar(M.oml, M.lb, -1.0, 1.0, ALU.mult, ALU.add))


def hgrn_gates(nc, M, W, n0, w_gate, prefetch=()):
    summed, copied = M.semaphore("hgrn_gates_summed"), M.semaphore("hgrn_gates_copied")
    with nc.Block() as block:
        @block.sync
        def _(sp):
            for c in range(4):
                if n0 + c not in M.sent:
                    dma_chunk(sp, M, W, n0 + c, (n0 + c) % 2, w_gate[c])
            for n, src in prefetch:
                dma_chunk(sp, M, W, n, n % 2, src)

        @block.tensor
        def _(pe):
            for c in range(4):
                n = n0 + c
                W.wait(pe, n)
                w = slot_view(M, n % 2, KD, 512)
                for m in range(4):
                    u = 4 * c + m
                    if u >= 4:
                        pe.wait_ge(copied, u - 3)
                    feature_tile(nc, M, u % 4, w, slice(m * P, (m + 1) * P)).then_inc(summed, 1)
                pe.wait_ge(summed, 4 * c + 4)
                pe.sem_inc(W.used, 1)

        @block.scalar
        def _(act):
            for u in range(KI):
                act.wait_ge(summed, u + 1)
                nc.scalar.activation(M.zt[:, u, :], M.ps[:, u % 4, :], ACT.Silu).then_inc(copied, 1)


def feature_tile(nc, M, unit, w, cols):
    for half in range(2):
        for k in range(KD):
            last = nc.tensor.matmul(M.ps[:, unit, half * 512:(half + 1) * 512], lhsT=w[:, k, cols],
                                    rhs=M.ht[:, k, half * 512:(half + 1) * 512],
                                    start=k == 0, stop=k == KD - 1)
    return last


def hgrn_heads(nc, M, W, n0, w_heads, prefetch=()):
    assert n0 % 2 == 0
    sem = M.semaphore
    cut = [0]

    def scratch(n):
        cut[0] += n
        return M.scr[:, cut[0] - n:cut[0]]

    def tiles(ap):
        return ap.rearrange("p (a n) -> p a n", a=TT)

    KEY = scratch(T)
    LOG = scratch(T)
    QRY = scratch(T)
    CUM = scratch(T)
    VAL = [tiles(scratch(T)) for _ in range(2)]
    LEV = [scratch(T) for _ in HALVES]
    DQ, DK = scratch(T), scratch(T)
    QE, KE = scratch(T), scratch(T)
    KET = scratch(T)
    SC = scratch(T)
    ST = tiles(scratch(T))
    END = M.small[:, 24:24 + TT]
    ones = M.c("ones")
    keep = M.hmask[:, 1792:1792 + T]
    ident = M.c("ident")
    gain = M.p("hgrn_g")

    cleared, begun, picked = sem("hgrn_cleared"), sem("scores_copy_begun"), sem("scores_picked")
    f_mm, q_mm, v_mm = sem("forget_summed"), sem("query_summed"), sem("value_summed")
    f_cp, q_cp, v_cp = sem("forget_copied"), sem("query_copied"), sem("value_copied")
    exped, plus1, recip = sem("forget_exp"), sem("forget_plus_one"), sem("forget_sigmoid")
    key, gate, log, cum = sem("key_ready"), sem("forget_gate"), sem("forget_log"), sem("decay_summed")
    offs, decayed = sem("level_offsets"), sem("level_decays")
    lev, ke = sem("levels_ready"), sem("edge_keys_ready")
    t_mm, t_cp = sem("edge_keys_turned"), sem("edge_keys_copied")
    s_mm, s_cp = sem("scores_summed"), sem("scores_copied")
    kv_mm, st = sem("tile_states_summed"), sem("states_ready")
    o_mm, o_cp, sq = sem("output_summed"), sem("output_copied"), sem("output_squared")
    n_mm, n_cp, rs = sem("square_sum"), sem("norm_log"), sem("norm_ready")
    z1, z = sem("output_scaled"), sem("head_done")
    U0, U1, U2, U3 = (M.ps[:, u, :] for u in range(4))

    def blocks(ap, h):
        return ap.rearrange("p (n two h) -> p n two h", two=2, h=h)

    def head(i, c):
        return i * 2 + c

    def loop(eng, body, first=None, last=None):
        body(0, 0, True)
        body(0, 1, False)
        with eng.Fori(1, HEADS // 2 - 1) as i:
            body(i, 0, False)
            body(i, 1, False)
        body(HEADS // 2 - 1, 0, False)
        body(HEADS // 2 - 1, 1, False, True)

    with nc.Block() as block:
        @block.sync
        def _(sp):
            for c in range(2):
                if n0 + c not in M.sent:
                    dma_chunk(sp, M, W, n0 + c, c, w_heads[c])
            with sp.Fori(1, HEADS // 2) as i:
                for c in range(2):
                    sp.wait_ge(W.used, i * 2 + (n0 + c - 1))
                    sp.dma_start(M.ring[:, c, 0:3 * KD * P], w_heads[i * 2 + c]).then_inc(W.loaded[c], 16)
            for n, src in prefetch:
                dma_chunk(sp, M, W, n, n % 2, src)

        @block.tensor
        def _(pe):
            def weights(i, c):
                pe.wait_ge(W.loaded[c % 2], i * 16 + 16 * ((n0 + c) // 2 + 1))
                return M.ring[:, c % 2, 0:3 * KD * P].rearrange("p (k n) -> p k n", k=KD)

            def project_forget(i, c, w):
                feature_tile(nc, M, 0, w, slice(P, 2 * P)).then_inc(f_mm, 1)

            def project_rest(i, c, w):
                feature_tile(nc, M, 2, w, slice(0, P)).then_inc(q_mm, 1)
                for t in range(TT):
                    for k in range(KD):
                        last = nc.tensor.matmul(M.ps[:, 3, t * P:(t + 1) * P], lhsT=M.ht[:, k, t * P:(t + 1) * P],
                                                rhs=w[:, k, 2 * P:3 * P], start=k == 0, stop=k == KD - 1)
                last.then_inc(v_mm, 1)
                pe.wait_ge(v_mm, head(i, c) + 1)
                pe.sem_inc(W.used, 1)

            def square_sum(i, c):
                pe.wait_ge(sq, head(i, c) + 1)
                for half in range(2):
                    last = nc.tensor.matmul(M.ps[:, 1, half * 512:(half + 1) * 512], lhsT=ones,
                                            rhs=KET[:, half * 512:(half + 1) * 512], start=True, stop=True)
                last.then_inc(n_mm, 1)

            def scores(i, c, g):
                a, b = (1, 2) if g == 0 else (3, 0)
                for j in range(4):
                    t = 4 * g + j
                    nc.tensor.matmul(M.ps[:, a, j * P:(j + 1) * P], lhsT=DK[:, t * P:(t + 1) * P],
                                     rhs=DQ[:, t * P:(t + 1) * P], start=True, stop=True)
                for n, h in enumerate(HALVES):
                    if n == 2:
                        last.then_inc(s_mm, 1)
                        if g == 0:
                            pe.wait_ge(q_cp, head(i, c) + (2 if (c < 1 or not M.last_head) else 1))
                        else:
                            pe.wait_ge(t_cp, head(i, c) + 1)
                    unit, at = (a, 512 + 256 * n) if n < 2 else (b, 256 * (n - 2))
                    for j in range(4):
                        t = 4 * g + j
                        last = nc.tensor.matmul(
                            M.ps[:, unit, at + 64 * j:at + 64 * (j + 1)], lhsT=LEV[n][:, t * P:(t + 1) * P],
                            rhs=blocks(LEV[n][:, t * P:(t + 1) * P], h)[:, :, 1, :], start=True, stop=True)
                last.then_inc(s_mm, 1)

            def body(i, c, first, last_head=False):
                h = head(i, c)
                M.last_head = last_head
                if not last_head:
                    ni, ncc = (i, c + 1) if c == 0 else (i + 1, 0)
                    w = weights(ni, ncc)
                    pe.wait_ge(*((f_cp, 1) if first else (s_cp, h * 4)))
                    project_forget(ni, ncc, w)
                if not first:
                    pi, pc = (i, 0) if c == 1 else (i - 1, 1)
                    pe.wait_ge(st, h * 7)
                    square_sum(pi, pc)
                    pe.wait_ge(o_cp, h)
                else:
                    pe.wait_ge(q_cp, 1)
                    pe.wait_ge(v_cp, 1)
                if not last_head:
                    project_rest(ni, ncc, w)
                    pe.wait_ge(f_cp, h + 2)
                elif not first:
                    pe.wait_ge(s_cp, h * 4)
                pe.wait_ge(ke, h + 1)
                for t in range(TT):
                    last = nc.tensor.transpose(M.ps[:, 0, t * P:(t + 1) * P], KE[:, t * P:(t + 1) * P], ident)
                last.then_inc(t_mm, 1)
                if not first:
                    pe.wait_ge(n_cp, h)
                scores(i, c, 0)
                pe.wait_ge(v_cp, h + (1 if last_head else 2))
                scores(i, c, 1)
                pe.wait_ge(s_cp, h * 4 + 1)
                for t in range(TT - 1):
                    last = nc.tensor.matmul(M.ps[:, 1, t * P:(t + 1) * P], lhsT=KET[:, t * P:(t + 1) * P],
                                            rhs=VAL[c][:, t, :], start=True, stop=True)
                last.then_inc(kv_mm, 1)
                pe.wait_ge(s_cp, h * 4 + 4)
                pe.wait_ge(st, h * 7 + 7)
                for t in range(TT):
                    nc.tensor.matmul(M.ps[:, 2, t * P:(t + 1) * P], lhsT=VAL[c][:, t, :],
                                     rhs=SC[:, t * P:(t + 1) * P], start=True, stop=t == 0)
                    if t:
                        last = nc.tensor.matmul(M.ps[:, 2, t * P:(t + 1) * P], lhsT=ST[:, t, :],
                                                rhs=QE[:, t * P:(t + 1) * P], start=False, stop=True)
                last.then_inc(o_mm, 1)

            w = weights(0, 0)
            project_forget(0, 0, w)
            project_rest(0, 0, w)
            loop(pe, body)
            pe.wait_ge(st, HEADS * 7)
            square_sum(HEADS // 2 - 1, 1)

        @block.scalar
        def _(act):
            act_ = nc.scalar.activation

            def forget_exp(h1):
                act.wait_ge(f_cp, h1)
                act_(KEY, KEY, ACT.Exp).then_inc(exped, 1)

            def forget_log(h1):
                act.wait_ge(gate, h1)
                act_(LOG, LOG, ACT.Ln).then_inc(log, 1)

            def copies(h1, slot, first=False):
                act.wait_ge(q_mm, h1)
                if not first:
                    act.wait_ge(lev, h1 - 1)
                act_(QRY, U2, ACT.Copy).then_inc(q_cp, 1)
                act.wait_ge(v_mm, h1)
                act_(VAL[slot], U3.rearrange("p (a n) -> p a n", a=TT), ACT.Copy).then_inc(v_cp, 1)

            def decays(h1):
                for n in range(len(HALVES)):
                    act.wait_ge(offs, (h1 - 1) * 7 + n + 1)
                    act_(LEV[n], LEV[n], ACT.Exp).then_inc(decayed, 1)
                act.wait_ge(offs, (h1 - 1) * 7 + 6)
                act_(DK, DQ, ACT.Exp, scale=-1.0).then_inc(decayed, 1)
                act.wait_ge(decayed, (h1 - 1) * 10 + 6)
                act_(DQ, DQ, ACT.Exp).then_inc(decayed, 1)
                act_(QE, CUM, ACT.Exp).then_inc(decayed, 1)
                act_(END, tiles(CUM)[:, :, P - 1], ACT.Exp).then_inc(decayed, 1)
                act.wait_ge(offs, (h1 - 1) * 7 + 7)
                act_(KE, KE, ACT.Exp).then_inc(decayed, 1)

            def inverse_norm(h1):
                act.wait_ge(n_mm, h1)
                act_(KET, U1, ACT.Ln, scale=1.0 / P, bias=M.eps).then_inc(n_cp, 1)
                act.wait_ge(n_cp, h1)
                act_(KET, KET, ACT.Exp, scale=-0.5).then_inc(rs, 1)

            def body(i, c, first, last_head=False):
                h = head(i, c)
                if not last_head:
                    forget_exp(h + 2)
                if not first:
                    inverse_norm(h)
                if not last_head:
                    forget_log(h + 2)
                    if not first:
                        act.wait_ge(o_mm, h)
                    copies(h + 2, 1 - c)
                act.wait_ge(t_mm, h + 1)
                if not first:
                    act.wait_ge(z1, h)
                act_(KET, U0, ACT.Copy).then_inc(t_cp, 1)
                act.wait_ge(o_cp, h + 1)
                act_(KET, LOG, ACT.Square).then_inc(sq, 1)
                if not last_head:
                    decays(h + 2)

            forget_exp(1)
            forget_log(1)
            copies(1, 0, True)
            decays(1)
            loop(act, body)
            inverse_norm(HEADS)

        @block.vector
        def _(dve):
            tt = nc.vector.tensor_tensor

            def forget(h1, col, before=None, first=False):
                dve.wait_ge(f_mm, h1)
                if not first:
                    dve.wait_ge(ke, h1 - 1)
                nc.vector.tensor_scalar(KEY, U0, -1.0, 40.0, ALU.mult, ALU.min).then_inc(f_cp, 1)
                if before is not None:
                    before()
                lb, oml = M.lb[:, col], M.oml[:, col]
                dve.wait_ge(exped, h1)
                nc.vector.tensor_scalar(LOG, KEY, 1.0, None, ALU.add).then_inc(plus1, 1)
                dve.wait_ge(plus1, h1)
                nc.vector.reciprocal(LOG, LOG).then_inc(recip, 1)
                dve.wait_ge(recip, h1)
                nc.vector.scalar_tensor_tensor(KEY, KEY, oml, LOG, ALU.mult, ALU.mult).then_inc(key, 1)
                nc.vector.tensor_scalar(LOG, LOG, oml, lb, ALU.mult, ALU.add).then_inc(gate, 1)
                dve.wait_ge(log, h1)
                nc.vector.tensor_tensor_scan(CUM, keep, LOG, 0.0, ALU.mult, ALU.add).then_inc(cum, 1)

            def levels(h1, first=False):
                dve.wait_ge(cum, h1)
                if not first:
                    dve.wait_ge(s_mm, (h1 - 1) * 4)
                for n, h in enumerate(HALVES):
                    b, x = blocks(CUM, h), blocks(LEV[n], h)
                    ref = b[:, :, 0, h - 1:h].to_broadcast([P, T // (2 * h), h])
                    tt(x[:, :, 0, :], ref, b[:, :, 0, :], ALU.subtract)
                    tt(x[:, :, 1, :], b[:, :, 1, :], ref, ALU.subtract).then_inc(offs, 1)
                b = CUM.rearrange("p (n f) -> p n f", f=4)
                tt(DQ.rearrange("p (n f) -> p n f", f=4), b, b[:, :, 1:2].to_broadcast([P, T // 4, 4]),
                   ALU.subtract).then_inc(offs, 1)
                if not first:
                    dve.wait_ge(t_mm, h1 - 1)
                b = tiles(CUM)
                tt(tiles(KE), b[:, :, P - 1:P].to_broadcast([P, TT, P]), b, ALU.subtract).then_inc(offs, 1)
                dve.wait_ge(q_cp, h1)
                dve.wait_ge(key, h1)
                for n, h in enumerate(HALVES):
                    dve.wait_ge(decayed, (h1 - 1) * 10 + n + 1)
                    x = blocks(LEV[n], h)
                    tt(x[:, :, 0, :], x[:, :, 0, :], blocks(KEY, h)[:, :, 0, :], ALU.mult)
                    tt(x[:, :, 1, :], x[:, :, 1, :], blocks(QRY, h)[:, :, 1, :], ALU.mult)
                dve.wait_ge(decayed, (h1 - 1) * 10 + 8)
                tt(DK, DK, KEY, ALU.mult)
                tt(DQ, DQ, QRY, ALU.mult)
                tt(QE, QE, QRY, ALU.mult).then_inc(lev, 1)
                dve.wait_ge(decayed, (h1 - 1) * 10 + 10)
                tt(KE, KE, KEY, ALU.mult).then_inc(ke, 1)

            def pick(g, at, h, data):
                out = SC[:, 512 * g:512 * (g + 1)]
                if h:
                    n = HALVES.index(h)
                    mask = M.hmask[:, 256 * n:256 * (n + 1)]
                    out = blocks(out, h)[:, :, 1, :]
                    data = data[:, at:at + 256].rearrange("p (n h) -> p n h", h=h)
                    mask = mask.rearrange("p (n h) -> p n h", h=h)
                else:
                    mask = M.hmask[:, 1280:1792]
                    data = data[:, 0:512]
                return nc.vector.copy_predicated(out, mask, data)

            def attend(h1, first=False):
                if not first:
                    dve.wait_ge(o_mm, h1 - 1)
                for g, (a, b) in enumerate(((U1, U2), (U3, U0))):
                    for n, (unit, at, h) in enumerate(((a, 0, 0), (a, 512, 64), (a, 768, 32),
                                                       (b, 0, 16), (b, 256, 8), (b, 512, 4))):
                        if n % 3 == 0:
                            dve.wait_ge(s_mm, (h1 - 1) * 4 + 2 * g + n // 3 + 1)
                        if n or g:
                            dve.wait_ge(picked if n % 3 else s_cp,
                                        (h1 - 1) * (8 if n % 3 else 4) + (4 * g + n - n // 3 if n % 3 else 2 * g + n // 3))
                        dve.sem_inc(begun, 1)
                        pick(g, at, h, unit).then_inc(s_cp if n % 3 == 2 else picked, 1)
                dve.wait_ge(kv_mm, h1)
                for t in range(TT - 1):
                    kv = U1[:, t * P:(t + 1) * P]
                    if t == 0:
                        nc.vector.tensor_copy(ST[:, 1, :], kv).then_inc(st, 1)
                    else:
                        dve.wait_ge(st, (h1 - 1) * 7 + t)
                        nc.vector.scalar_tensor_tensor(ST[:, t + 1, :], ST[:, t, :], END[:, t:t + 1], kv,
                                                       ALU.mult, ALU.add).then_inc(st, 1)
                dve.wait_ge(o_mm, h1)
                nc.vector.tensor_copy(LOG, U2).then_inc(o_cp, 1)

            def finish(h, h1):
                dve.wait_ge(rs, h1)
                dve.wait_ge(o_cp, h1)
                nc.vector.scalar_tensor_tensor(LOG, LOG, gain[:, bass.ds(h, 1)], KET, ALU.mult,
                                               ALU.mult).then_inc(z1, 1)
                dve.wait_ge(z1, h1)
                zt = M.zt[:, bass.ds(h, 1), :]
                tt(zt, zt, LOG.unsqueeze(1), ALU.mult).then_inc(z, 1)
                dve.wait_ge(z, h1)

            def body(i, c, first, last_head=False):
                h = head(i, c)
                if not last_head:
                    forget(h + 2, bass.ds(h + 1, 1), None if first else (lambda: finish(h - 1, h)))
                else:
                    finish(h - 1, h)
                attend(h + 1, first)
                if not last_head:
                    levels(h + 2)

            nc.vector.memset(SC, 0.0).then_inc(cleared, 1)
            dve.wait_ge(cleared, 1)
            forget(1, bass.ds(0, 1), None, True)
            levels(1, True)
            loop(dve, body)
            finish(HEADS - 1, HEADS)


class Cut:

    def __init__(self, ap):
        self.ap, self.at = ap, 0

    def __call__(self, n, a=None):
        assert self.at + n <= self.ap.shape[1], (self.at, n)
        piece = self.ap[:, self.at:self.at + n]
        self.at += n
        return piece if a is None else piece.rearrange("p (a n) -> p a n", a=a)


class Link:

    def __init__(self, eng, sem):
        self.eng, self.sem, self.n = eng, sem, 0

    def __call__(self, ins):
        self.n += 1
        ins.then_inc(self.sem, 1)
        self.eng.wait_ge(self.sem, self.n)


def zt_flat(M):
    return M.zt[:, :, :].rearrange("p a n -> p (a n)")


def ht_flat(M):
    return M.ht[:, :, :].rearrange("p a n -> p (a n)")


def mix_memory(M):
    z, c = Cut(zt_flat(M)), Cut(M.scr[:, :])
    M.pf = z(RT * T, RT)
    M.conv = z(CT * T, CT)
    M.qt = c(2 * T, 2)
    M.u = c(CT * (T + 2 * CPAD + 2), CT)
    M.kt = c(2 * MEM, 2)
    M.vm = c(2 * MEM, 2)
    M.mix_free = c.at


def memory_keys(nc, M, W, n0, mem, w_kv, prefetch=()):
    sem = M.semaphore
    rows, sq, root, step = (sem(f"mem_{x}") for x in ("rows_in", "squares", "root", "step"))
    turned, copied, k_mm, v_mm, done = (sem(f"mem_{x}") for x in ("turned", "copied", "keys", "values", "done"))
    c = Cut(zt_flat(M))
    rowsb, junk, mt = c(2 * D, 2), c(D), c(KD * MEM, KD)
    with nc.Block() as block:
        @block.sync
        def _(sp):
            for t in range(2):
                sp.dma_start(rowsb[:, t, :], mem[t * P:(t + 1) * P, :]).then_inc(rows, 16)
            if n0 not in M.sent:
                dma_chunk(sp, M, W, n0, n0 % 2, w_kv)
            for n, src in prefetch:
                dma_chunk(sp, M, W, n, n % 2, src)

        @block.scalar
        def _(act):
            act.wait_ge(rows, 32)
            for t in range(2):
                if t:
                    act.wait_ge(sq, t)
                nc.scalar.activation(junk, rowsb[:, t, :], ACT.Square, accum_out=M.small[:, t:t + 1]).then_inc(sq, 1)
            act.wait_ge(sq, 2)
            nc.scalar.activation(M.small[:, 8:10], M.small[:, 0:2], ACT.Sqrt, scale=1.0 / D,
                                 bias=M.eps).then_inc(root, 1)

        @block.vector
        def _(dve):
            link = Link(dve, step)
            dve.wait_ge(root, 1)
            link(nc.vector.reciprocal(M.small[:, 16:18], M.small[:, 8:10]))
            for t in range(2):
                link(nc.vector.tensor_scalar(rowsb[:, t, :], rowsb[:, t, :], M.small[:, 16 + t:17 + t], None,
                                             ALU.mult))
            for t in range(2):
                dve.wait_ge(turned, t + 1)
                nc.vector.tensor_tensor(mt[:, :, t * P:(t + 1) * P],
                                        M.ps[:, t, :].rearrange("p (k n) -> p k n", k=KD),
                                        M.p("norm_mem").unsqueeze(2).to_broadcast([P, KD, P]),
                                        ALU.mult).then_inc(copied, 1)
            dve.wait_ge(k_mm, 1)
            nc.vector.tensor_copy(M.kt, M.ps[:, 2, 0:2 * MEM].rearrange("p (a n) -> p a n", a=2)).then_inc(done, 1)
            dve.wait_ge(v_mm, 1)
            nc.vector.tensor_copy(M.vm, M.ps[:, 3, 0:2 * MEM].rearrange("p (a n) -> p a n", a=2)).then_inc(done, 1)

        @block.tensor
        def _(pe):
            for t in range(2):
                pe.wait_ge(step, 2 + t)
                for k in range(KD):
                    last = nc.tensor.transpose(M.ps[:, t, k * P:(k + 1) * P], rowsb[:, t, k * P:(k + 1) * P],
                                               M.c("ident"))
                last.then_inc(turned, 1)
            pe.wait_ge(copied, 2)
            W.wait(pe, n0)
            w = slot_view(M, n0 % 2, KD, 2 * MEM)
            for a in range(2):
                for k in range(KD):
                    last = nc.tensor.matmul(M.ps[:, 2, a * MEM:(a + 1) * MEM], lhsT=w[:, k, a * P:(a + 1) * P],
                                            rhs=mt[:, k, :], start=k == 0, stop=k == KD - 1)
            last.then_inc(k_mm, 1)
            for a in range(2):
                for k in range(KD):
                    last = nc.tensor.matmul(M.ps[:, 3, a * MEM:(a + 1) * MEM], lhsT=mt[:, k, a * P:(a + 1) * P],
                                            rhs=w[:, k, MEM:2 * MEM], start=k == 0, stop=k == KD - 1)
            last.then_inc(v_mm, 1)
            pe.wait_ge(v_mm, 1)
            pe.sem_inc(W.used, 1)


def mixer_projections(nc, M, W, n0, w_in, prefetch=()):
    sem = M.semaphore
    summed, copied, gated, glu = (sem(f"mix_{x}") for x in ("summed", "copied", "gated", "glu"))
    ready, step, shifted, conv = (sem(f"mix_{x}") for x in ("ready", "step", "shifted", "conv"))
    taps = [sem(f"conv_tap_{j}") for j in range(CT)]
    c = Cut(M.scr[:, M.mix_free:])
    val = c(CT * T, CT)
    raw = [c(T + 2) for _ in range(2)]
    mu0, mu1 = M.p("mu_prev"), M.p("mu_next")
    own = M.small[:, 32:32 + RT]
    taps_w = M.p("conv_w").rearrange("p (a k) -> p a k", a=CT)
    TILES = 20
    RW0 = TILES - RT
    with nc.Block() as block:
        @block.sync
        def _(sp):
            for j in range(TILES // 4):
                if n0 + j not in M.sent:
                    dma_chunk(sp, M, W, n0 + j, (n0 + j) % 2, w_in[j])
            for n, src in prefetch:
                dma_chunk(sp, M, W, n, n % 2, src)

        @block.tensor
        def _(pe):
            for j in range(TILES // 4):
                n = n0 + j
                W.wait(pe, n)
                w = slot_view(M, n % 2, KD, 512)
                for m in range(4):
                    u = 4 * j + m
                    if u >= 4:
                        pe.wait_ge(copied, u - 3)
                    feature_tile(nc, M, u % 4, w, slice(m * P, (m + 1) * P)).then_inc(summed, 1)
                pe.wait_ge(summed, 4 * j + 4)
                pe.sem_inc(W.used, 1)

        @block.scalar
        def _(act):
            act.wait_ge(ready, 1)
            for u in range(TILES):
                act.wait_ge(summed, u + 1)
                src = M.ps[:, u % 4, :]
                if u < 2:
                    nc.scalar.activation(M.qt[:, u, :], src, ACT.Copy).then_inc(copied, 1)
                elif u < 2 + CT:
                    nc.scalar.activation(val[:, u - 2, :], src, ACT.Copy).then_inc(copied, 1)
                elif u < RW0:
                    nc.scalar.activation(M.u[:, u - 2 - CT, CPAD:CPAD + T], src, ACT.Sigmoid).then_inc(copied, 1)
                else:
                    r = u - RW0
                    if r >= 2:
                        act.wait_ge(shifted, r - 1)
                    nc.scalar.activation(raw[r % 2][:, 1:1 + T], src, ACT.Copy).then_inc(copied, 1)

        @block.vector
        def _(dve):
            link = Link(dve, step)
            link(nc.vector.memset(M.u, 0.0))
            link(nc.vector.memset(raw[0], 0.0))
            link(nc.vector.memset(raw[1], 0.0))
            link(nc.vector.tensor_tensor(own, mu0, mu1, ALU.add))
            nc.vector.tensor_scalar(own, own, -1.0, 1.0, ALU.mult, ALU.add).then_inc(ready, 1)
            dve.wait_ge(ready, 1)
            dve.wait_ge(copied, RW0)
            mid = M.u[:, :, CPAD:CPAD + T]
            link(nc.vector.tensor_tensor(mid, mid, val, ALU.mult))

            def tap(k, a):
                x = M.u[:, a, k:k + T]
                if k == 0:
                    nc.vector.tensor_scalar(M.conv[:, a, :], x, taps_w[:, a, 0:1], M.p("conv_b")[:, a:a + 1],
                                            ALU.mult, ALU.add).then_inc(taps[a], 1)
                else:
                    dve.wait_ge(taps[a], k)
                    nc.vector.scalar_tensor_tensor(M.conv[:, a, :], x, taps_w[:, a, k:k + 1], M.conv[:, a, :],
                                                   ALU.mult, ALU.add).then_inc(taps[a], 1)

            todo = [(k, a) for k in range(CONV_K) for a in range(CT)]
            for r in range(RT):
                dve.wait_ge(copied, RW0 + r + 1)
                x, y = raw[r % 2], M.pf[:, r, :]
                link(nc.vector.tensor_scalar(y, x[:, 1:1 + T], own[:, r:r + 1], None, ALU.mult))
                link(nc.vector.scalar_tensor_tensor(y, x[:, 0:T], mu0[:, r:r + 1], y, ALU.mult, ALU.add))
                nc.vector.scalar_tensor_tensor(y, x[:, 2:2 + T], mu1[:, r:r + 1], y, ALU.mult,
                                               ALU.add).then_inc(shifted, 1)
                dve.wait_ge(shifted, r + 1)
                for k, a in todo[:8]:
                    tap(k, a)
                todo = todo[8:]
            for k, a in todo:
                tap(k, a)
            for a in range(CT):
                dve.wait_ge(taps[a], CONV_K)


def attention(nc, M):
    sem = M.semaphore
    s_mm, mx, ng, ex, rc, pr = (sem(f"att_{x}") for x in ("scores", "max", "bias", "exp", "recip", "probs"))
    p_mm, p_cp, o_mm, o_cp = (sem(f"att_{x}") for x in ("probs_turned", "probs_copied", "out_summed", "out_copied"))
    c = Cut(M.scr[:, M.mix_free:])
    prob = [c(AH * MEM, AH) for _ in range(2)]
    pt = [c(AH * MEM) for _ in range(2)]
    scale = 64.0 ** -0.5
    ORDER = (0, 2, 1, 3)

    def stat(j, t):
        return M.small[:, 24 * (t % 2) + 4 * j:24 * (t % 2) + 4 * j + 4]

    with nc.Block() as block:
        @block.tensor
        def _(pe):
            def scores(t):
                if t >= 2:
                    pe.wait_ge(ex, AH * (t - 1))
                for at, a in enumerate(ORDER):
                    o = 64 * (a % 2)
                    last = nc.tensor.matmul(M.ps[:, t % 2, at * MEM:(at + 1) * MEM],
                                            lhsT=M.qt[o:o + 64, a // 2, t * P:(t + 1) * P],
                                            rhs=M.kt[o:o + 64, a // 2, :], start=True, stop=True)
                last.then_inc(s_mm, 1)

            scores(0)
            for t in range(TT):
                if t + 1 < TT:
                    scores(t + 1)
                pe.wait_ge(pr, t + 1)
                if t:
                    pe.wait_ge(p_cp, t)
                for a in range(AH):
                    for m in range(2):
                        j = 2 * a + m
                        last = nc.tensor.transpose(M.ps[:, 2, j * P:(j + 1) * P],
                                                   prob[t % 2][:, a, m * P:(m + 1) * P], M.c("ident"))
                last.then_inc(p_mm, 1)
                pe.wait_ge(p_cp, t + 1)
                if t:
                    pe.wait_ge(o_cp, t)
                for at, a in enumerate(ORDER):
                    o = 64 * (a % 2)
                    for m in range(2):
                        j = 2 * at + m
                        last = nc.tensor.matmul(M.ps[o:o + 64, 3, (a // 2) * P:(a // 2 + 1) * P],
                                                lhsT=M.vm[:, m, 64 * a:64 * a + 64],
                                                rhs=pt[t % 2][:, j * P:(j + 1) * P], start=m == 0, stop=m == 1)
                last.then_inc(o_mm, 1)

        @block.scalar
        def _(act):
            def exps(t):
                act.wait_ge(ng, t + 1)
                if t >= 2:
                    act.wait_ge(p_mm, t - 1)
                for a in range(AH):
                    nc.scalar.activation(prob[t % 2][:, a, :], M.ps[:, t % 2, a * MEM:(a + 1) * MEM], ACT.Exp,
                                         scale=scale, bias=stat(1, t)[:, a:a + 1],
                                         accum_out=stat(2, t)[:, a:a + 1]).then_inc(ex, 1)

            def probs_copy(t):
                act.wait_ge(p_mm, t + 1)
                if t >= 2:
                    act.wait_ge(o_mm, t - 1)
                nc.scalar.activation(pt[t % 2], M.ps[:, 2, :], ACT.Copy).then_inc(p_cp, 1)

            exps(0)
            for t in range(TT):
                if t + 1 < TT:
                    exps(t + 1)
                probs_copy(t)

        @block.vector
        def _(dve):
            def maxes(t):
                dve.wait_ge(s_mm, t + 1)
                if t >= 2:
                    dve.wait_ge(ex, AH * (t - 1))
                nc.vector.reduce_max(stat(0, t), M.ps[:, t % 2, :].rearrange("p (a n) -> p a n", a=AH),
                                     mybir.AxisListType.X).then_inc(mx, 1)
                dve.wait_ge(mx, t + 1)
                nc.vector.tensor_scalar(stat(1, t), stat(0, t), -scale, None, ALU.mult).then_inc(ng, 1)

            maxes(0)
            for t in range(TT):
                if t + 1 < TT:
                    maxes(t + 1)
                dve.wait_ge(ex, AH * (t + 1))
                nc.vector.reciprocal(stat(3, t), stat(2, t)).then_inc(rc, 1)
                dve.wait_ge(rc, t + 1)
                nc.vector.tensor_tensor(prob[t % 2], prob[t % 2],
                                        stat(3, t).unsqueeze(2).to_broadcast([P, AH, MEM]),
                                        ALU.mult).then_inc(pr, 1)
                dve.wait_ge(o_mm, t + 1)
                nc.vector.tensor_copy(M.ht[:, 0:2, t * P:(t + 1) * P],
                                      M.ps[:, 3, 0:2 * P].rearrange("p (a n) -> p a n", a=2)).then_inc(o_cp, 1)


def conv_norm(nc, M):
    sem = M.semaphore
    m_mm, cen, sq, v_mm, root, step, fin = (
        sem(f"cn_{x}") for x in ("mean", "centred", "squared", "var", "root", "step", "out"))
    c = Cut(M.scr[:, M.mix_free:])
    sqr, mean = c(CT * T, CT), c(T)
    eps = M.small[:, 62:63]
    width = CT * P

    def channel_sum(unit, x):
        for half in range(2):
            for a in range(CT):
                last = nc.tensor.matmul(M.ps[:, unit, half * 512:(half + 1) * 512], lhsT=M.c("ones"),
                                        rhs=x[:, a, half * 512:(half + 1) * 512], start=a == 0, stop=a == CT - 1)
        return last

    with nc.Block() as block:
        @block.tensor
        def _(pe):
            channel_sum(0, M.conv).then_inc(m_mm, 1)
            pe.wait_ge(sq, 1)
            channel_sum(1, sqr).then_inc(v_mm, 1)

        @block.scalar
        def _(act):
            act.wait_ge(cen, CT)
            nc.scalar.activation(sqr, M.conv, ACT.Square).then_inc(sq, 1)
            act.wait_ge(v_mm, 1)
            nc.scalar.activation(mean, M.ps[:, 1, :], ACT.Sqrt, scale=1.0 / width, bias=eps).then_inc(root, 1)
            for a in range(CT):
                act.wait_ge(step, 3 + a)
                nc.scalar.activation(M.ht[:, 2 + a, :], M.conv[:, a, :], ACT.Silu,
                                     scale=M.p("conv_g")[:, a:a + 1], bias=M.p("conv_beta")[:, a:a + 1]).then_inc(fin, 1)

        @block.vector
        def _(dve):
            link = Link(dve, step)
            link(nc.vector.memset(eps, 1e-5))
            dve.wait_ge(m_mm, 1)
            for a in range(CT):
                nc.vector.scalar_tensor_tensor(M.conv[:, a, :], M.ps[:, 0, :], -1.0 / width, M.conv[:, a, :],
                                               ALU.mult, ALU.add).then_inc(cen, 1)
            dve.wait_ge(root, 1)
            link(nc.vector.reciprocal(mean, mean))
            for a in range(CT):
                link(nc.vector.tensor_tensor(M.conv[:, a, :], M.conv[:, a, :], mean, ALU.mult))


def rwkv_common(nc, M, small_w, vt_dram, g_dram, prefetch=(), W=None):
    sem = M.semaphore
    w_in, ranks, step, sqd, ssq = (sem(f"rc_{x}") for x in ("weights_in", "ranks", "step", "squared", "square_sum"))
    root, vt_mm, vt_cp, g_mm, g_cp, out = (
        sem(f"rc_{x}") for x in ("root", "values_turned", "values_copied", "gate_summed", "gate_copied", "stored"))
    z, c, h = Cut(zt_flat(M)[:, RT * T:]), Cut(M.scr[:, :]), Cut(ht_flat(M)[:, 5 * T:])
    M.rw_w = z(9 * P, 3)
    M.kk = c(CT * T, CT)
    M.ks = c(CT * T, CT)
    M.rw_tiles = [c(T) for _ in range(12)] + [z(T) for _ in range(2)]
    sq = c.ap[:, 6 * T:9 * T].rearrange("p (a n) -> p a n", a=CT)
    vt = c.ap[:, 9 * T:12 * T].rearrange("p (a c n) -> p a c n", a=CT, n=P)
    g = c.ap[:, 12 * T:15 * T].rearrange("p (a n) -> p a n", a=CT)
    eps = M.small[:, 61:62]
    PS = M.ps
    with nc.Block() as block:
        @block.sync
        def _(sp):
            sp.dma_start(M.rw_w, small_w.rearrange("p (a n) -> p a n", a=3)).then_inc(w_in, 16)
            for n, src in prefetch:
                dma_chunk(sp, M, W, n, n % 2, src)
            for a in range(CT):
                sp.wait_ge(vt_cp, a + 1)
                sp.dma_start(vt_dram[:, :, a * P:(a + 1) * P].rearrange("c p n -> p c n"), vt[:, a]).then_inc(out, 16)
            for a in range(CT):
                sp.wait_ge(g_cp, a + 1)
                sp.dma_start(g_dram[a], g[:, a, :]).then_inc(out, 16)
            sp.wait_ge(out, 16 * 6)

        @block.scalar
        def _(act):
            nc.scalar.activation(M.pf[:, 11, :], M.pf[:, 11, :], ACT.Sigmoid).then_inc(ranks, 1)
            nc.scalar.activation(M.pf[:, 9, :], M.pf[:, 9, :], ACT.Tanh).then_inc(ranks, 1)
            for a in range(CT):
                act.wait_ge(vt_mm, a + 1)
                nc.scalar.activation(vt[:, a].rearrange("p c n -> p (c n)"), PS[:, a, :], ACT.Copy).then_inc(vt_cp, 1)
            for a in range(CT):
                act.wait_ge(g_mm, a + 1)
                nc.scalar.activation(g[:, a, :], PS[:, a, :], ACT.Copy).then_inc(g_cp, 1)
            for a in range(CT):
                act.wait_ge(ssq, a + 1)
                act.wait_ge(sqd, 2)
                nc.scalar.activation(sq[:, a, :], PS[:, (a + 3) % 4, :], ACT.Sqrt, bias=eps).then_inc(root, 1)

        @block.tensor
        def _(pe):
            for a in range(CT):
                for t in range(TT):
                    last = nc.tensor.transpose(PS[:, a, t * P:(t + 1) * P], M.pf[:, 6 + a, t * P:(t + 1) * P],
                                               M.c("ident"))
                last.then_inc(vt_mm, 1)
            pe.wait_ge(w_in, 16)
            pe.wait_ge(ranks, 1)
            for a in range(CT):
                pe.wait_ge(vt_cp, a + 1)
                for half in range(2):
                    last = nc.tensor.matmul(PS[:, a, half * 512:(half + 1) * 512],
                                            lhsT=M.rw_w[:, 2, a * P:(a + 1) * P],
                                            rhs=M.pf[:, 11, half * 512:(half + 1) * 512], start=True, stop=True)
                last.then_inc(g_mm, 1)
            pe.wait_ge(sqd, 1)
            for a in range(CT):
                if a:
                    pe.wait_ge(g_cp, a)
                for half in range(2):
                    last = nc.tensor.matmul(PS[:, (a + 3) % 4, half * 512:(half + 1) * 512], lhsT=M.c("blocks64"),
                                            rhs=sq[:, a, half * 512:(half + 1) * 512], start=True, stop=True)
                last.then_inc(ssq, 1)
            pe.wait_ge(ssq, CT)
            pe.sem_inc(sqd, 1)

        @block.vector
        def _(dve):
            link = Link(dve, step)
            link(nc.vector.memset(eps, 1e-12))
            k = M.pf[:, 3:6, :]
            link(nc.vector.tensor_tensor(M.kk, k, M.p("k_k").unsqueeze(2).to_broadcast([P, CT, T]), ALU.mult))
            nc.vector.tensor_tensor(sq, M.kk, M.kk, ALU.mult).then_inc(sqd, 1)
            dve.wait_ge(root, CT)
            link(nc.vector.reciprocal(sq, sq))
            link(nc.vector.tensor_tensor(M.kk, M.kk, sq, ALU.mult))


def rwkv_directions(nc, M, rw_dram, bonus_dram):
    sem = M.semaphore
    up, sw, aa, lw, cum, kd, offs = (sem(f"rd_{x}") for x in ("ranks_up", "decay", "rate", "log", "cum", "key", "offs"))
    bo, ex, prod, out, step, c_mm, c_cp, cr = (
        sem(f"rd_{x}") for x in ("ks", "exps", "products", "stored", "step", "coef", "bonus", "carry"))
    tiles = M.rw_tiles
    PS = M.ps

    def t8(ap):
        return ap.rearrange("p (c n) -> p c n", n=P)

    def bufs(n):
        return tiles[7 * (n % 2):7 * (n % 2) + 7]

    with nc.Block() as block:
        @block.tensor
        def _(pe):
            for n in range(6):
                d, p = divmod(n, CT)
                o = 64 * d
                for j in range(2):
                    if n >= 2:
                        pe.wait_ge((sw, aa)[j], n - 1)
                    for half in range(2):
                        last = nc.tensor.matmul(PS[:, 2 * (n % 2) + j, half * 512:(half + 1) * 512],
                                                lhsT=M.rw_w[o:o + 64, j, p * P:(p + 1) * P],
                                                rhs=M.pf[o:o + 64, 9 + j, half * 512:(half + 1) * 512],
                                                start=True, stop=True)
                    last.then_inc(up, 1)
            for p in range(CT):
                pe.wait_ge(bo, 1 + p)
                pe.wait_ge(aa, 6)
                for half in range(2):
                    last = nc.tensor.matmul(PS[:, p, half * 512:(half + 1) * 512], lhsT=M.c("blocks64"),
                                            rhs=M.ks[:, p, half * 512:(half + 1) * 512], start=True, stop=True)
                last.then_inc(c_mm, 1)

        @block.scalar
        def _(act):
            def sigmoids(n):
                T0, T1 = bufs(n)[0:2]
                if n >= 2:
                    act.wait_ge(out, 64 * (n - 1))
                act.wait_ge(up, 2 * n + 1)
                nc.scalar.activation(T0, PS[:, 2 * (n % 2), :], ACT.Sigmoid,
                                     bias=M.p("w0")[:, n:n + 1]).then_inc(sw, 1)
                act.wait_ge(up, 2 * n + 2)
                nc.scalar.activation(T1, PS[:, 2 * (n % 2) + 1, :], ACT.Sigmoid,
                                     bias=M.p("a0")[:, n:n + 1]).then_inc(aa, 1)

            sigmoids(0)
            sigmoids(1)
            for n in range(6):
                T2, T4, T5, T6 = (bufs(n)[j] for j in (2, 4, 5, 6))
                act.wait_ge(offs, 2 * n + 2)
                nc.scalar.activation(T4, T4, ACT.Exp).then_inc(ex, 1)
                nc.scalar.activation(T5, T2, ACT.Exp).then_inc(ex, 1)
                nc.scalar.activation(T6, T2, ACT.Exp, scale=-1.0).then_inc(ex, 1)
                if n + 2 < 6:
                    sigmoids(n + 2)
            act.wait_ge(cr, 12)
            nc.scalar.activation(M.carry[:, :, :], M.carry[:, :, :], ACT.Exp).then_inc(ex, 1)

        @block.vector
        def _(dve):
            tt, stt, ts = nc.vector.tensor_tensor, nc.vector.scalar_tensor_tensor, nc.vector.tensor_scalar
            link = Link(dve, step)

            def offsets(n):
                d, p = divmod(n, CT)
                T0, T1, T2, T3, T4, _, _ = bufs(n)
                mid, end = ((63, P - 1), (64, 0))[d]
                dve.wait_ge(sw, n + 1)
                link(ts(T0, T0, -DECAY_SCALE, None, ALU.mult))
                keep = M.hmask[:, 1792 + T * d:1792 + T * (d + 1)]
                if d == 0:
                    link(nc.vector.tensor_tensor_scan(T2, keep, T0, 0.0, ALU.mult, ALU.add))
                else:
                    link(nc.vector.tensor_tensor_scan(T2[:, ::-1], keep[:, ::-1], T0[:, ::-1], 0.0,
                                                      ALU.mult, ALU.add))
                cm = t8(T2)
                mids, ends = cm[:, :, mid], cm[:, :, end]
                if d == 1:
                    mids, ends = mids[:, ::-1], ends[:, ::-1]
                col = M.carry[:, :, n]
                tt(col, ends, mids, ALU.subtract).then_inc(cr, 1)
                dve.wait_ge(cr, 2 * n + 1)
                tt(col[:, 0:TT - 1], col[:, 0:TT - 1], mids[:, 1:TT], ALU.add).then_inc(cr, 1)
                dve.wait_ge(aa, n + 1)
                link(ts(T3, T1, -1.0, M.p("k_a")[:, p:p + 1], ALU.add, ALU.mult))
                link(stt(T3, T3, 1.0, M.pf[:, 3 + p, :], ALU.add, ALU.mult))
                if d == 0:
                    link(nc.vector.tensor_copy(M.ks[:, p, :], T3))
                else:
                    link(tt(M.ks[:, p, :], M.ks[:, p, :], T3, ALU.add))
                link(tt(T1, T1, M.kk[:, p, :], ALU.mult))
                dve.wait_ge(cr, 2 * n + 2)
                T5 = bufs(n)[5]
                link(nc.vector.tensor_copy(T5[:, 0:TT], cm[:, :, mid]))
                tt(cm, cm, T5[:, 0:TT].unsqueeze(2).to_broadcast([P, TT, P]), ALU.subtract).then_inc(offs, 1)
                dve.wait_ge(offs, 2 * n + 1)
                tt(T4, T2, T0, ALU.subtract).then_inc(offs, 1)

            def products(n):
                d, p = divmod(n, CT)
                _, T1, _, T3, T4, T5, T6 = bufs(n)
                dve.wait_ge(ex, 3 * n + 3)
                tt(T4, T4, M.kk[:, p, :], ALU.mult).then_inc(prod, 1)
                tt(T5, T5, M.pf[:, p, :], ALU.mult).then_inc(prod, 1)
                tt(T1, T1, T6, ALU.mult).then_inc(prod, 1)
                tt(T3, T3, T6, ALU.mult).then_inc(prod, 1)

            offsets(0)
            for n in range(6):
                if n + 1 < 6:
                    if n >= 1:
                        dve.wait_ge(out, 64 * n)
                    offsets(n + 1)
                products(n)
            for p in range(CT):
                stt(M.ks[:, p, :], M.ks[:, p, :], M.p("r_k")[:, p:p + 1], M.pf[:, p, :], ALU.mult,
                    ALU.mult).then_inc(bo, 1)
            for p in range(CT):
                dve.wait_ge(c_mm, p + 1)
                tt(M.ks[:, p, :], PS[:, p, :], M.pf[:, 6 + p, :], ALU.mult).then_inc(c_cp, 1)

        @block.sync
        def _(sp):
            for n in range(6):
                d, p = divmod(n, CT)
                b = bufs(n)
                for w, j in enumerate((4, 5, 1, 3)):
                    sp.wait_ge(prod, 4 * n + w + 1)
                    at = (4 * p + w) * P
                    sp.dma_start(rw_dram[d, :, :, at:at + P].rearrange("c p n -> p c n"), t8(b[j])).then_inc(out, 16)
            for p in range(CT):
                sp.wait_ge(c_cp, p + 1)
                sp.dma_start(bonus_dram[p], M.ks[:, p, :]).then_inc(out, 16)
            sp.wait_ge(out, 16 * (24 + CT))


def rwkv_steps(nc, M, rw_dram, vt_dram, masks_dram):
    sem = M.semaphore
    loaded = [sem(f"rs_loaded_{c}") for c in range(2)]
    m_in, zero = sem("rs_masks_in"), sem("rs_zeroed")
    a_mm, a_cp, init, initp = sem("rs_triangles"), sem("rs_triangles_masked"), sem("rs_inverse_begun"), sem("rs_pairs")
    p_mm, p_cp, x_mm, x_cp = (sem(f"rs_{x}") for x in ("half_summed", "half_masked", "join_summed", "joined"))
    t_mm, t_cp, r_mm, r_cp, u_mm, u_cp = (
        sem(f"rs_{x}") for x in ("turned", "turned_copied", "rhs_summed", "rhs_copied", "u_summed", "u_copied"))
    y_mm, y_cp, s_mm, s_ad, s_cp = (sem(f"rs_{x}") for x in ("y_summed", "y_added", "state_summed", "state_added",
                                                           "state_ready"))
    c = Cut(zt_flat(M))
    e = Cut(M.scr[:, :])
    IN = [c(2 * 3 * 4 * P).rearrange("p (d a w n) -> p d a w n", d=2, a=3, w=4) for _ in range(2)]
    V = [c(2 * CT * P, 2) for _ in range(2)]
    KM = [c(CT * 256, CT) for _ in range(4)]
    LL = [c(CT * P, CT) for _ in range(4)]
    X = [c(CT * P, CT) for _ in range(4)]
    BM = [e(CT * 256, CT) for _ in range(4)]
    Z = [e(CT * P, CT) for _ in range(4)]
    P1 = [[e(CT * P, CT) for _ in range(2)] for _ in JOINS]
    R0 = [e(2 * CT * 64).rearrange("p (d a n) -> p d a n", d=2, a=CT) for _ in range(2)]
    U = e(2 * CT * P, 2)
    TOK = e(12 * P, 12)
    MASKS = e(RWM_N)
    SM = [c(6 * 64, 6) for _ in range(2)]
    Y = M.ht[:, 5:8, :]

    def mask(name):
        a, n = RWM[name]
        return MASKS[:, a:a + n]

    rwm, pair = mask("rw_mask"), mask("pair_mask")
    F = M.ps[:, :, :].rearrange("p a n -> p (a n)")
    L = len(JOINS)

    def b3(ap):
        return ap.unsqueeze(1).to_broadcast([P, CT, ap.shape[1]])

    def halves(ap, b):
        return ap.rearrange("p a (n two h) -> p a n two h", two=2, h=b)

    groups = [(g // 2, g % 2) for g in range(4)]

    def run(eng, body):
        body(0, 0, True)
        body(0, 1, False)
        with eng.Fori(1, TT // 2) as i:
            body(i, 0, False)
            body(i, 1, False)

    with nc.Block() as block:
        @block.sync
        def _(sp):
            sp.dma_start(MASKS, masks_dram).then_inc(m_in, 16)

            def load(i, c):
                s = i * 2 + c
                chunks = (s, -s + (TT - 1))
                for d in range(2):
                    src = rw_dram[d, bass.ds(chunks[d], 1), :, :].rearrange("o p n -> (o p) n")
                    sp.dma_start(IN[c][:, d].rearrange("p a w n -> p (a w n)"), src).then_inc(loaded[c], 16)
                    sp.dma_start(V[c][:, d, :], vt_dram[bass.ds(chunks[d], 1), :, :].rearrange("o p n -> (o p) n")
                                 ).then_inc(loaded[c], 16)

            load(0, 0)
            load(0, 1)
            with sp.Fori(1, TT // 2) as i:
                for c in range(2):
                    sp.wait_ge(y_mm, i * 2 + (c - 1))
                    load(i, c)

        @block.tensor
        def _(pe):
            def body(i, c, first):
                s = i * 2 + c
                inp, v, sm = IN[c], V[c], SM[c]
                pe.wait_ge(loaded[c], i * 64 + 64)
                for g, (d, par) in enumerate(groups):
                    o, base = 64 * par, 2048 * par
                    if g < 2:
                        if not first:
                            if g == 0:
                                pe.wait_ge(t_cp, s)
                            else:
                                pe.wait_ge(y_cp, s)
                                pe.wait_ge(s_ad, s)
                    else:
                        pe.wait_ge(a_cp, s * 4 + (g - 1))
                    for p in range(CT):
                        k, b, a = (inp[o:o + 64, d, p, w, :] for w in (0, 2, 3))
                        kr = inp[o:o + 64, d, p, 0:2, :].rearrange("p w n -> p (w n)")
                        nc.tensor.matmul(F[:, base + 256 * p:base + 256 * (p + 1)], lhsT=b, rhs=kr,
                                         start=True, stop=True)
                        at = base + 768 + 256 * p
                        nc.tensor.matmul(F[:, at:at + 256], lhsT=a, rhs=kr, start=True, stop=True)
                        at = base + 1536 + P * p
                        last = nc.tensor.matmul(F[:, at:at + P], lhsT=k, rhs=b, start=True, stop=True)
                    last.then_inc(a_mm, 1)
                pe.wait_ge(a_cp, s * 4 + 4)
                for n, b in enumerate(JOINS):
                    for g, (d, par) in enumerate(groups):
                        if n == 0:
                            pe.wait_ge(init, s * 4 + (g + 1))
                        else:
                            pe.wait_ge(x_cp, s * (4 * L) + (4 * (n - 1) + g + 1))
                        low = LL[g] if d else BM[g]
                        for p in range(CT):
                            at = 512 * g + 64 * p
                            last = nc.tensor.matmul(F[:, at:at + 64], lhsT=low[:, p, 0:P],
                                                    rhs=halves(X[g], b)[:, p, :, 0, :], start=True, stop=True)
                        last.then_inc(p_mm, 1)
                    for g, (d, par) in enumerate(groups):
                        pe.wait_ge(p_cp, s * (4 * L) + (4 * n + g + 1))
                        p1 = P1[n][g % 2]
                        for p in range(CT):
                            at = 2048 + 512 * g + 64 * p
                            if n < L - 1 or d == 1:
                                last = nc.tensor.matmul(F[:, at:at + 64], lhsT=Z[g][:, p, :],
                                                        rhs=halves(p1, b)[:, p, :, 0, :], start=True, stop=True)
                            if n < L - 1 or d == 0:
                                last = nc.tensor.matmul(F[:, at + 192:at + 256], lhsT=p1[:, p, :],
                                                        rhs=halves(Z[g], b)[:, p, :, 1, :], start=True, stop=True)
                        last.then_inc(x_mm, 1)
                for w in range(2):
                    for dp in range(6):
                        at = (6 * w + dp) * P
                        last = nc.tensor.transpose(F[:, at:at + P], inp[:, dp // 3, dp % 3, 2 + w, :], M.c("ident"))
                last.then_inc(t_mm, 1)
                pe.wait_ge(x_cp, s * (4 * L) + 4 * L)
                pe.wait_ge(zero, 1)
                if not first:
                    pe.wait_ge(s_cp, s)
                for g, (d, par) in enumerate(groups):
                    o = 64 * par
                    for p in range(CT):
                        at = 2048 + 512 * par + 192 * d + 64 * p
                        nc.tensor.matmul(F[:, at:at + 64], lhsT=inp[o:o + 64, d, p, 0, :], rhs=sm[o:o + 64, 3 * d + p, :],
                                         start=True, stop=False)
                        h = 64 * (2 * p + par)
                        last = nc.tensor.matmul(F[:, at:at + 64], lhsT=KM[g][:, p, 0:P], rhs=v[:, d, h:h + 64],
                                                start=False, stop=True)
                last.then_inc(r_mm, 1)
                pe.wait_ge(r_cp, s * 2 + 2)
                for g, (d, par) in enumerate(groups):
                    inv_t = X[g] if d else Z[g]
                    for p in range(CT):
                        at = 3072 + 512 * d + 64 * (2 * p + par)
                        last = nc.tensor.matmul(F[:, at:at + 64], lhsT=inv_t[:, p, :], rhs=R0[par][:, d, p, :],
                                                start=True, stop=True)
                last.then_inc(u_mm, 1)
                pe.wait_ge(t_cp, s + 1)
                pe.wait_ge(u_cp, s + 1)
                for g, (d, par) in enumerate(groups):
                    o = 64 * par
                    for p in range(CT):
                        at, h = 3072 + 64 * (3 * d + p), 64 * (2 * p + par)
                        nc.tensor.matmul(F[o:o + 64, at:at + 64], lhsT=TOK[:, 3 * d + p, o:o + 64],
                                         rhs=U[:, d, h:h + 64], start=True, stop=False)
                        last = nc.tensor.matmul(F[o:o + 64, at:at + 64], lhsT=TOK[:, 6 + 3 * d + p, o:o + 64],
                                                rhs=v[:, d, h:h + 64], start=False, stop=True)
                last.then_inc(s_mm, 1)
                for g, (d, par) in enumerate(groups):
                    o = 64 * par
                    for p in range(CT):
                        at, h = 2048 + 512 * d + P * p, 64 * (2 * p + par)
                        y = F[o:o + 64, at:at + P]
                        nc.tensor.matmul(y, lhsT=U[:, d, h:h + 64], rhs=BM[g][:, p, P:2 * P], start=True, stop=False)
                        nc.tensor.matmul(y, lhsT=v[:, d, h:h + 64], rhs=KM[g][:, p, P:2 * P], start=False, stop=False)
                        last = nc.tensor.matmul(y, lhsT=sm[o:o + 64, 3 * d + p, :], rhs=inp[o:o + 64, d, p, 1, :],
                                                start=False, stop=True)
                last.then_inc(y_mm, 1)

            run(pe, body)

        @block.scalar
        def _(act):
            def body(i, c, first):
                s = i * 2 + c
                act.wait_ge(t_mm, s + 1)
                if not first:
                    act.wait_ge(s_mm, s)
                nc.scalar.activation(TOK.rearrange("p a n -> p (a n)"), F[:, 0:12 * P], ACT.Copy).then_inc(t_cp, 1)
                act.wait_ge(r_mm, s + 1)
                for par in range(2):
                    at = 2048 + 512 * par
                    nc.scalar.activation(R0[par].rearrange("p d a n -> p (d a n)"), F[:, at:at + 384], ACT.Copy,
                                         scale=-1.0).then_inc(r_cp, 1)
            run(act, body)

        @block.gpsimd
        def _(pool):
            def body(i, c, first):
                s = i * 2 + c
                for g, (d, par) in enumerate(groups):
                    pool.wait_ge(a_cp, s * 4 + (g + 1))
                    if not first:
                        pool.wait_ge(u_mm, s)
                    src = (LL[g], BM[g][:, :, 0:P]) if d == 0 else (BM[g][:, :, 0:P], LL[g])
                    nc.gpsimd.tensor_tensor(X[g], src[0], b3(pair[:, 0:P]), ALU.mult).then_inc(initp, 1)
                    nc.gpsimd.tensor_tensor(Z[g], src[1], b3(pair[:, P:2 * P]), ALU.mult).then_inc(initp, 1)
                    pool.wait_ge(initp, s * 12 + (3 * g + 2))
                    nc.gpsimd.tensor_tensor(X[g], X[g], b3(M.c("ident")), ALU.add).then_inc(initp, 1)
                    nc.gpsimd.tensor_tensor(Z[g], Z[g], b3(M.c("ident")), ALU.add).then_inc(init, 1)
                    pool.wait_ge(initp, s * 12 + (3 * g + 3))

            pool.wait_ge(m_in, 16)
            run(pool, body)

        @block.vector
        def _(dve):
            tt = nc.vector.tensor_tensor

            def body(i, c, first):
                s = i * 2 + c
                sm, new = SM[c], SM[1 - c]
                for g, (d, par) in enumerate(groups):
                    base = 2048 * par
                    dve.wait_ge(a_mm, s * 4 + (g + 1))
                    if not first:
                        dve.wait_ge(y_mm, s)
                        dve.wait_ge(init, s * 4)
                    m = 640 * d
                    tt(BM[g], F[:, base:base + 768].rearrange("p (a n) -> p a n", a=CT), b3(rwm[:, m:m + 256]), ALU.mult)
                    tt(KM[g], F[:, base + 768:base + 1536].rearrange("p (a n) -> p a n", a=CT),
                       b3(rwm[:, m + 256:m + 512]), ALU.mult)
                    tt(LL[g], F[:, base + 1536:base + 1920].rearrange("p (a n) -> p a n", a=CT),
                       b3(rwm[:, m + 512:m + 640]), ALU.mult).then_inc(a_cp, 1)
                for n, b in enumerate(JOINS):
                    for g, (d, par) in enumerate(groups):
                        dve.wait_ge(p_mm, s * (4 * L) + (4 * n + g + 1))
                        if g >= 2:
                            dve.wait_ge(x_mm, s * (4 * L) + (4 * n + g - 1))
                        src = F[:, 512 * g:512 * g + 192].rearrange("p (a n h) -> p a n h", a=CT, h=b)
                        m = mask("join_mask")[:, 64 * n:64 * (n + 1)].rearrange("p (n h) -> p n h", h=b)
                        m = m.unsqueeze(1).to_broadcast([P, CT, 64 // b, b])
                        tt(halves(P1[n][g % 2], b)[:, :, :, 0, :], src, m, ALU.mult).then_inc(p_cp, 1)
                    for g, (d, par) in enumerate(groups):
                        dve.wait_ge(x_mm, s * (4 * L) + (4 * n + g + 1))
                        for k, (dst, half) in enumerate(((X[g], 0), (Z[g], 1))):
                            if n == L - 1 and k == d:
                                continue
                            if n == L - 1 and k != 1 - d:
                                continue
                            at = 2048 + 512 * g + 192 * k
                            src = F[:, at:at + 192].rearrange("p (a n h) -> p a n h", a=CT, h=b)
                            part = halves(dst, b)[:, :, :, half, :]
                            last = tt(part, part, src, ALU.add)
                        last.then_inc(x_cp, 1)
                dve.wait_ge(u_mm, s + 1)
                if not first:
                    dve.wait_ge(y_mm, s)
                nc.vector.tensor_copy(U, F[:, 3072:4096].rearrange("p (d n) -> p d n", d=2)[:, :, 0:384]
                                      ).then_inc(u_cp, 1)
                dve.wait_ge(s_mm, s + 1)
                tt(new, sm, F[:, 3072:3072 + 384].rearrange("p (a n) -> p a n", a=6), ALU.add).then_inc(s_ad, 1)
                dve.wait_ge(s_ad, s + 1)
                car = M.carry[:, bass.ds(s, 1), :].rearrange("p o n -> p (o n)")
                tt(new, new, car.unsqueeze(2).to_broadcast([P, 6, 64]), ALU.mult).then_inc(s_cp, 1)
                dve.wait_ge(y_mm, s + 1)
                for d, ch in enumerate((s, -s + (TT - 1))):
                    y = Y[:, :, bass.ds(ch * P, P)]
                    last = tt(y, y, F[:, 2048 + 512 * d:2048 + 512 * d + 384].rearrange("p (a n) -> p a n", a=CT),
                              ALU.add)
                last.then_inc(y_cp, 1)
                dve.wait_ge(y_cp, s + 1)

            nc.vector.memset(SM[0], 0.0).then_inc(zero, 1)
            nc.vector.memset(Y, 0.0).then_inc(zero, 1)
            for n in range(L):
                for g in range(2):
                    nc.vector.memset(P1[n][g], 0.0).then_inc(zero, 1)
            dve.wait_ge(zero, 2 + 2 * L)
            dve.wait_ge(m_in, 16)
            run(dve, body)


def rwkv_finish(nc, M, bonus_dram, g_dram):
    sem = M.semaphore
    ins, m_mm, cen, sqd, v_mm, root, step, fin = (
        sem(f"rf_{x}") for x in ("in", "mean", "centred", "squared", "var", "root", "step", "done"))
    c = Cut(M.scr[:, :])
    bonus, gate, sq = (c(CT * T, CT) for _ in range(3))
    Y = M.ht[:, 5:8, :]
    eps = M.small[:, 60:61]

    def head_sum(unit, x):
        for half in range(2):
            last = nc.tensor.matmul(M.ps[:, unit, half * 512:(half + 1) * 512], lhsT=M.c("blocks64"),
                                    rhs=x[:, half * 512:(half + 1) * 512], start=True, stop=True)
        return last

    with nc.Block() as block:
        @block.sync
        def _(sp):
            for a in range(CT):
                sp.dma_start(bonus[:, a, :], bonus_dram[a]).then_inc(ins, 16)
                sp.dma_start(gate[:, a, :], g_dram[a]).then_inc(ins, 16)

        @block.tensor
        def _(pe):
            for a in range(CT):
                head_sum(a, Y[:, a, :]).then_inc(m_mm, 1)
            for a in range(CT):
                pe.wait_ge(sqd, a + 1)
                head_sum((a + 3) % 4, sq[:, a, :]).then_inc(v_mm, 1)

        @block.scalar
        def _(act):
            for a in range(CT):
                act.wait_ge(cen, a + 1)
                nc.scalar.activation(sq[:, a, :], Y[:, a, :], ACT.Square).then_inc(sqd, 1)
            act.wait_ge(step, 1)
            for a in range(CT):
                act.wait_ge(v_mm, a + 1)
                nc.scalar.activation(sq[:, a, :], M.ps[:, (a + 3) % 4, :], ACT.Sqrt, scale=1.0 / 64,
                                     bias=eps).then_inc(root, 1)

        @block.vector
        def _(dve):
            tt, stt = nc.vector.tensor_tensor, nc.vector.scalar_tensor_tensor
            link = Link(dve, step)
            link(nc.vector.memset(eps, 64e-5))
            for a in range(CT):
                dve.wait_ge(m_mm, a + 1)
                stt(Y[:, a, :], M.ps[:, a, :], -1.0 / 64, Y[:, a, :], ALU.mult, ALU.add).then_inc(cen, 1)
            dve.wait_ge(ins, 16 * 2 * CT)
            for a in range(CT):
                y = Y[:, a, :]
                dve.wait_ge(root, a + 1)
                link(nc.vector.reciprocal(sq[:, a, :], sq[:, a, :]))
                link(stt(y, y, M.p("lnx_g")[:, a:a + 1], sq[:, a, :], ALU.mult, ALU.mult))
                link(stt(y, y, M.p("lnx_b")[:, a:a + 1], bonus[:, a, :], ALU.add, ALU.add))
                link(tt(y, y, gate[:, a, :], ALU.mult))


class ExpertMemory:

    def __init__(self, nc, M):
        z = Cut(zt_flat(M))
        self.w = {"gate": [M.ring[:, 0, :], M.ring[:, 1, :]],
                  "up": [z(CHUNK_W), z(CHUNK_W)], "down": [z(CHUNK_W), z(CHUNK_W)]}
        self.loaded = {k: [nc.alloc_semaphore(f"expert_{k}_loaded_{j}") for j in range(2)] for k in self.w}
        self.gates = M.par[:, 0:NE]
        self.idx = M.par[:, NE:2 * NE].bitcast(U32)

    def first(self, w):
        return [(self.w[k][j], w[k][0, j], self.loaded[k][j]) for k in ("gate", "up", "down") for j in range(2)]


def route(nc, M, E):
    sem = M.semaphore
    t_mm, t_cp, l_mm, mx, ce, ex, step, a_mm, pick, i_mm = (
        sem(f"rt_{x}") for x in ("turned", "turned_copied", "logits", "max", "centred", "exp", "step",
                                "affinity_turned", "pick", "picks_turned"))
    c = Cut(M.scr[:, TT * D:])
    aff = c(TT * NE, TT)
    rows = [c(T)[0:NE, :] for _ in range(2)]
    best = c(CAP)[0:NE, :]
    where = c(CAP)[0:NE, :].bitcast(U32)
    where_f = c(CAP)[0:NE, :]
    router = M.p("router").rearrange("p (k n) -> p k n", k=KD)
    LG = M.ps[:, 3, 0:TT * NE].rearrange("p (a n) -> p a n", a=TT)
    AX = mybir.AxisListType.X
    with nc.Block() as block:
        @block.tensor
        def _(pe):
            for t in range(TT):
                if t >= 3:
                    pe.wait_ge(t_cp, t - 2)
                for k in range(KD):
                    last = nc.tensor.transpose(M.ps[:, t % 3, k * P:(k + 1) * P], M.h[:, t, k * P:(k + 1) * P],
                                               M.c("ident"))
                last.then_inc(t_mm, 1)
            for t in range(TT):
                pe.wait_ge(t_cp, t + 1)
                for k in range(KD):
                    last = nc.tensor.matmul(LG[:, t, :], lhsT=M.ht[:, k, t * P:(t + 1) * P], rhs=router[:, k, :],
                                            start=k == 0, stop=k == KD - 1)
            last.then_inc(l_mm, 1)
            pe.wait_ge(ce, 2)
            for t in range(TT):
                last = nc.tensor.transpose(M.ps[0:NE, 0, t * P:(t + 1) * P], aff[:, t, :], M.c("ident"))
            last.then_inc(a_mm, 1)
            pe.wait_ge(i_mm, 1)
            nc.tensor.transpose(M.ps[:, 1, 0:NE], best, M.c("ident")[0:NE, 0:NE])
            nc.tensor.transpose(M.ps[:, 1, NE:2 * NE], where_f, M.c("ident")[0:NE, 0:NE]).then_inc(i_mm, 1)

        @block.scalar
        def _(act):
            for t in range(TT):
                act.wait_ge(t_mm, t + 1)
                nc.scalar.activation(M.ht[:, :, t * P:(t + 1) * P],
                                     M.ps[:, t % 3, :].rearrange("p (k n) -> p k n", k=KD), ACT.Copy).then_inc(t_cp, 1)
            act.wait_ge(ce, 1)
            nc.scalar.activation(aff, aff, ACT.Exp).then_inc(ex, 1)

        @block.vector
        def _(dve):
            link = Link(dve, step)
            stat = M.small[:, 0:TT]
            dve.wait_ge(l_mm, 1)
            link(nc.vector.reduce_max(stat, LG, AX))
            nc.vector.tensor_tensor(aff, LG, stat.unsqueeze(2).to_broadcast([P, TT, NE]), ALU.subtract).then_inc(ce, 1)
            dve.wait_ge(ex, 1)
            link(nc.vector.reduce_sum(stat, aff, AX))
            link(nc.vector.reciprocal(stat, stat))
            nc.vector.tensor_tensor(aff, aff, stat.unsqueeze(2).to_broadcast([P, TT, NE]), ALU.mult).then_inc(ce, 1)
            dve.wait_ge(a_mm, 1)
            link(nc.vector.tensor_copy(rows[0], M.ps[0:NE, 0, :]))
            for r in range(CAP // 8):
                src, dst = rows[r % 2], rows[1 - r % 2]
                eight = best[:, 8 * r:8 * r + 8]
                link(nc.vector.max(eight, src))
                nc.vector.max_index(where[:, 8 * r:8 * r + 8], eight, src)
                link(nc.vector.match_replace(dst, eight, src, -1.0))
            link(nc.vector.tensor_copy(where_f, where))
            dve.sem_inc(i_mm, 1)
            dve.wait_ge(i_mm, 2)
            link(nc.vector.tensor_copy(E.gates, M.ps[:, 1, 0:NE]))
            link(nc.vector.tensor_copy(E.idx, M.ps[:, 1, NE:2 * NE]))


def experts(nc, M, E, w, hf_dram, acc_dram):
    sem = M.semaphore
    xe_in, xt_mm, xt_cp, g_mm, g_cp, u_mm, h_ok, th_mm, th_cp, d_mm, ye_ok, out = (
        sem(f"ex_{x}") for x in ("rows_in", "rows_turned", "turned_copied", "gate_summed", "gate_done", "up_summed",
                                 "hidden", "hidden_turned", "hidden_copied", "down_summed", "rows_out", "added"))
    c = Cut(M.scr[:, :])
    XE, XT, GA, H, HT, YE = c(D), c(D, KD), c(D), c(D), c(D, KD), c(D)

    def half(kind, j):
        return E.w[kind][j].rearrange("p (k n) -> p k n", k=KD)

    with nc.Block() as block:
        @block.sync
        def _(sp):
            def load(kind, j, e):
                src = w[kind][bass.ds(e, 1), j, :, :].rearrange("o p n -> (o p) n")
                sp.dma_start(E.w[kind][j], src).then_inc(E.loaded[kind][j], 16)

            with sp.Fori(0, NE - 1) as e:
                for kind, used in (("gate", g_mm), ("up", u_mm), ("down", d_mm)):
                    for j in range(2):
                        sp.wait_ge(used, e * 2 + (j + 1))
                        load(kind, j, e + 1)

        @block.gpsimd
        def _(pool):
            def gather(e):
                if e:
                    pool.wait_ge(xt_mm, e)
                pool.indirect_dma_start(XE, None, hf_dram, bass.IndirectOffsetOnAxis(E.idx[:, e:e + 1], 0)
                                        ).then_inc(xe_in, 16)
            gather(0)
            gather(1)
            for e in range(NE):
                if e + 2 < NE:
                    gather(e + 2)
                pool.wait_ge(ye_ok, e + 1)
                pool.indirect_dma_start(acc_dram, bass.IndirectOffsetOnAxis(E.idx[:, e:e + 1], 0), YE, None,
                                        compute_op=ALU.add).then_inc(out, 16)
                pool.wait_ge(out, 16 * (e + 1))

        @block.tensor
        def _(pe):
            def turn(dst, src):
                for k in range(KD):
                    last = nc.tensor.transpose(M.ps[:, dst, k * P:(k + 1) * P], src[:, k * P:(k + 1) * P], M.c("ident"))
                return last

            def product(unit, kind, e, lhs, done):
                for j in range(2):
                    pe.wait_ge(E.loaded[kind][j], e * 16 + 16)
                    ww = half(kind, j)
                    for k in range(KD):
                        last = nc.tensor.matmul(M.ps[:, unit, j * 512:(j + 1) * 512], lhsT=lhs[:, k, :],
                                                rhs=ww[:, k, :], start=k == 0, stop=k == KD - 1)
                    last.then_inc(done, 1)

            def gate(e, first=False):
                pe.wait_ge(xe_in, e * 16 + 16)
                if not first:
                    pe.wait_ge(th_cp, e - 1) if not isinstance(e, int) or e > 1 else None
                turn(3, XE).then_inc(xt_mm, 1)
                pe.wait_ge(xt_cp, e + 1)
                if not first:
                    pe.wait_ge(g_cp, e)
                product(0, "gate", e, XT, g_mm)

            def down(e, first=False):
                pe.wait_ge(h_ok, e + 1)
                turn(3, H).then_inc(th_mm, 1)
                pe.wait_ge(th_cp, e + 1)
                if not first:
                    pe.wait_ge(ye_ok, e)
                product(2, "down", e, HT, d_mm)

            def up(e, first=False):
                if not first:
                    pe.wait_ge(h_ok, e)
                product(1, "up", e, XT, u_mm)

            gate(0, True)
            up(0, True)
            gate(1)
            down(0, True)
            up(1)
            with pe.Fori(2, NE) as e:
                gate(e)
                down(e - 1)
                up(e)
            down(NE - 1)

        @block.scalar
        def _(act):
            def turned(e, first=False):
                act.wait_ge(xt_mm, e + 1)
                if not first:
                    act.wait_ge(u_mm, e * 2)
                nc.scalar.activation(XT.rearrange("p k n -> p (k n)"), M.ps[:, 3, :], ACT.Copy).then_inc(xt_cp, 1)

            def silu(e, first=False):
                act.wait_ge(g_mm, e * 2 + 2)
                if not first:
                    act.wait_ge(h_ok, e)
                nc.scalar.activation(GA, M.ps[:, 0, :], ACT.Silu).then_inc(g_cp, 1)

            def hidden(e, first=False):
                act.wait_ge(th_mm, e + 1)
                if not first:
                    act.wait_ge(d_mm, e * 2)
                nc.scalar.activation(HT.rearrange("p k n -> p (k n)"), M.ps[:, 3, :], ACT.Copy).then_inc(th_cp, 1)

            turned(0, True)
            silu(0, True)
            turned(1)
            silu(1)
            hidden(0, True)
            with act.Fori(2, NE) as e:
                turned(e)
                silu(e)
                hidden(e - 1)
            hidden(NE - 1)

        @block.vector
        def _(dve):
            def hid(e, first=False):
                dve.wait_ge(u_mm, e * 2 + 2)
                dve.wait_ge(g_cp, e + 1)
                if not first:
                    dve.wait_ge(th_mm, e)
                nc.vector.tensor_tensor(H, GA, M.ps[:, 1, :], ALU.mult).then_inc(h_ok, 1)

            def rows(e, first=False):
                dve.wait_ge(d_mm, e * 2 + 2)
                if not first:
                    dve.wait_ge(out, e * 16)
                nc.vector.tensor_scalar(YE, M.ps[:, 2, :], E.gates[:, bass.ds(e, 1)], None,
                                        ALU.mult).then_inc(ye_ok, 1)

            hid(0, True)
            rows(0, True)
            hid(1)
            with dve.Fori(2, NE) as e:
                rows(e - 1)
                hid(e)
            rows(NE - 1)


def program(nc, A, out):
    def scratch(name, shape):
        return nc.dram_tensor(name, shape, F32, kind="Internal").ap()

    M, W = Memory(nc), Weights(nc)
    h1, x2, hf, acc = (scratch(n, [T, D]) for n in ("h1_rows", "x2_rows", "ffn_rows", "acc_rows"))
    rw, vt = scratch("rwkv_operands", [2, TT, P, CT * 4 * P]), scratch("rwkv_values", [TT, P, CT * P])
    gate, bonus = scratch("rwkv_gate", [CT, P, T]), scratch("rwkv_bonus", [CT, P, T])

    setup(nc, M, A["par"], A["con"], A["bytes"])
    M.stage_end()
    lower_bounds(nc, M)
    M.stage_end()
    n = 0
    pool_in = [A["pool_in"][g + 4 * j] for g in range(G) for j in range(2)]
    stages = (pool_in, [A["pool_out"][c] for c in range(4)], [A["hgrn_gate"][c] for c in range(4)],
              [A["hgrn_heads"][h] for h in range(HEADS)], [A["hgrn_out"][c] for c in range(4)],
              [A["mem_kv"][0]], [A["mix_in"][c] for c in range(5)], [A["mix_out"][c] for c in range(2)])
    chunks = [c for s in stages for c in s]
    starts = [sum(len(s) for s in stages[:j]) for j in range(len(stages))]

    def ahead(n):
        return [(m, chunks[m]) for m in (n, n + 1) if m < len(chunks) and m not in M.sent]

    norm_transpose(nc, M, W, "norm0", M.p("norm0"), load=A["x"], prefetch=ahead(starts[0]))
    M.stage_end()
    M.sent = {0, 1}
    pool_layer(nc, M, W, starts[0], A["pool_in"], A["pool_grp"], prefetch=ahead(starts[1]))
    M.stage_end()
    M.sent = {starts[1], starts[1] + 1}
    out_projection(nc, M, W, "pool_out", starts[1], M.zt, KI, A["pool_out"], A["x"], prefetch=ahead(starts[2]))
    M.stage_end()
    M.sent = {starts[2], starts[2] + 1}
    norm_transpose(nc, M, W, "norm1", M.p("norm1"), store=h1)
    M.stage_end()
    hgrn_gates(nc, M, W, starts[2], A["hgrn_gate"], prefetch=ahead(starts[3]))
    M.stage_end()
    M.sent = {starts[3], starts[3] + 1}
    hgrn_heads(nc, M, W, starts[3], A["hgrn_heads"], prefetch=ahead(starts[4]))
    M.stage_end()
    M.sent = {starts[4], starts[4] + 1}
    out_projection(nc, M, W, "hgrn_out", starts[4], M.zt, KI, A["hgrn_out"], h1, prefetch=ahead(starts[5]))
    M.stage_end()
    M.sent = {starts[5], starts[5] + 1}
    row_norm(nc, M, "final1", A["final_g"], x2)
    M.stage_end()
    norm_transpose(nc, M, W, "norm_mix", M.p("norm_mix"))
    M.stage_end()
    mix_memory(M)
    memory_keys(nc, M, W, starts[5], A["mem"], A["mem_kv"][0], prefetch=[(starts[6] + 1, chunks[starts[6] + 1])])
    M.stage_end()
    M.sent = {starts[6], starts[6] + 1}
    mixer_projections(nc, M, W, starts[6], A["mix_in"], prefetch=ahead(starts[7]))
    M.stage_end()
    M.sent = {starts[7], starts[7] + 1}
    attention(nc, M)
    M.stage_end()
    conv_norm(nc, M)
    M.stage_end()
    rwkv_common(nc, M, A["rwkv_small"], vt, gate)
    M.stage_end()
    rwkv_directions(nc, M, rw, bonus)
    M.stage_end()
    rwkv_steps(nc, M, rw, vt, A["rwkv_masks"])
    M.stage_end()
    rwkv_finish(nc, M, bonus, gate)
    M.stage_end()
    out_projection(nc, M, W, "mix_out", starts[7], M.ht, KD, A["mix_out"], x2)
    M.stage_end()
    E = ExpertMemory(nc, M)
    w = {k: A["expert_" + k] for k in E.w}
    row_norm(nc, M, "norm_ffn", A["norm_ffn_g"], hf, raw=acc, prefetch=E.first(w))
    M.stage_end()
    route(nc, M, E)
    M.stage_end()
    experts(nc, M, E, w, hf, acc)
    M.stage_end()
    row_norm(nc, M, "final2", A["final_norm_g"], out, load=acc)
    M.stage_end()


def by_feature(v):
    return v.reshape(-1, P).T


def by_chunk(w, cols):
    k = w.shape[0] // P
    return np.ascontiguousarray(w.reshape(k, P, -1, cols).transpose(2, 1, 0, 3)).reshape(-1, P, k * cols)


def layout(x):
    f32 = np.float32
    par = np.zeros((P, PAR_N), f32)
    second = {k[:-2]: v for k, v in x.items() if k.endswith("_2")}
    features = {
        "norm0": x["norm_g"][0], "norm1": x["norm_g"][1], "pool_scale": x["pool_scale"],
        "lb0": x["hgrn_lower_bounds"][0], "lb1": x["hgrn_lower_bounds"][1], "hgrn_g": x["hgrn_norm_g"],
        "norm_mix": second["norm_mix_g"], "norm_mem": second["norm_mem_g"], "conv_b": second["conv_b"],
        "conv_g": second["conv_ln_g"], "conv_beta": second["conv_ln_b"], "mu_prev": second["shift_mu"][0, 0],
        "mu_next": second["shift_mu"][0, 1], "w0": second["decay_w0"], "a0": second["iclr_a0"],
        "k_k": second["k_k"], "k_a": second["k_a"], "r_k": second["r_k"], "lnx_g": second["lnx_g"],
        "lnx_b": second["lnx_b"],
    }
    for name, v in features.items():
        at, n = PAR[name]
        par[:, at:at + n] = by_feature(v)
    at, n = PAR["conv_w"]
    par[:, at:at + n] = second["conv_w"][0].reshape(CONV_K, CT, P).transpose(2, 1, 0).reshape(P, n)
    at, n = PAR["router"]
    par[:, at:at + n] = second["w_router"][0].reshape(KD, P, NE).transpose(1, 0, 2).reshape(P, n)
    w = x["hgrn_w_in"][0]
    heads = w[:, 0:3 * DI].reshape(KD, P, 3, HEADS, P).transpose(3, 1, 0, 2, 4)
    arrays = {
        "x": x["x"][0], "mem": second["mem"][0], "par": par, "con": constants(), "bytes": level_masks(),
        "rwkv_masks": rwkv_masks(),
        "pool_in": by_chunk(x["pool_w_in"][0], 512),
        "pool_grp": np.concatenate([by_chunk(g, 512) for g in x["pool_w_grp"][0]]),
        "pool_out": by_chunk(x["pool_w_out"][0], 256),
        "hgrn_gate": by_chunk(w[:, 3 * DI:], 512),
        "hgrn_heads": np.ascontiguousarray(heads).reshape(HEADS, P, KD * 3 * P),
        "hgrn_out": by_chunk(x["hgrn_w_out"][0], 256),
        "mem_kv": by_chunk(np.concatenate([second["w_mk"][0], second["w_mv"][0]], 1), 512),
        "mix_in": by_chunk(second["w_in"][0], 512),
        "mix_out": by_chunk(second["w_out"][0], 512),
        "rwkv_small": np.concatenate([second["decay_up"][0].reshape(P, CT * P),
                                      second["iclr_up"][0].reshape(P, CT * P), second["gate_up"][0]], 1),
        "final_g": x["final_g"].reshape(1, D), "norm_ffn_g": second["norm_ffn_g"].reshape(1, D),
        "final_norm_g": second["final_norm_g"].reshape(1, D),
    }
    for kind in ("gate", "up", "down"):
        e = second["w_e_" + kind][0].reshape(NE, KD, P, 2, 512).transpose(0, 3, 2, 1, 4)
        arrays["expert_" + kind] = np.ascontiguousarray(e).reshape(NE, 2, P, KD * 512)
    return arrays


def kernel(**inputs):
    import concourse.bacc as bacc
    from concourse.bass_utils import run_bass_kernel_spmd

    nc = bacc.Bacc("TRN2", target_bir_lowering=False, num_devices=1)
    arrays = layout({k: np.asarray(v) for k, v in inputs.items()})
    arrays = {f"in_{k}": np.ascontiguousarray(v) for k, v in arrays.items()}
    aps = {k[3:]: nc.dram_tensor(k, v.shape, mybir.dt.from_np(v.dtype), kind="ExternalInput").ap()
           for k, v in arrays.items()}
    out = nc.dram_tensor("out_rows", [T, D], F32, kind="ExternalOutput").ap()
    program(nc, aps, out)
    r = run_bass_kernel_spmd(nc, [arrays], core_ids=[0])
    return np.asarray(r.results[0]["out_rows"]).reshape(1, T, D)
```

```python
import concourse.bass as bass
from concourse import mybir
import numpy as np

F32 = mybir.dt.float32
U8 = mybir.dt.uint8
U32 = mybir.dt.uint32
ALU = mybir.AluOpType
ACT = mybir.ActivationFunctionType

P = 128
T = 1024
D = 1024
TT = T // P
KD = D // P
DI = 2048
KI = DI // P
G = 4
GT = DI // G // P
WINDOWS = (2, 4, 8, 16)
PADL = 16
HEADS = DI // P
EPS = 1e-6
HALVES = (64, 32, 16, 8, 4)
MEM = 256
AH = 4
CT = 3
CONV_K = 31
CPAD = CONV_K // 2
DECAY_SCALE = 0.606531
RT = 12
NE = 16
CAP = 2 * T // NE
JOINS = (2, 4, 8, 16, 32, 64)
CHUNK_W = 4096

PAR = {}
_at = 0
for _name, _n in (("norm0", KD), ("norm1", KD), ("pool_scale", KI), ("lb0", KI), ("lb1", KI),
                  ("hgrn_g", KI), ("norm_mix", KD), ("norm_mem", KD),
                  ("conv_w", CT * CONV_K), ("conv_b", CT), ("conv_g", CT), ("conv_beta", CT),
                  ("mu_prev", RT), ("mu_next", RT), ("w0", 2 * CT), ("a0", 2 * CT), ("k_k", CT),
                  ("k_a", CT), ("r_k", CT), ("lnx_g", CT), ("lnx_b", CT), ("router", KD * NE)):
    PAR[_name] = (_at, _n)
    _at += _n
PAR_N = _at

CON = {}
_at = 0
for _name, _n in (("ident", P), ("ones", P), ("inv_count", PADL), ("blocks64", P)):
    CON[_name] = (_at, _n)
    _at += _n
CON_N = _at

RWM = {}
_at = 0
for _name, _n in (("rw_mask", 2 * 640), ("join_mask", 6 * P), ("pair_mask", 2 * P)):
    RWM[_name] = (_at, _n)
    _at += _n
RWM_N = _at


def constants():
    c = np.zeros((P, CON_N), np.float32)
    a, n = CON["ident"]
    c[:, a:a + n] = np.eye(P)
    a, n = CON["ones"]
    c[:, a:a + n] = 1.0
    a, n = CON["inv_count"]
    c[:, a:a + n] = 1.0 / (np.arange(n) + 1)
    r, q = np.arange(P)[:, None], np.arange(P)[None, :]
    a, n = CON["blocks64"]
    c[:, a:a + n] = r // 64 == q // 64
    return c


def rwkv_masks():
    c = np.zeros((P, RWM_N), np.float32)
    r, q = np.arange(P)[:, None], np.arange(P)[None, :]
    a, n = RWM["rw_mask"]
    for d, before in enumerate((r < q, r > q)):
        upto = before | (r == q)
        c[:, a + 640 * d:a + 640 * (d + 1)] = np.concatenate(
            [-1.0 * before, 1.0 * upto, 1.0 * before, 1.0 * upto, -1.0 * before.T], 1)
    a, n = RWM["join_mask"]
    for n, b in enumerate(JOINS):
        c[:, a + P * n:a + P * (n + 1)] = (r // (2 * b) == q // (2 * b)) & (r % (2 * b) >= b) & (q % (2 * b) < b)
    a, n = RWM["pair_mask"]
    c[:, a:a + P] = (r // 2 == q // 2) & (r > q)
    c[:, a + P:a + 2 * P] = (r // 2 == q // 2) & (r < q)
    return c


def level_masks():
    s = np.arange(P)[:, None]
    parts = []
    for h in HALVES:
        t = np.array([t for t in range(P) if t % (2 * h) >= h])[None, :]
        parts.append((s // (2 * h) == t // (2 * h)) & (s % (2 * h) < h))
    t = np.arange(P)[None, :]
    parts.append((s // 4 == t // 4) & (s <= t))
    t = np.arange(T)[None, :] % P
    keep = [np.repeat(t != 0, P, 0), np.repeat(t != P - 1, P, 0)]
    return np.concatenate([np.tile(m, (1, 4)) for m in parts] + keep, 1).astype(np.float32)


class Memory:

    def __init__(self, nc):
        self.nc = nc
        self.stage = []
        sb = nc.alloc_sbuf_tensor
        self.sent = set()
        self.par = sb("sb_par", [P, PAR_N], F32)
        self.con = sb("sb_con", [P, CON_N], F32)
        self.hmask = sb("sb_hmask", [P, 4 * (5 * 64 + P) + 2 * T], U8)
        self.ring = sb("sb_ring", [P, 2, CHUNK_W], F32)
        self.ht = sb("sb_ht", [P, KD, T], F32)
        self.zt = sb("sb_zt", [P, KI, T], F32)
        self.scr_n = 18432
        self.scr = sb("sb_scr", [P, self.scr_n], F32)
        self.carry = sb("sb_carry", [P, TT, 6], F32)
        self.bounds = sb("sb_bounds", [P, 2 * KI], F32)
        self.small = sb("sb_small", [P, 64], F32)
        self.ps = nc.alloc_psum_tensor("ps", [P, 4, 1024], F32)
        self.h = self.scr[:, 0:TT * D].rearrange("p (a n) -> p a n", a=TT)

        self.normed = self.scr[:, TT * D:2 * TT * D].rearrange("p (a n) -> p a n", a=TT)
        self.junk = self.scr[:, 2 * TT * D:2 * TT * D + D]
        self.gain_row = self.scr[:, 2 * TT * D + D:2 * TT * D + 2 * D]

    def semaphore(self, name):
        s = self.nc.alloc_semaphore(name)
        self.stage.append(s)
        return s

    def stage_end(self):
        self.nc.clear_and_free_semaphores(self.stage)
        self.nc.all_engine_barrier()
        self.stage = []

    def p(self, name):
        a, n = PAR[name]
        return self.par[:, a:a + n]

    def c(self, name):
        a, n = CON[name]
        return self.con[:, a:a + n]


class Weights:

    def __init__(self, nc):
        self.loaded = [nc.alloc_semaphore(f"weights_loaded_{s}") for s in range(2)]
        self.used = nc.alloc_semaphore("weights_used")
        self.sources = []

    def wait(self, eng, n):
        eng.wait_ge(self.loaded[n % 2], 16 * (n // 2 + 1))


def dma_chunk(eng, M, W, n, slot, src):
    if isinstance(n, int):
        if n >= 2:
            eng.wait_ge(W.used, n - 1)
    else:
        eng.wait_ge(W.used, n - 1)
    width = src.shape[-1]
    eng.dma_start(M.ring[:, slot, 0:width], src).then_inc(W.loaded[slot], 16)


def slot_view(M, slot, kt, cols):
    return M.ring[:, slot, 0:kt * cols].rearrange("p (k n) -> p k n", k=kt)


class RowNorm:

    def __init__(self, M, tag, squared=False, place=16):
        self.M, self.squared, self.place = M, squared, place
        self.sq, self.root, self.inv = (M.semaphore(f"{tag}_{x}") for x in ("squares", "root", "rstd"))

    def rstd(self, t):
        return self.M.small[:, self.place + t:self.place + t + 1]

    def scalar(self, nc, act, t, ready):
        M = self.M
        if not self.squared:
            ready(act, t)
            if t:
                act.wait_ge(self.sq, t)
            nc.scalar.activation(M.junk, M.h[:, t, :], ACT.Square, accum_out=M.small[:, t:t + 1]
                                 ).then_inc(self.sq, 1)
            act.wait_ge(self.sq, t + 1)
        nc.scalar.activation(self.rstd(t), M.small[:, t:t + 1], ACT.Sqrt,
                             scale=1.0 / D, bias=M.eps).then_inc(self.root, 1)

    def vector(self, nc, dve, t):
        dve.wait_ge(self.root, t + 1)
        nc.vector.reciprocal(self.rstd(t), self.rstd(t)).then_inc(self.inv, 1)


def norm_transpose(nc, M, W, tag, gain, load=None, store=None, squared=False, final=None, prefetch=()):
    sem = M.semaphore
    rows_in = [sem(f"{tag}_rows_in_{t}") for t in range(TT)] if load is not None else None
    rows_out, gain_in, first = sem(f"{tag}_rows_out"), sem(f"{tag}_gain_in"), sem(f"{tag}_first_norm")
    scaled, turned, copied = sem(f"{tag}_scaled"), sem(f"{tag}_turned"), sem(f"{tag}_copied")
    before = RowNorm(M, f"{tag}_before", squared, place=24) if final else None
    norm = RowNorm(M, tag, squared and not final)
    ident = M.c("ident")
    with nc.Block() as block:
        @block.sync
        def _(sp):
            if final:
                sp.dma_start(M.gain_row, final[0].to_broadcast([P, D])).then_inc(gain_in, 16)
            for t in range(TT):
                if load is not None:
                    sp.dma_start(M.h[:, t, :], load[t * P:(t + 1) * P, :]).then_inc(rows_in[t], 16)
                if final:
                    sp.wait_ge(first, t + 1)
                    sp.dma_start(final[1][t * P:(t + 1) * P, :], M.h[:, t, :]).then_inc(rows_out, 16)
                if store is not None:
                    sp.dma_start(store[t * P:(t + 1) * P, :], M.h[:, t, :]).then_inc(rows_out, 16)
            for n, src in prefetch:
                dma_chunk(sp, M, W, n, n % 2, src)
            if store is not None or final:
                sp.wait_ge(rows_out, 16 * TT)

        @block.scalar
        def _(act):
            def ready(act, t):
                if load is not None:
                    act.wait_ge(rows_in[t], 16)
                if final:
                    act.wait_ge(first, t + 1)

            def scale(t):
                act.wait_ge(norm.inv, t + 1)
                nc.scalar.activation(M.normed[:, t, :], M.h[:, t, :], ACT.Copy, scale=norm.rstd(t)
                                     ).then_inc(scaled, 1)

            if final:
                for t in range(TT):
                    before.scalar(nc, act, t, None)
            norm.scalar(nc, act, 0, ready)
            for t in range(TT):
                if t + 1 < TT:
                    norm.scalar(nc, act, t + 1, ready)
                scale(t)

        @block.vector
        def _(dve):
            def first_norm(t):
                dve.wait_ge(before.inv, t + 1)
                nc.vector.scalar_tensor_tensor(M.h[:, t, :], M.h[:, t, :], before.rstd(t), M.gain_row,
                                               ALU.mult, ALU.mult).then_inc(first, 1)

            def copy(t):
                dve.wait_ge(turned, t + 1)
                nc.vector.tensor_tensor(
                    M.ht[:, :, t * P:(t + 1) * P],
                    M.ps[:, t % 4, :].rearrange("p (k n) -> p k n", k=KD),
                    gain.unsqueeze(2).to_broadcast([P, KD, P]), ALU.mult).then_inc(copied, 1)

            if final:
                for t in range(TT):
                    before.vector(nc, dve, t)
                dve.wait_ge(gain_in, 16)
                first_norm(0)
                first_norm(1)
            for t in range(TT):
                if final and t + 2 < TT:
                    first_norm(t + 2)
                norm.vector(nc, dve, t)
                if t >= 2:
                    copy(t - 2)
            copy(TT - 2)
            copy(TT - 1)

        @block.tensor
        def _(pe):
            for t in range(TT):
                pe.wait_ge(scaled, t + 1)
                if t >= 4:
                    pe.wait_ge(copied, t - 3)
                for k in range(KD):
                    last = nc.tensor.transpose(M.ps[:, t % 4, k * P:(k + 1) * P],
                                               M.normed[:, t, k * P:(k + 1) * P], ident)
                last.then_inc(turned, 1)


def pool_layer(nc, M, W, n0, w_in, w_grp, prefetch=()):
    sem = M.semaphore
    grp_in = sem("pool_group_weights")
    zeroed = sem("pool_pads_zeroed")
    v_mm, v_cp = sem("pool_values_summed"), sem("pool_values_copied")
    g_mm, g_cp = sem("pool_gates_summed"), sem("pool_gates_copied")
    m_mm, m_cp = sem("pool_mixed_summed"), sem("pool_mixed_copied")
    win = sem("pool_window_step")
    pooled = sem("pool_pooled")
    LW = PADL + T
    cut = [0]

    def scratch(n):
        cut[0] += n
        return M.scr[:, cut[0] - n:cut[0]]

    V = scratch(GT * LW).rearrange("p (a n) -> p a n", a=GT)
    S = [scratch(2 * LW).rearrange("p (a n) -> p a n", a=2) for _ in range(2)]
    PL = scratch(GT * T).rearrange("p (a n) -> p a n", a=GT)
    WG = scratch(4 * 512).rearrange("p (k n) -> p k n", k=4)
    inv_count = M.c("inv_count")
    scale = M.p("pool_scale")
    steps = [0]

    with nc.Block() as block:
        @block.sync
        def _(sp):
            for g in range(G):
                for j in range(2):
                    n = n0 + 2 * g + j
                    dma_chunk(sp, M, W, n, n % 2, w_in[g + 4 * j]) if n not in M.sent else None
                if g:
                    sp.wait_ge(m_mm, GT * g)
                sp.dma_start(WG, w_grp[g].rearrange("p (k n) -> p k n", k=4)).then_inc(grp_in, 16)
            for n, src in prefetch:
                dma_chunk(sp, M, W, n, n % 2, src)

        @block.tensor
        def _(pe):
            unit = 0

            def free(u):
                if u < 4:
                    return
                u -= 4
                g, r = divmod(u, 3 * GT)
                pe.wait_ge((v_cp, g_cp, m_cp)[r // GT], g * GT + r % GT + 1)

            for g in range(G):
                for j, done in ((0, v_mm), (1, g_mm)):
                    n = n0 + 2 * g + j
                    W.wait(pe, n)
                    w = slot_view(M, n % 2, KD, 512)
                    for m in range(GT):
                        free(unit)
                        for half in range(2):
                            for k in range(KD):
                                last = nc.tensor.matmul(
                                    M.ps[:, unit % 4, half * 512:(half + 1) * 512],
                                    lhsT=w[:, k, m * P:(m + 1) * P],
                                    rhs=M.ht[:, k, half * 512:(half + 1) * 512],
                                    start=k == 0, stop=k == KD - 1)
                        last.then_inc(done, 1)
                        unit += 1
                    pe.wait_ge(done, GT * (g + 1))
                    pe.sem_inc(W.used, 1)
                pe.wait_ge(grp_in, 16 * (g + 1))
                pe.wait_ge(pooled, 2 * (g + 1))
                for m in range(GT):
                    free(unit)
                    for half in range(2):
                        for k in range(GT):
                            last = nc.tensor.matmul(
                                M.ps[:, unit % 4, half * 512:(half + 1) * 512],
                                lhsT=WG[:, k, m * P:(m + 1) * P],
                                rhs=PL[:, k, half * 512:(half + 1) * 512],
                                start=k == 0, stop=k == GT - 1)
                    last.then_inc(m_mm, 1)
                    unit += 1

        @block.scalar
        def _(act):
            u = 0
            act.wait_ge(zeroed, 3)
            for g in range(G):
                for m in range(GT):
                    act.wait_ge(v_mm, g * GT + m + 1)
                    if g:
                        act.wait_ge(pooled, 2 * g)
                    nc.scalar.activation(V[:, m, PADL:LW], M.ps[:, u % 4, :], ACT.Copy).then_inc(v_cp, 1)
                    u += 1
                for m in range(GT):
                    act.wait_ge(g_mm, g * GT + m + 1)
                    nc.scalar.activation(M.zt[:, g * GT + m, :], M.ps[:, u % 4, :], ACT.Silu).then_inc(g_cp, 1)
                    u += 1
                u += GT

        @block.vector
        def _(dve):
            nc.vector.memset(V, 0.0).then_inc(zeroed, 1)
            nc.vector.memset(S[0], 0.0).then_inc(zeroed, 1)
            nc.vector.memset(S[1], 0.0).then_inc(zeroed, 1)
            dve.wait_ge(zeroed, 3)

            def step(ins):
                steps[0] += 1
                ins.then_inc(win, 1)
                dve.wait_ge(win, steps[0])

            u = 0
            for g, w in enumerate(WINDOWS):
                for pair in range(2):
                    dve.wait_ge(v_cp, g * GT + 2 * pair + 2)
                    if g:
                        dve.wait_ge(m_mm, GT * g)
                    v = V[:, 2 * pair:2 * pair + 2, :]
                    src, span = v, 1
                    while span < w:
                        dst = S[(span.bit_length() - 1) % 2]
                        step(nc.vector.tensor_tensor(dst[:, :, PADL:LW], src[:, :, PADL:LW],
                                                     src[:, :, PADL - span:LW - span], ALU.add))
                        src, span = dst, 2 * span
                    out = PL[:, 2 * pair:2 * pair + 2, :]
                    step(nc.vector.scalar_tensor_tensor(out, src[:, :, PADL:LW], 1.0 / w, v[:, :, PADL:LW],
                                                        ALU.mult, ALU.subtract))
                    head = src[:, :, PADL:PADL + w]
                    step(nc.vector.tensor_tensor(head, head,
                                                 inv_count[:, 0:w].unsqueeze(1).to_broadcast([P, 2, w]), ALU.mult))
                    nc.vector.tensor_tensor(out[:, :, 0:w], head, v[:, :, PADL:PADL + w],
                                            ALU.subtract).then_inc(pooled, 1)
                    dve.wait_ge(pooled, 2 * g + pair + 1)
                for m in range(GT):
                    dve.wait_ge(m_mm, g * GT + m + 1)
                    dve.wait_ge(g_cp, g * GT + m + 1)
                    z = M.zt[:, g * GT + m, :]
                    nc.vector.scalar_tensor_tensor(
                        z, M.ps[:, (3 * GT * g + 2 * GT + m) % 4, :], scale[:, g * GT + m:g * GT + m + 1], z,
                        ALU.mult, ALU.mult).then_inc(m_cp, 1)


def out_projection(nc, M, W, tag, n0, zt, kt, w_out, residual, prefetch=()):
    sem = M.semaphore
    rows_in = sem(f"{tag}_residual_in")
    summed, added, sq = sem(f"{tag}_summed"), sem(f"{tag}_added"), sem(f"{tag}_squares")
    cols = CHUNK_W // kt
    chunks = D // cols
    with nc.Block() as block:
        @block.sync
        def _(sp):
            for t in range(TT):
                sp.dma_start(M.h[:, t, :], residual[t * P:(t + 1) * P, :]).then_inc(rows_in, 16)
            for c in range(chunks):
                if n0 + c not in M.sent:
                    dma_chunk(sp, M, W, n0 + c, (n0 + c) % 2, w_out[c])
            for n, src in prefetch:
                dma_chunk(sp, M, W, n, n % 2, src)

        @block.tensor
        def _(pe):
            for c in range(chunks):
                n = n0 + c
                W.wait(pe, n)
                w = slot_view(M, n % 2, kt, cols)
                for t in range(TT):
                    u = c * TT + t
                    if u >= 8:
                        pe.wait_ge(added, u - 7)
                    for k in range(kt):
                        last = nc.tensor.matmul(bank(M, u % 8)[:, 0:cols], lhsT=zt[:, k, t * P:(t + 1) * P],
                                                rhs=w[:, k, :], start=k == 0, stop=k == kt - 1)
                    last.then_inc(summed, 1)
                pe.wait_ge(summed, (c + 1) * TT)
                pe.sem_inc(W.used, 1)

        @block.vector
        def _(dve):
            dve.wait_ge(rows_in, 16 * TT)
            for c in range(chunks):
                for t in range(TT):
                    u = c * TT + t
                    dve.wait_ge(summed, u + 1)
                    h = M.h[:, t, c * cols:(c + 1) * cols]
                    nc.vector.tensor_tensor(h, bank(M, u % 8)[:, 0:cols], h, ALU.add).then_inc(added, 1)

        @block.scalar
        def _(act):
            for t in range(TT):
                act.wait_ge(added, (chunks - 1) * TT + t + 1)
                if t:
                    act.wait_ge(sq, t)
                nc.scalar.activation(M.junk, M.h[:, t, :], ACT.Square, accum_out=M.small[:, t:t + 1]
                                     ).then_inc(sq, 1)


def bank(M, b):
    return M.ps[:, b // 2, (b % 2) * 512:(b % 2) * 512 + 512]


def row_norm(nc, M, tag, gain_row, store, out, load=None, raw=None, raw_out=None, turn=False, prefetch=()):
    sem = M.semaphore
    turned, copied = sem(f"{tag}_turned"), sem(f"{tag}_copied")
    gain_in, done = sem(f"{tag}_gain_in"), sem(f"{tag}_done")
    rows_in = [sem(f"{tag}_rows_in_{t}") for t in range(TT)] if load is not None else None
    norm = RowNorm(M, tag, load is None)
    with nc.Block() as block:
        @block.sync
        def _(sp):
            sp.dma_start(M.gain_row, gain_row.to_broadcast([P, D])).then_inc(gain_in, 16)
            if load is not None:
                for t in range(TT):
                    sp.dma_start(M.h[:, t, :], load[t * P:(t + 1) * P, :]).then_inc(rows_in[t], 16)
            if raw is not None:
                for t in range(TT):
                    sp.dma_start(raw[t * P:(t + 1) * P, :], M.h[:, t, :]).then_inc(raw_out, 16)
            for t in range(TT):
                sp.wait_ge(done, t + 1)
                sp.dma_start(store[t * P:(t + 1) * P, :], M.normed[:, t, :]).then_inc(out, 16)
            for place, src, arrived in prefetch:
                sp.dma_start(place, src).then_inc(arrived, 16)

        @block.scalar
        def _(act):
            for t in range(TT):
                norm.scalar(nc, act, t, lambda eng, t: eng.wait_ge(rows_in[t], 16))
            if turn:
                for t in range(TT):
                    act.wait_ge(turned, t + 1)
                    nc.scalar.activation(M.ht[:, :, t * P:(t + 1) * P],
                                         M.ps[:, t % 4, :].rearrange("p (k n) -> p k n", k=KD),
                                         ACT.Copy).then_inc(copied, 1)

        @block.tensor
        def _(pe):
            if turn:
                for t in range(TT):
                    pe.wait_ge(done, t + 1)
                    if t >= 4:
                        pe.wait_ge(copied, t - 3)
                    for k in range(KD):
                        last = nc.tensor.transpose(M.ps[:, t % 4, k * P:(k + 1) * P],
                                                   M.normed[:, t, k * P:(k + 1) * P], M.c("ident"))
                    last.then_inc(turned, 1)

        @block.vector
        def _(dve):
            for t in range(TT):
                norm.vector(nc, dve, t)
                if t == 0:
                    dve.wait_ge(gain_in, 16)
                dve.wait_ge(norm.inv, t + 1)
                nc.vector.scalar_tensor_tensor(M.normed[:, t, :], M.h[:, t, :], norm.rstd(t), M.gain_row,
                                               ALU.mult, ALU.mult).then_inc(done, 1)


def setup(nc, M, par, con, hmask):
    s, z, m = M.semaphore("setup_in"), M.semaphore("setup_eps"), M.semaphore("setup_masks")
    M.eps = M.small[:, 63:64]
    floats = M.scr[:, 0:hmask.shape[1]]
    with nc.Block() as block:
        @block.sync
        def _(sp):
            sp.dma_start(M.par[:, :], par).then_inc(s, 16)
            sp.dma_start(M.con[:, :], con).then_inc(s, 16)
            sp.dma_start(floats, hmask).then_inc(s, 16)
            sp.wait_ge(s, 48)

        @block.vector
        def _(dve):
            nc.vector.memset(M.eps, EPS).then_inc(z, 1)
            dve.wait_ge(s, 48)
            nc.vector.tensor_copy(M.hmask[:, :], floats).then_inc(m, 1)
            dve.wait_ge(z, 1)
            dve.wait_ge(m, 1)


def lower_bounds(nc, M):
    sem = M.semaphore
    step, ex = sem("bounds_step"), sem("bounds_exp")
    w = M.scr
    top, e0, e1, tot = (w[:, 16 * j:16 * j + 16] for j in range(4))
    M.lb, M.oml = M.bounds[:, 0:KI], M.bounds[:, KI:2 * KI]
    l0, l1 = M.p("lb0"), M.p("lb1")
    with nc.Block() as block:
        @block.scalar
        def _(act):
            act.wait_ge(step, 3)
            nc.scalar.activation(w[:, 16:48], w[:, 16:48], ACT.Exp).then_inc(ex, 1)

        @block.vector
        def _(dve):
            n = [0]

            def link(ins):
                n[0] += 1
                ins.then_inc(step, 1)
                dve.wait_ge(step, n[0])
            tt = nc.vector.tensor_tensor
            link(tt(top, l0, l1, ALU.max))
            link(tt(e0, l0, top, ALU.subtract))
            link(tt(e1, l1, top, ALU.subtract))
            dve.wait_ge(ex, 1)
            link(tt(tot, e0, e1, ALU.add))
            link(nc.vector.reciprocal(tot, tot))
            link(tt(e0, e0, tot, ALU.mult))
            link(tt(e1, e1, tot, ALU.mult))
            link(tt(e1, e0, e1, ALU.add))
            link(tt(M.lb, e1, e0, ALU.subtract))
            link(nc.vector.tensor_scalar(M.oml, M.lb, -1.0, 1.0, ALU.mult, ALU.add))


def hgrn_gates(nc, M, W, n0, w_gate, prefetch=()):
    summed, copied = M.semaphore("hgrn_gates_summed"), M.semaphore("hgrn_gates_copied")
    with nc.Block() as block:
        @block.sync
        def _(sp):
            for c in range(4):
                if n0 + c not in M.sent:
                    dma_chunk(sp, M, W, n0 + c, (n0 + c) % 2, w_gate[c])
            for n, src in prefetch:
                dma_chunk(sp, M, W, n, n % 2, src)

        @block.tensor
        def _(pe):
            for c in range(4):
                n = n0 + c
                W.wait(pe, n)
                w = slot_view(M, n % 2, KD, 512)
                for m in range(4):
                    u = 4 * c + m
                    if u >= 4:
                        pe.wait_ge(copied, u - 3)
                    feature_tile(nc, M, u % 4, w, slice(m * P, (m + 1) * P)).then_inc(summed, 1)
                pe.wait_ge(summed, 4 * c + 4)
                pe.sem_inc(W.used, 1)

        @block.scalar
        def _(act):
            for u in range(KI):
                act.wait_ge(summed, u + 1)
                nc.scalar.activation(M.zt[:, u, :], M.ps[:, u % 4, :], ACT.Silu).then_inc(copied, 1)


def feature_tile(nc, M, unit, w, cols):
    for half in range(2):
        for k in range(KD):
            last = nc.tensor.matmul(M.ps[:, unit, half * 512:(half + 1) * 512], lhsT=w[:, k, cols],
                                    rhs=M.ht[:, k, half * 512:(half + 1) * 512],
                                    start=k == 0, stop=k == KD - 1)
    return last


def hgrn_heads(nc, M, W, n0, w_heads, prefetch=()):
    assert n0 % 2 == 0
    sem = M.semaphore
    cut = [0]

    def scratch(n):
        cut[0] += n
        return M.scr[:, cut[0] - n:cut[0]]

    def tiles(ap):
        return ap.rearrange("p (a n) -> p a n", a=TT)

    KEY = scratch(T)
    LOG = scratch(T)
    QRY = scratch(T)
    CUM = scratch(T)
    VAL = [tiles(scratch(T)) for _ in range(2)]
    LEV = [scratch(T) for _ in HALVES]
    DQ, DK = scratch(T), scratch(T)
    QE, KE = scratch(T), scratch(T)
    KET = scratch(T)
    SC = scratch(T)
    ST = tiles(scratch(T))
    END = M.small[:, 24:24 + TT]
    ones = M.c("ones")
    keep = M.hmask[:, 1792:1792 + T]
    ident = M.c("ident")
    gain = M.p("hgrn_g")

    cleared, begun, picked = sem("hgrn_cleared"), sem("scores_copy_begun"), sem("scores_picked")
    f_mm, q_mm, v_mm = sem("forget_summed"), sem("query_summed"), sem("value_summed")
    f_cp, q_cp, v_cp = sem("forget_copied"), sem("query_copied"), sem("value_copied")
    exped, plus1, recip = sem("forget_exp"), sem("forget_plus_one"), sem("forget_sigmoid")
    key, gate, log, cum = sem("key_ready"), sem("forget_gate"), sem("forget_log"), sem("decay_summed")
    offs, decayed = sem("level_offsets"), sem("level_decays")
    lev, ke = sem("levels_ready"), sem("edge_keys_ready")
    t_mm, t_cp = sem("edge_keys_turned"), sem("edge_keys_copied")
    s_mm, s_cp = sem("scores_summed"), sem("scores_copied")
    kv_mm, st = sem("tile_states_summed"), sem("states_ready")
    o_mm, o_cp, sq = sem("output_summed"), sem("output_copied"), sem("output_squared")
    n_mm, n_cp, rs = sem("square_sum"), sem("norm_log"), sem("norm_ready")
    z1, z = sem("output_scaled"), sem("head_done")
    U0, U1, U2, U3 = (M.ps[:, u, :] for u in range(4))

    def blocks(ap, h):
        return ap.rearrange("p (n two h) -> p n two h", two=2, h=h)

    def head(i, c):
        return i * 2 + c

    def loop(eng, body, first=None, last=None):
        body(0, 0, True)
        body(0, 1, False)
        with eng.Fori(1, HEADS // 2 - 1) as i:
            body(i, 0, False)
            body(i, 1, False)
        body(HEADS // 2 - 1, 0, False)
        body(HEADS // 2 - 1, 1, False, True)

    with nc.Block() as block:
        @block.sync
        def _(sp):
            for c in range(2):
                if n0 + c not in M.sent:
                    dma_chunk(sp, M, W, n0 + c, c, w_heads[c])
            with sp.Fori(1, HEADS // 2) as i:
                for c in range(2):
                    sp.wait_ge(W.used, i * 2 + (n0 + c - 1))
                    sp.dma_start(M.ring[:, c, 0:3 * KD * P], w_heads[i * 2 + c]).then_inc(W.loaded[c], 16)
            for n, src in prefetch:
                dma_chunk(sp, M, W, n, n % 2, src)

        @block.tensor
        def _(pe):
            def weights(i, c):
                pe.wait_ge(W.loaded[c % 2], i * 16 + 16 * ((n0 + c) // 2 + 1))
                return M.ring[:, c % 2, 0:3 * KD * P].rearrange("p (k n) -> p k n", k=KD)

            def project_forget(i, c, w):
                feature_tile(nc, M, 0, w, slice(P, 2 * P)).then_inc(f_mm, 1)

            def project_rest(i, c, w):
                feature_tile(nc, M, 2, w, slice(0, P)).then_inc(q_mm, 1)
                for t in range(TT):
                    for k in range(KD):
                        last = nc.tensor.matmul(M.ps[:, 3, t * P:(t + 1) * P], lhsT=M.ht[:, k, t * P:(t + 1) * P],
                                                rhs=w[:, k, 2 * P:3 * P], start=k == 0, stop=k == KD - 1)
                last.then_inc(v_mm, 1)
                pe.wait_ge(v_mm, head(i, c) + 1)
                pe.sem_inc(W.used, 1)

            def square_sum(i, c):
                pe.wait_ge(sq, head(i, c) + 1)
                for half in range(2):
                    last = nc.tensor.matmul(M.ps[:, 1, half * 512:(half + 1) * 512], lhsT=ones,
                                            rhs=KET[:, half * 512:(half + 1) * 512], start=True, stop=True)
                last.then_inc(n_mm, 1)

            def scores(i, c, g, free):
                pairs = [(DK, DQ)] + [(x, x) for x in LEV]
                for n, (key, query) in enumerate(pairs):
                    unit = (3 * g + n // 2 + 1) % 4
                    if n % 2 == 0:
                        free(n // 2)
                    for j in range(4):
                        t = 4 * g + j
                        at = 512 * (n % 2) + j * P
                        last = nc.tensor.matmul(M.ps[:, unit, at:at + P], lhsT=key[:, t * P:(t + 1) * P],
                                                rhs=query[:, t * P:(t + 1) * P], start=True, stop=True)
                    if n % 2:
                        last.then_inc(s_mm, 1)

            def body(i, c, first, last_head=False):
                h = head(i, c)
                if not last_head:
                    ni, ncc = (i, c + 1) if c == 0 else (i + 1, 0)
                    w = weights(ni, ncc)
                    pe.wait_ge(*((f_cp, 1) if first else (s_cp, h * 6)))
                    project_forget(ni, ncc, w)
                if not first:
                    pi, pc = (i, 0) if c == 1 else (i - 1, 1)
                    square_sum(pi, pc)
                    pe.wait_ge(st, h * 7)
                else:
                    pe.wait_ge(q_cp, 1)
                    pe.wait_ge(v_cp, 1)
                if not last_head:
                    project_rest(ni, ncc, w)
                    pe.wait_ge(f_cp, h + 2)
                elif not first:
                    pe.wait_ge(s_cp, h * 6)
                pe.wait_ge(ke, h + 1)
                for t in range(TT):
                    last = nc.tensor.transpose(M.ps[:, 0, t * P:(t + 1) * P], KE[:, t * P:(t + 1) * P], ident)
                last.then_inc(t_mm, 1)
                ahead = 1 if last_head else 2

                def free_first(n):
                    if n == 0 and not first:
                        pe.wait_ge(n_cp, h)
                    elif n == 1:
                        pe.wait_ge(q_cp, h + ahead)
                    elif n == 2:
                        pe.wait_ge(v_cp, h + ahead)

                def free_second(n):
                    if n == 0:
                        pe.wait_ge(t_cp, h + 1)
                    else:
                        pe.wait_ge(s_cp, h * 6 + n)

                scores(i, c, 0, free_first)
                scores(i, c, 1, free_second)
                pe.wait_ge(s_cp, h * 6 + 3)
                for t in range(TT - 1):
                    last = nc.tensor.matmul(M.ps[:, 3, t * P:(t + 1) * P], lhsT=KET[:, t * P:(t + 1) * P],
                                            rhs=VAL[c][:, t, :], start=True, stop=True)
                last.then_inc(kv_mm, 1)
                pe.wait_ge(s_cp, h * 6 + 6)
                for t in range(TT):
                    if t:
                        pe.wait_ge(st, h * 7 + t)
                    nc.tensor.matmul(M.ps[:, 1, t * P:(t + 1) * P], lhsT=VAL[c][:, t, :],
                                     rhs=SC[:, t * P:(t + 1) * P], start=True, stop=t == 0)
                    if t:
                        last = nc.tensor.matmul(M.ps[:, 1, t * P:(t + 1) * P], lhsT=ST[:, t, :],
                                                rhs=QE[:, t * P:(t + 1) * P], start=False, stop=True)
                last.then_inc(o_mm, 1)

            w = weights(0, 0)
            project_forget(0, 0, w)
            project_rest(0, 0, w)
            loop(pe, body)
            pe.wait_ge(st, HEADS * 7)
            square_sum(HEADS // 2 - 1, 1)

        @block.scalar
        def _(act):
            act_ = nc.scalar.activation

            def forget_exp(h1):
                act.wait_ge(f_cp, h1)
                act_(KEY, KEY, ACT.Exp).then_inc(exped, 1)

            def forget_log(h1):
                act.wait_ge(gate, h1)
                act_(LOG, LOG, ACT.Ln).then_inc(log, 1)

            def copies(h1, slot, first=False):
                act.wait_ge(q_mm, h1)
                if not first:
                    act.wait_ge(lev, h1 - 1)
                act_(QRY, U2, ACT.Copy).then_inc(q_cp, 1)
                act.wait_ge(v_mm, h1)
                act_(VAL[slot], U3.rearrange("p (a n) -> p a n", a=TT), ACT.Copy).then_inc(v_cp, 1)

            def decays(h1):
                for n in range(len(HALVES)):
                    act.wait_ge(offs, (h1 - 1) * 7 + n + 1)
                    act_(LEV[n], LEV[n], ACT.Exp).then_inc(decayed, 1)
                act.wait_ge(offs, (h1 - 1) * 7 + 6)
                act_(DK, DQ, ACT.Exp, scale=-1.0).then_inc(decayed, 1)
                act.wait_ge(decayed, (h1 - 1) * 10 + 6)
                act_(DQ, DQ, ACT.Exp).then_inc(decayed, 1)
                act_(QE, CUM, ACT.Exp).then_inc(decayed, 1)
                act_(END, tiles(CUM)[:, :, P - 1], ACT.Exp).then_inc(decayed, 1)
                act.wait_ge(offs, (h1 - 1) * 7 + 7)
                act_(KE, KE, ACT.Exp).then_inc(decayed, 1)

            def inverse_norm(h1):
                act.wait_ge(n_mm, h1)
                act_(KET, U1, ACT.Ln, scale=1.0 / P, bias=M.eps).then_inc(n_cp, 1)
                act.wait_ge(n_cp, h1)
                act_(KET, KET, ACT.Exp, scale=-0.5).then_inc(rs, 1)

            def body(i, c, first, last_head=False):
                h = head(i, c)
                if not last_head:
                    forget_exp(h + 2)
                if not first:
                    inverse_norm(h)
                if not last_head:
                    forget_log(h + 2)
                    if not first:
                        act.wait_ge(o_mm, h)
                    copies(h + 2, 1 - c)
                act.wait_ge(t_mm, h + 1)
                if not first:
                    act.wait_ge(z1, h)
                act_(KET, U0, ACT.Copy).then_inc(t_cp, 1)
                act.wait_ge(o_cp, h + 1)
                act_(KET, LOG, ACT.Square).then_inc(sq, 1)
                if not last_head:
                    decays(h + 2)

            forget_exp(1)
            forget_log(1)
            copies(1, 0, True)
            decays(1)
            loop(act, body)
            inverse_norm(HEADS)

        @block.vector
        def _(dve):
            tt = nc.vector.tensor_tensor

            def forget(h1, col, before=None, first=False):
                dve.wait_ge(f_mm, h1)
                if not first:
                    dve.wait_ge(ke, h1 - 1)
                nc.vector.tensor_scalar(KEY, U0, -1.0, 40.0, ALU.mult, ALU.min).then_inc(f_cp, 1)
                if before is not None:
                    before()
                lb, oml = M.lb[:, col], M.oml[:, col]
                dve.wait_ge(exped, h1)
                nc.vector.tensor_scalar(LOG, KEY, 1.0, None, ALU.add).then_inc(plus1, 1)
                dve.wait_ge(plus1, h1)
                nc.vector.reciprocal(LOG, LOG).then_inc(recip, 1)
                dve.wait_ge(recip, h1)
                nc.vector.scalar_tensor_tensor(KEY, KEY, oml, LOG, ALU.mult, ALU.mult).then_inc(key, 1)
                nc.vector.tensor_scalar(LOG, LOG, oml, lb, ALU.mult, ALU.add).then_inc(gate, 1)
                dve.wait_ge(log, h1)
                nc.vector.tensor_tensor_scan(CUM, keep, LOG, 0.0, ALU.mult, ALU.add).then_inc(cum, 1)

            def levels(h1, first=False):
                dve.wait_ge(cum, h1)
                if not first:
                    dve.wait_ge(s_mm, (h1 - 1) * 6)
                for n, h in enumerate(HALVES):
                    b, x = blocks(CUM, h), blocks(LEV[n], h)
                    ref = b[:, :, 0, h - 1:h].to_broadcast([P, T // (2 * h), h])
                    tt(x[:, :, 0, :], ref, b[:, :, 0, :], ALU.subtract)
                    tt(x[:, :, 1, :], b[:, :, 1, :], ref, ALU.subtract).then_inc(offs, 1)
                b = CUM.rearrange("p (n f) -> p n f", f=4)
                tt(DQ.rearrange("p (n f) -> p n f", f=4), b, b[:, :, 1:2].to_broadcast([P, T // 4, 4]),
                   ALU.subtract).then_inc(offs, 1)
                if not first:
                    dve.wait_ge(t_mm, h1 - 1)
                b = tiles(CUM)
                tt(tiles(KE), b[:, :, P - 1:P].to_broadcast([P, TT, P]), b, ALU.subtract).then_inc(offs, 1)
                dve.wait_ge(q_cp, h1)
                dve.wait_ge(key, h1)
                for n, h in enumerate(HALVES):
                    dve.wait_ge(decayed, (h1 - 1) * 10 + n + 1)
                    x = blocks(LEV[n], h)
                    tt(x[:, :, 0, :], x[:, :, 0, :], blocks(KEY, h)[:, :, 0, :], ALU.mult)
                    tt(x[:, :, 1, :], x[:, :, 1, :], blocks(QRY, h)[:, :, 1, :], ALU.mult)
                dve.wait_ge(decayed, (h1 - 1) * 10 + 8)
                tt(DK, DK, KEY, ALU.mult)
                tt(DQ, DQ, QRY, ALU.mult)
                tt(QE, QE, QRY, ALU.mult).then_inc(lev, 1)
                dve.wait_ge(decayed, (h1 - 1) * 10 + 10)
                tt(KE, KE, KEY, ALU.mult).then_inc(ke, 1)

            def pick(g, h, data):
                out = SC[:, 512 * g:512 * (g + 1)]
                if h:
                    n = HALVES.index(h)
                    mask = M.hmask[:, 256 * n:256 * (n + 1)]
                    out = blocks(out, h)[:, :, 1, :]
                    data = blocks(data, h)[:, :, 1, :]
                    mask = mask.rearrange("p (n h) -> p n h", h=h)
                else:
                    mask = M.hmask[:, 1280:1792]
                return nc.vector.copy_predicated(out, mask, data)

            def attend(h1, first=False):
                if not first:
                    dve.wait_ge(o_mm, h1 - 1)
                for k in range(6):
                    unit = M.ps[:, (k + 1) % 4, :]
                    for j in range(2):
                        if j == 0:
                            dve.wait_ge(s_mm, (h1 - 1) * 6 + k + 1)
                        if j:
                            dve.wait_ge(picked, (h1 - 1) * 6 + k + 1)
                        elif k:
                            dve.wait_ge(s_cp, (h1 - 1) * 6 + k)
                        dve.sem_inc(begun, 1)
                        level = (0,) + HALVES
                        pick(k // 3, level[2 * (k % 3) + j], unit[:, 512 * j:512 * (j + 1)]
                             ).then_inc(s_cp if j else picked, 1)
                dve.wait_ge(kv_mm, h1)
                for t in range(TT - 1):
                    kv = U3[:, t * P:(t + 1) * P]
                    if t == 0:
                        nc.vector.tensor_copy(ST[:, 1, :], kv).then_inc(st, 1)
                    else:
                        dve.wait_ge(st, (h1 - 1) * 7 + t)
                        nc.vector.scalar_tensor_tensor(ST[:, t + 1, :], ST[:, t, :], END[:, t:t + 1], kv,
                                                       ALU.mult, ALU.add).then_inc(st, 1)
                dve.wait_ge(o_mm, h1)
                nc.vector.tensor_copy(LOG, U1).then_inc(o_cp, 1)

            def finish(h, h1):
                dve.wait_ge(rs, h1)
                dve.wait_ge(o_cp, h1)
                nc.vector.scalar_tensor_tensor(LOG, LOG, gain[:, bass.ds(h, 1)], KET, ALU.mult,
                                               ALU.mult).then_inc(z1, 1)
                dve.wait_ge(z1, h1)
                zt = M.zt[:, bass.ds(h, 1), :]
                tt(zt, zt, LOG.unsqueeze(1), ALU.mult).then_inc(z, 1)
                dve.wait_ge(z, h1)

            def body(i, c, first, last_head=False):
                h = head(i, c)
                if not last_head:
                    forget(h + 2, bass.ds(h + 1, 1), None if first else (lambda: finish(h - 1, h)))
                else:
                    finish(h - 1, h)
                attend(h + 1, first)
                if not last_head:
                    levels(h + 2)

            nc.vector.memset(SC, 0.0).then_inc(cleared, 1)
            dve.wait_ge(cleared, 1)
            forget(1, bass.ds(0, 1), None, True)
            levels(1, True)
            loop(dve, body)
            finish(HEADS - 1, HEADS)


class Cut:

    def __init__(self, ap):
        self.ap, self.at = ap, 0

    def __call__(self, n, a=None):
        assert self.at + n <= self.ap.shape[1], (self.at, n)
        piece = self.ap[:, self.at:self.at + n]
        self.at += n
        return piece if a is None else piece.rearrange("p (a n) -> p a n", a=a)


class Link:

    def __init__(self, eng, sem):
        self.eng, self.sem, self.n = eng, sem, 0

    def __call__(self, ins):
        self.n += 1
        ins.then_inc(self.sem, 1)
        self.eng.wait_ge(self.sem, self.n)


def zt_flat(M):
    return M.zt[:, :, :].rearrange("p a n -> p (a n)")


def ht_flat(M):
    return M.ht[:, :, :].rearrange("p a n -> p (a n)")


def mix_memory(M):
    z, c = Cut(zt_flat(M)), Cut(M.scr[:, :])
    M.pf = z(RT * T, RT)
    M.conv = z(CT * T, CT)
    M.qt = c(2 * T, 2)
    M.u = c(CT * (T + 2 * CPAD + 2), CT)
    M.kt = c(2 * MEM, 2)
    M.vm = c(2 * MEM, 2)
    M.mix_free = c.at


def memory_keys(nc, M, W, n0, mem, w_kv, prefetch=()):
    sem = M.semaphore
    rows, sq, root, step = (sem(f"mem_{x}") for x in ("rows_in", "squares", "root", "step"))
    turned, copied, k_mm, v_mm, done = (sem(f"mem_{x}") for x in ("turned", "copied", "keys", "values", "done"))
    c = Cut(zt_flat(M))
    rowsb, junk, mt = c(2 * D, 2), c(D), c(KD * MEM, KD)
    with nc.Block() as block:
        @block.sync
        def _(sp):
            for t in range(2):
                sp.dma_start(rowsb[:, t, :], mem[t * P:(t + 1) * P, :]).then_inc(rows, 16)
            if n0 not in M.sent:
                dma_chunk(sp, M, W, n0, n0 % 2, w_kv)
            for n, src in prefetch:
                dma_chunk(sp, M, W, n, n % 2, src)

        @block.scalar
        def _(act):
            act.wait_ge(rows, 32)
            for t in range(2):
                if t:
                    act.wait_ge(sq, t)
                nc.scalar.activation(junk, rowsb[:, t, :], ACT.Square, accum_out=M.small[:, t:t + 1]).then_inc(sq, 1)
            act.wait_ge(sq, 2)
            nc.scalar.activation(M.small[:, 8:10], M.small[:, 0:2], ACT.Sqrt, scale=1.0 / D,
                                 bias=M.eps).then_inc(root, 1)

        @block.vector
        def _(dve):
            link = Link(dve, step)
            dve.wait_ge(root, 1)
            link(nc.vector.reciprocal(M.small[:, 16:18], M.small[:, 8:10]))
            for t in range(2):
                link(nc.vector.tensor_scalar(rowsb[:, t, :], rowsb[:, t, :], M.small[:, 16 + t:17 + t], None,
                                             ALU.mult))
            for t in range(2):
                dve.wait_ge(turned, t + 1)
                nc.vector.tensor_tensor(mt[:, :, t * P:(t + 1) * P],
                                        M.ps[:, t, :].rearrange("p (k n) -> p k n", k=KD),
                                        M.p("norm_mem").unsqueeze(2).to_broadcast([P, KD, P]),
                                        ALU.mult).then_inc(copied, 1)
            dve.wait_ge(k_mm, 1)
            nc.vector.tensor_copy(M.kt, M.ps[:, 2, 0:2 * MEM].rearrange("p (a n) -> p a n", a=2)).then_inc(done, 1)
            dve.wait_ge(v_mm, 1)
            nc.vector.tensor_copy(M.vm, M.ps[:, 3, 0:2 * MEM].rearrange("p (a n) -> p a n", a=2)).then_inc(done, 1)

        @block.tensor
        def _(pe):
            for t in range(2):
                pe.wait_ge(step, 2 + t)
                for k in range(KD):
                    last = nc.tensor.transpose(M.ps[:, t, k * P:(k + 1) * P], rowsb[:, t, k * P:(k + 1) * P],
                                               M.c("ident"))
                last.then_inc(turned, 1)
            pe.wait_ge(copied, 2)
            W.wait(pe, n0)
            w = slot_view(M, n0 % 2, KD, 2 * MEM)
            for a in range(2):
                for k in range(KD):
                    last = nc.tensor.matmul(M.ps[:, 2, a * MEM:(a + 1) * MEM], lhsT=w[:, k, a * P:(a + 1) * P],
                                            rhs=mt[:, k, :], start=k == 0, stop=k == KD - 1)
            last.then_inc(k_mm, 1)
            for a in range(2):
                for k in range(KD):
                    last = nc.tensor.matmul(M.ps[:, 3, a * MEM:(a + 1) * MEM], lhsT=mt[:, k, a * P:(a + 1) * P],
                                            rhs=w[:, k, MEM:2 * MEM], start=k == 0, stop=k == KD - 1)
            last.then_inc(v_mm, 1)
            pe.wait_ge(v_mm, 1)
            pe.sem_inc(W.used, 1)


def mixer_projections(nc, M, W, n0, w_in, prefetch=()):
    sem = M.semaphore
    summed, copied, gated, glu = (sem(f"mix_{x}") for x in ("summed", "copied", "gated", "glu"))
    ready, step, shifted, conv = (sem(f"mix_{x}") for x in ("ready", "step", "shifted", "conv"))
    taps = [sem(f"conv_tap_{j}") for j in range(CT)]
    c = Cut(M.scr[:, M.mix_free:])
    val = c(CT * T, CT)
    raw = [c(T + 2) for _ in range(2)]
    mu0, mu1 = M.p("mu_prev"), M.p("mu_next")
    own = M.small[:, 32:32 + RT]
    taps_w = M.p("conv_w").rearrange("p (a k) -> p a k", a=CT)
    TILES = 20
    RW0 = TILES - RT
    with nc.Block() as block:
        @block.sync
        def _(sp):
            for j in range(TILES // 4):
                if n0 + j not in M.sent:
                    dma_chunk(sp, M, W, n0 + j, (n0 + j) % 2, w_in[j])
            for n, src in prefetch:
                dma_chunk(sp, M, W, n, n % 2, src)

        @block.tensor
        def _(pe):
            for j in range(TILES // 4):
                n = n0 + j
                W.wait(pe, n)
                w = slot_view(M, n % 2, KD, 512)
                for m in range(4):
                    u = 4 * j + m
                    if u >= 4:
                        pe.wait_ge(copied, u - 3)
                    feature_tile(nc, M, u % 4, w, slice(m * P, (m + 1) * P)).then_inc(summed, 1)
                pe.wait_ge(summed, 4 * j + 4)
                pe.sem_inc(W.used, 1)

        @block.scalar
        def _(act):
            act.wait_ge(ready, 1)
            for u in range(TILES):
                act.wait_ge(summed, u + 1)
                src = M.ps[:, u % 4, :]
                if u < 2:
                    nc.scalar.activation(M.qt[:, u, :], src, ACT.Copy).then_inc(copied, 1)
                elif u < 2 + CT:
                    nc.scalar.activation(val[:, u - 2, :], src, ACT.Copy).then_inc(copied, 1)
                elif u < RW0:
                    nc.scalar.activation(M.u[:, u - 2 - CT, CPAD:CPAD + T], src, ACT.Sigmoid).then_inc(copied, 1)
                else:
                    r = u - RW0
                    if r >= 2:
                        act.wait_ge(shifted, r - 1)
                    nc.scalar.activation(raw[r % 2][:, 1:1 + T], src, ACT.Copy).then_inc(copied, 1)

        @block.vector
        def _(dve):
            link = Link(dve, step)
            link(nc.vector.memset(M.u, 0.0))
            link(nc.vector.memset(raw[0], 0.0))
            link(nc.vector.memset(raw[1], 0.0))
            link(nc.vector.tensor_tensor(own, mu0, mu1, ALU.add))
            nc.vector.tensor_scalar(own, own, -1.0, 1.0, ALU.mult, ALU.add).then_inc(ready, 1)
            dve.wait_ge(ready, 1)
            dve.wait_ge(copied, RW0)
            mid = M.u[:, :, CPAD:CPAD + T]
            link(nc.vector.tensor_tensor(mid, mid, val, ALU.mult))

            def tap(k, a):
                x = M.u[:, a, k:k + T]
                if k == 0:
                    nc.vector.tensor_scalar(M.conv[:, a, :], x, taps_w[:, a, 0:1], M.p("conv_b")[:, a:a + 1],
                                            ALU.mult, ALU.add).then_inc(taps[a], 1)
                else:
                    dve.wait_ge(taps[a], k)
                    nc.vector.scalar_tensor_tensor(M.conv[:, a, :], x, taps_w[:, a, k:k + 1], M.conv[:, a, :],
                                                   ALU.mult, ALU.add).then_inc(taps[a], 1)

            todo = [(k, a) for k in range(CONV_K) for a in range(CT)]
            for r in range(RT):
                dve.wait_ge(copied, RW0 + r + 1)
                x, y = raw[r % 2], M.pf[:, r, :]
                link(nc.vector.tensor_scalar(y, x[:, 1:1 + T], own[:, r:r + 1], None, ALU.mult))
                link(nc.vector.scalar_tensor_tensor(y, x[:, 0:T], mu0[:, r:r + 1], y, ALU.mult, ALU.add))
                nc.vector.scalar_tensor_tensor(y, x[:, 2:2 + T], mu1[:, r:r + 1], y, ALU.mult,
                                               ALU.add).then_inc(shifted, 1)
                dve.wait_ge(shifted, r + 1)
                for k, a in todo[:8]:
                    tap(k, a)
                todo = todo[8:]
            for k, a in todo:
                tap(k, a)
            for a in range(CT):
                dve.wait_ge(taps[a], CONV_K)


def attention(nc, M):
    sem = M.semaphore
    s_mm, mx, ng, ex, rc, pr = (sem(f"att_{x}") for x in ("scores", "max", "bias", "exp", "recip", "probs"))
    p_mm, p_cp, o_mm, o_cp = (sem(f"att_{x}") for x in ("probs_turned", "probs_copied", "out_summed", "out_copied"))
    c = Cut(M.scr[:, M.mix_free:])
    prob = [c(AH * MEM, AH) for _ in range(2)]
    pt = [c(AH * MEM) for _ in range(2)]
    scale = 64.0 ** -0.5
    ORDER = (0, 2, 1, 3)

    def stat(j, t):
        return M.small[:, 24 * (t % 2) + 4 * j:24 * (t % 2) + 4 * j + 4]

    with nc.Block() as block:
        @block.tensor
        def _(pe):
            def scores(t):
                if t >= 2:
                    pe.wait_ge(ex, AH * (t - 1))
                for at, a in enumerate(ORDER):
                    o = 64 * (a % 2)
                    last = nc.tensor.matmul(M.ps[:, t % 2, at * MEM:(at + 1) * MEM],
                                            lhsT=M.qt[o:o + 64, a // 2, t * P:(t + 1) * P],
                                            rhs=M.kt[o:o + 64, a // 2, :], start=True, stop=True)
                last.then_inc(s_mm, 1)

            def turn(t):
                pe.wait_ge(pr, t + 1)
                if t:
                    pe.wait_ge(p_cp, t)
                for a in range(AH):
                    for m in range(2):
                        j = 2 * a + m
                        last = nc.tensor.transpose(M.ps[:, 2, j * P:(j + 1) * P],
                                                   prob[t % 2][:, a, m * P:(m + 1) * P], M.c("ident"))
                last.then_inc(p_mm, 1)

            def output(t):
                pe.wait_ge(p_cp, t + 1)
                if t:
                    pe.wait_ge(o_cp, t)
                for at, a in enumerate(ORDER):
                    o = 64 * (a % 2)
                    for m in range(2):
                        j = 2 * at + m
                        last = nc.tensor.matmul(M.ps[o:o + 64, 3, (a // 2) * P:(a // 2 + 1) * P],
                                                lhsT=M.vm[:, m, 64 * a:64 * a + 64],
                                                rhs=pt[t % 2][:, j * P:(j + 1) * P], start=m == 0, stop=m == 1)
                last.then_inc(o_mm, 1)

            scores(0)
            for t in range(TT):
                if t + 1 < TT:
                    scores(t + 1)
                turn(t)
                if t:
                    output(t - 1)
            output(TT - 1)

        @block.scalar
        def _(act):
            def exps(t):
                act.wait_ge(ng, t + 1)
                if t >= 2:
                    act.wait_ge(p_mm, t - 1)
                for a in range(AH):
                    nc.scalar.activation(prob[t % 2][:, a, :], M.ps[:, t % 2, a * MEM:(a + 1) * MEM], ACT.Exp,
                                         scale=scale, bias=stat(1, t)[:, a:a + 1],
                                         accum_out=stat(2, t)[:, a:a + 1]).then_inc(ex, 1)

            def probs_copy(t):
                act.wait_ge(p_mm, t + 1)
                if t >= 2:
                    act.wait_ge(o_mm, t - 1)
                nc.scalar.activation(pt[t % 2], M.ps[:, 2, :], ACT.Copy).then_inc(p_cp, 1)

            exps(0)
            for t in range(TT):
                if t + 1 < TT:
                    exps(t + 1)
                probs_copy(t)

        @block.vector
        def _(dve):
            def maxes(t):
                dve.wait_ge(s_mm, t + 1)
                if t >= 2:
                    dve.wait_ge(ex, AH * (t - 1))
                nc.vector.reduce_max(stat(0, t), M.ps[:, t % 2, :].rearrange("p (a n) -> p a n", a=AH),
                                     mybir.AxisListType.X).then_inc(mx, 1)
                dve.wait_ge(mx, t + 1)
                nc.vector.tensor_scalar(stat(1, t), stat(0, t), -scale, None, ALU.mult).then_inc(ng, 1)

            def copy_out(t):
                dve.wait_ge(o_mm, t + 1)
                nc.vector.tensor_copy(M.ht[:, 0:2, t * P:(t + 1) * P],
                                      M.ps[:, 3, 0:2 * P].rearrange("p (a n) -> p a n", a=2)).then_inc(o_cp, 1)

            maxes(0)
            for t in range(TT):
                dve.wait_ge(ex, AH * (t + 1))
                nc.vector.reciprocal(stat(3, t), stat(2, t)).then_inc(rc, 1)
                dve.wait_ge(rc, t + 1)
                nc.vector.tensor_tensor(prob[t % 2], prob[t % 2],
                                        stat(3, t).unsqueeze(2).to_broadcast([P, AH, MEM]),
                                        ALU.mult).then_inc(pr, 1)
                if t + 1 < TT:
                    maxes(t + 1)
                if t:
                    copy_out(t - 1)
            copy_out(TT - 1)


def conv_norm(nc, M):
    sem = M.semaphore
    m_mm, cen, sq, v_mm, root, step, fin = (
        sem(f"cn_{x}") for x in ("mean", "centred", "squared", "var", "root", "step", "out"))
    c = Cut(M.scr[:, M.mix_free:])
    sqr, mean = c(CT * T, CT), c(T)
    eps = M.small[:, 62:63]
    width = CT * P

    def channel_sum(unit, x):
        for half in range(2):
            for a in range(CT):
                last = nc.tensor.matmul(M.ps[:, unit, half * 512:(half + 1) * 512], lhsT=M.c("ones"),
                                        rhs=x[:, a, half * 512:(half + 1) * 512], start=a == 0, stop=a == CT - 1)
        return last

    with nc.Block() as block:
        @block.tensor
        def _(pe):
            channel_sum(0, M.conv).then_inc(m_mm, 1)
            pe.wait_ge(sq, 1)
            channel_sum(1, sqr).then_inc(v_mm, 1)

        @block.scalar
        def _(act):
            act.wait_ge(cen, CT)
            nc.scalar.activation(sqr, M.conv, ACT.Square).then_inc(sq, 1)
            act.wait_ge(v_mm, 1)
            nc.scalar.activation(mean, M.ps[:, 1, :], ACT.Ln, scale=1.0 / width, bias=eps).then_inc(root, 1)
            act.wait_ge(root, 1)
            nc.scalar.activation(mean, mean, ACT.Exp, scale=-0.5).then_inc(root, 1)
            for a in range(CT):
                act.wait_ge(step, 2 + a)
                nc.scalar.activation(M.ht[:, 2 + a, :], M.conv[:, a, :], ACT.Silu,
                                     scale=M.p("conv_g")[:, a:a + 1], bias=M.p("conv_beta")[:, a:a + 1]).then_inc(fin, 1)

        @block.vector
        def _(dve):
            link = Link(dve, step)
            link(nc.vector.memset(eps, 1e-5))
            dve.wait_ge(m_mm, 1)
            for a in range(CT):
                nc.vector.scalar_tensor_tensor(M.conv[:, a, :], M.ps[:, 0, :], -1.0 / width, M.conv[:, a, :],
                                               ALU.mult, ALU.add).then_inc(cen, 1)
            dve.wait_ge(root, 2)
            for a in range(CT):
                link(nc.vector.tensor_tensor(M.conv[:, a, :], M.conv[:, a, :], mean, ALU.mult))


def rwkv_common(nc, M, small_w, vt_dram, g_dram, prefetch=(), W=None):
    sem = M.semaphore
    w_in, ranks, step, sqd, ssq = (sem(f"rc_{x}") for x in ("weights_in", "ranks", "step", "squared", "square_sum"))
    root, vt_mm, vt_cp, g_mm, g_cp, out = (
        sem(f"rc_{x}") for x in ("root", "values_turned", "values_copied", "gate_summed", "gate_copied", "stored"))
    z, c, h = Cut(zt_flat(M)[:, RT * T:]), Cut(M.scr[:, :]), Cut(ht_flat(M)[:, 5 * T:])
    M.rw_w = z(9 * P, 3)
    M.kk = c(CT * T, CT)
    M.ks = c(CT * T, CT)
    M.rw_tiles = [c(T) for _ in range(12)] + [z(T) for _ in range(2)] + [h(T) for _ in range(2)]
    sq = c.ap[:, 6 * T:9 * T].rearrange("p (a n) -> p a n", a=CT)
    vt = c.ap[:, 9 * T:12 * T].rearrange("p (a c n) -> p a c n", a=CT, n=P)
    g = c.ap[:, 12 * T:15 * T].rearrange("p (a n) -> p a n", a=CT)
    eps = M.small[:, 61:62]
    PS = M.ps
    with nc.Block() as block:
        @block.sync
        def _(sp):
            sp.dma_start(M.rw_w, small_w.rearrange("p (a n) -> p a n", a=3)).then_inc(w_in, 16)
            for n, src in prefetch:
                dma_chunk(sp, M, W, n, n % 2, src)
            for a in range(CT):
                sp.wait_ge(vt_cp, a + 1)
                sp.dma_start(vt_dram[:, :, a * P:(a + 1) * P].rearrange("c p n -> p c n"), vt[:, a]).then_inc(out, 16)
            for a in range(CT):
                sp.wait_ge(g_cp, a + 1)
                sp.dma_start(g_dram[a], g[:, a, :]).then_inc(out, 16)
            sp.wait_ge(out, 16 * 6)

        @block.scalar
        def _(act):
            nc.scalar.activation(M.pf[:, 11, :], M.pf[:, 11, :], ACT.Sigmoid).then_inc(ranks, 1)
            nc.scalar.activation(M.pf[:, 9, :], M.pf[:, 9, :], ACT.Tanh).then_inc(ranks, 1)
            for a in range(CT):
                act.wait_ge(vt_mm, a + 1)
                nc.scalar.activation(vt[:, a].rearrange("p c n -> p (c n)"), PS[:, a, :], ACT.Copy).then_inc(vt_cp, 1)
            for a in range(CT):
                act.wait_ge(g_mm, a + 1)
                nc.scalar.activation(g[:, a, :], PS[:, a, :], ACT.Copy).then_inc(g_cp, 1)
            for a in range(CT):
                act.wait_ge(ssq, a + 1)
                act.wait_ge(sqd, 2)
                nc.scalar.activation(sq[:, a, :], PS[:, (a + 3) % 4, :], ACT.Ln, bias=eps).then_inc(root, 1)
            for a in range(CT):
                act.wait_ge(root, a + 1)
                nc.scalar.activation(sq[:, a, :], sq[:, a, :], ACT.Exp, scale=-0.5).then_inc(root, 1)

        @block.tensor
        def _(pe):
            for a in range(CT):
                for t in range(TT):
                    last = nc.tensor.transpose(PS[:, a, t * P:(t + 1) * P], M.pf[:, 6 + a, t * P:(t + 1) * P],
                                               M.c("ident"))
                last.then_inc(vt_mm, 1)
            pe.wait_ge(w_in, 16)
            pe.wait_ge(ranks, 1)
            for a in range(CT):
                pe.wait_ge(vt_cp, a + 1)
                for half in range(2):
                    last = nc.tensor.matmul(PS[:, a, half * 512:(half + 1) * 512],
                                            lhsT=M.rw_w[:, 2, a * P:(a + 1) * P],
                                            rhs=M.pf[:, 11, half * 512:(half + 1) * 512], start=True, stop=True)
                last.then_inc(g_mm, 1)
            pe.wait_ge(sqd, 1)
            for a in range(CT):
                if a:
                    pe.wait_ge(g_cp, a)
                for half in range(2):
                    last = nc.tensor.matmul(PS[:, (a + 3) % 4, half * 512:(half + 1) * 512], lhsT=M.c("blocks64"),
                                            rhs=sq[:, a, half * 512:(half + 1) * 512], start=True, stop=True)
                last.then_inc(ssq, 1)
            pe.wait_ge(ssq, CT)
            pe.sem_inc(sqd, 1)

        @block.vector
        def _(dve):
            link = Link(dve, step)
            link(nc.vector.memset(eps, 1e-12))
            k = M.pf[:, 3:6, :]
            link(nc.vector.tensor_tensor(M.kk, k, M.p("k_k").unsqueeze(2).to_broadcast([P, CT, T]), ALU.mult))
            nc.vector.tensor_tensor(sq, M.kk, M.kk, ALU.mult).then_inc(sqd, 1)
            for a in range(CT):
                dve.wait_ge(root, CT + a + 1)
                link(nc.vector.tensor_tensor(M.kk[:, a, :], M.kk[:, a, :], sq[:, a, :], ALU.mult))


def rwkv_directions(nc, M, rw_dram, bonus_dram):
    sem = M.semaphore
    up, sw, aa, lw, cum, kd, offs = (sem(f"rd_{x}") for x in ("ranks_up", "decay", "rate", "log", "cum", "key", "offs"))
    bo, ex, prod, bonus_out, step, c_mm, c_cp, cr = (
        sem(f"rd_{x}") for x in ("ks", "exps", "products", "bonus_stored", "step", "coef", "bonus", "carry"))
    keyed, shared = sem("rd_keyed"), sem("rd_keys_and_rates")
    stored = [[sem(f"rd_stored_{x}_{c}") for c in range(2)] for x in ("kk", "r", "kk_a", "k_d")]
    tiles = M.rw_tiles
    PS = M.ps

    def t8(ap):
        return ap.rearrange("p (c n) -> p c n", n=P)

    def rates(n):
        return tiles[2 * (n % 3):2 * (n % 3) + 2]

    def bufs(n):
        return tiles[6 + 5 * (n % 2):11 + 5 * (n % 2)]

    with nc.Block() as block:
        @block.tensor
        def _(pe):
            for n in range(6):
                d, p = divmod(n, CT)
                o = 64 * d
                for j in range(2):
                    if n >= 2:
                        pe.wait_ge((sw, aa)[j], n - 1)
                    for half in range(2):
                        last = nc.tensor.matmul(PS[:, 2 * (n % 2) + j, half * 512:(half + 1) * 512],
                                                lhsT=M.rw_w[o:o + 64, j, p * P:(p + 1) * P],
                                                rhs=M.pf[o:o + 64, 9 + j, half * 512:(half + 1) * 512],
                                                start=True, stop=True)
                    last.then_inc(up, 1)
            for p in range(CT):
                pe.wait_ge(bo, 1 + p)
                pe.wait_ge(aa, 6)
                for half in range(2):
                    last = nc.tensor.matmul(PS[:, p, half * 512:(half + 1) * 512], lhsT=M.c("blocks64"),
                                            rhs=M.ks[:, p, half * 512:(half + 1) * 512], start=True, stop=True)
                last.then_inc(c_mm, 1)

        @block.scalar
        def _(act):
            def sigmoids(n):
                T0, T1 = rates(n)
                if n >= 3:
                    act.wait_ge(prod, 4 * (n - 2))
                act.wait_ge(up, 2 * n + 1)
                nc.scalar.activation(T0, PS[:, 2 * (n % 2), :], ACT.Sigmoid,
                                     bias=M.p("w0")[:, n:n + 1]).then_inc(sw, 1)
                act.wait_ge(up, 2 * n + 2)
                nc.scalar.activation(T1, PS[:, 2 * (n % 2) + 1, :], ACT.Sigmoid,
                                     bias=M.p("a0")[:, n:n + 1]).then_inc(aa, 1)

            sigmoids(0)
            sigmoids(1)
            for n in range(6):
                T2, _, T4, T5, T6 = bufs(n)
                act.wait_ge(offs, 2 * n + 2)
                nc.scalar.activation(T4, T4, ACT.Exp, scale=-DECAY_SCALE).then_inc(ex, 1)
                nc.scalar.activation(T5, T2, ACT.Exp, scale=-DECAY_SCALE).then_inc(ex, 1)
                if n >= 2:
                    act.wait_ge(stored[2][n % 2], 16 * (n // 2))
                nc.scalar.activation(T6, T2, ACT.Exp, scale=DECAY_SCALE).then_inc(ex, 1)
                if n + 2 < 6:
                    sigmoids(n + 2)
            act.wait_ge(cr, 12)
            nc.scalar.activation(M.carry[:, :, :], M.carry[:, :, :], ACT.Exp, scale=-DECAY_SCALE).then_inc(ex, 1)

        @block.vector
        def _(dve):
            tt, stt, ts = nc.vector.tensor_tensor, nc.vector.scalar_tensor_tensor, nc.vector.tensor_scalar
            link = Link(dve, step)

            def offsets(n):
                d, p = divmod(n, CT)
                T0, T1 = rates(n)
                T2, T3, T4, T5, _ = bufs(n)
                mid, end = ((63, P - 1), (64, 0))[d]
                dve.wait_ge(sw, n + 1)
                keep = M.hmask[:, 1792 + T * d:1792 + T * (d + 1)]
                if d == 0:
                    link(nc.vector.tensor_tensor_scan(T2, keep, T0, 0.0, ALU.mult, ALU.add))
                else:
                    link(nc.vector.tensor_tensor_scan(T2[:, ::-1], keep[:, ::-1], T0[:, ::-1], 0.0,
                                                      ALU.mult, ALU.add))
                cm = t8(T2)
                mids, ends = cm[:, :, mid], cm[:, :, end]
                if d == 1:
                    mids, ends = mids[:, ::-1], ends[:, ::-1]
                col = M.carry[:, :, n]
                tt(col, ends, mids, ALU.subtract).then_inc(cr, 1)
                dve.wait_ge(cr, 2 * n + 1)
                tt(col[:, 0:TT - 1], col[:, 0:TT - 1], mids[:, 1:TT], ALU.add).then_inc(cr, 1)
                dve.wait_ge(aa, n + 1)
                if n >= 2:
                    dve.wait_ge(stored[3][n % 2], 16 * (n // 2))
                link(ts(T3, T1, -1.0, M.p("k_a")[:, p:p + 1], ALU.add, ALU.mult))
                link(stt(T3, T3, 1.0, M.pf[:, 3 + p, :], ALU.add, ALU.mult))
                dve.sem_inc(keyed, 1)
                dve.wait_ge(cr, 2 * n + 2)
                if n >= 2:
                    for w in range(2):
                        dve.wait_ge(stored[w][n % 2], 16 * (n // 2))
                link(nc.vector.tensor_copy(T5[:, 0:TT], cm[:, :, mid]))
                tt(cm, cm, T5[:, 0:TT].unsqueeze(2).to_broadcast([P, TT, P]), ALU.subtract).then_inc(offs, 1)
                dve.wait_ge(offs, 2 * n + 1)
                tt(T4, T2, T0, ALU.subtract).then_inc(offs, 1)

            def products(n):
                d, p = divmod(n, CT)
                T1 = rates(n)[1]
                _, T3, T4, T5, T6 = bufs(n)
                dve.wait_ge(ex, 3 * n + 3)
                dve.wait_ge(shared, 2 * n + 2)
                tt(T4, T4, M.kk[:, p, :], ALU.mult).then_inc(prod, 1)
                tt(T5, T5, M.pf[:, p, :], ALU.mult).then_inc(prod, 1)
                tt(T3, T3, T6, ALU.mult).then_inc(prod, 1)
                dve.wait_ge(prod, 4 * n + 3)
                tt(T6, T1, T6, ALU.mult).then_inc(prod, 1)

            offsets(0)
            for n in range(6):
                if n + 1 < 6:
                    offsets(n + 1)
                products(n)
            for p in range(CT):
                stt(M.ks[:, p, :], M.ks[:, p, :], M.p("r_k")[:, p:p + 1], M.pf[:, p, :], ALU.mult,
                    ALU.mult).then_inc(bo, 1)
            for p in range(CT):
                dve.wait_ge(c_mm, p + 1)
                tt(M.ks[:, p, :], PS[:, p, :], M.pf[:, 6 + p, :], ALU.mult).then_inc(c_cp, 1)

        @block.gpsimd
        def _(pool):
            for n in range(6):
                d, p = divmod(n, CT)
                T1, T3 = rates(n)[1], bufs(n)[1]
                pool.wait_ge(keyed, n + 1)
                if d:
                    pool.wait_ge(shared, 2 * (n - CT) + 1)
                    nc.gpsimd.tensor_tensor(M.ks[:, p, :], M.ks[:, p, :], T3, ALU.add).then_inc(shared, 1)
                else:
                    nc.gpsimd.tensor_copy(M.ks[:, p, :], T3).then_inc(shared, 1)
                nc.gpsimd.tensor_tensor(T1, T1, M.kk[:, p, :], ALU.mult).then_inc(shared, 1)

        @block.sync
        def _(sp):
            for n in range(6):
                d, p = divmod(n, CT)
                b = bufs(n)
                for k, (w, j) in enumerate(((0, 2), (1, 3), (3, 1), (2, 4))):
                    sp.wait_ge(prod, 4 * n + k + 1)
                    at = (4 * p + w) * P
                    sp.dma_start(rw_dram[d, :, :, at:at + P].rearrange("c p n -> p c n"), t8(b[j])
                                 ).then_inc(stored[w][n % 2], 16)
            for p in range(CT):
                sp.wait_ge(c_cp, p + 1)
                sp.dma_start(bonus_dram[p], M.ks[:, p, :]).then_inc(bonus_out, 16)
            for w in range(4):
                for c in range(2):
                    sp.wait_ge(stored[w][c], 16 * 3)
            sp.wait_ge(bonus_out, 16 * CT)


def rwkv_steps(nc, M, rw_dram, vt_dram, masks_dram):
    sem = M.semaphore
    loaded = [sem(f"rs_loaded_{c}") for c in range(2)]
    m_in, zero, cleared = sem("rs_masks_in"), sem("rs_zeroed"), sem("rs_values_cleared")
    a_mm, a_cp, init, initp = sem("rs_triangles"), sem("rs_triangles_masked"), sem("rs_inverse_begun"), sem("rs_pairs")
    init_last = sem("rs_last_inverse_begun")
    p_mm, p_cp, x_mm, x_cp = (sem(f"rs_{x}") for x in ("half_summed", "half_masked", "join_summed", "joined"))
    t_mm, t_cp, r_mm, r_cp, u_mm, u_cp = (
        sem(f"rs_{x}") for x in ("turned", "turned_copied", "rhs_summed", "rhs_copied", "u_summed", "u_copied"))
    y_mm, y_cp, s_mm, s_ad, s_cp = (sem(f"rs_{x}") for x in ("y_summed", "y_added", "state_summed", "state_added",
                                                           "state_ready"))
    c = Cut(zt_flat(M))
    e = Cut(M.scr[:, :])
    IN = [c(2 * 3 * 4 * P).rearrange("p (d a w n) -> p d a w n", d=2, a=3, w=4) for _ in range(2)]
    V = [c(2 * CT * 2 * P).rearrange("p (d a e n) -> p d a e n", d=2, a=CT, e=2) for _ in range(2)]
    KM = [c(CT * 256, CT) for _ in range(4)]
    LL = [c(CT * P, CT) for _ in range(4)]
    X = [c(CT * P, CT) for _ in range(4)]
    BM = [e(CT * 256, CT) for _ in range(4)]
    Z = [e(CT * P, CT) for _ in range(4)]
    P1 = [e(CT * P, CT) for _ in range(4)]
    R0 = e(2 * CT * 2 * P).rearrange("p (d a e n) -> p d a e n", d=2, a=CT, e=2)
    U = e(2 * CT * P, 2)
    TOK = e(12 * P, 12)
    MASKS = e(RWM_N)
    SM = [e(6 * P, 6) for _ in range(2)]
    Y = M.ht[:, 5:8, :]

    def mask(name):
        a, n = RWM[name]
        return MASKS[:, a:a + n]

    rwm, pair = mask("rw_mask"), mask("pair_mask")
    F = M.ps[:, :, :].rearrange("p a n -> p (a n)")
    L = len(JOINS)

    def b3(ap):
        return ap.unsqueeze(1).to_broadcast([P, CT, ap.shape[1]])

    groups = [(g // 2, g % 2) for g in range(4)]

    def run(eng, body):
        body(0, 0, True)
        body(0, 1, False)
        with eng.Fori(1, TT // 2) as i:
            body(i, 0, False)
            body(i, 1, False)

    with nc.Block() as block:
        @block.sync
        def _(sp):
            sp.dma_start(MASKS, masks_dram).then_inc(m_in, 16)

            def load(i, c):
                s = i * 2 + c
                chunks = (s, -s + (TT - 1))
                for d in range(2):
                    src = rw_dram[d, bass.ds(chunks[d], 1), :, :].rearrange("o p n -> (o p) n")
                    sp.dma_start(IN[c][:, d].rearrange("p a w n -> p (a w n)"), src).then_inc(loaded[c], 16)
                    vt = vt_dram[bass.ds(chunks[d], 1), :, :].rearrange("o p (a e n) -> (o p) a e n", e=2, n=64)
                    for par in range(2):
                        sp.dma_start(V[c][:, d, :, par, 64 * par:64 * par + 64], vt[:, :, par, :]
                                     ).then_inc(loaded[c], 16)

            sp.wait_ge(cleared, 2)
            load(0, 0)
            load(0, 1)
            with sp.Fori(1, TT // 2) as i:
                for c in range(2):
                    sp.wait_ge(s_mm, i * 2 + (c - 1))
                    load(i, c)

        @block.tensor
        def _(pe):
            def body(i, c, first):
                s = i * 2 + c
                inp, v, sm = IN[c], V[c], SM[c]
                pe.wait_ge(loaded[c], i * 96 + 96)
                for g, (d, par) in enumerate(groups):
                    o, base = 64 * par, 2048 * par
                    if g < 2:
                        if not first:
                            if g == 0:
                                pe.wait_ge(t_cp, s)
                            else:
                                pe.wait_ge(y_cp, s)
                                pe.wait_ge(s_ad, s * 2)
                    else:
                        pe.wait_ge(a_cp, s * 4 + (g - 1))
                    for p in range(CT):
                        k, b, a = (inp[o:o + 64, d, p, w, :] for w in (0, 2, 3))
                        kr = inp[o:o + 64, d, p, 0:2, :].rearrange("p w n -> p (w n)")
                        nc.tensor.matmul(F[:, base + 256 * p:base + 256 * (p + 1)], lhsT=b, rhs=kr,
                                         start=True, stop=True)
                        at = base + 768 + 256 * p
                        nc.tensor.matmul(F[:, at:at + 256], lhsT=a, rhs=kr, start=True, stop=True)
                        at = base + 1536 + P * p
                        last = nc.tensor.matmul(F[:, at:at + P], lhsT=k, rhs=b, start=True, stop=True)
                    last.then_inc(a_mm, 1)
                pe.wait_ge(a_cp, s * 4 + 4)
                for n, b in enumerate(JOINS):
                    for g, (d, par) in enumerate(groups):
                        if n == 0 and g < 3:
                            pe.wait_ge(init, s * 3 + (g + 1))
                        elif n == 0:
                            pe.wait_ge(init_last, s * 4 + 4)
                        else:
                            pe.wait_ge(x_cp, s * (4 * L) + (4 * (n - 1) + g + 1))
                        low = LL[g] if d else BM[g]
                        for p in range(CT):
                            at = 512 * g + P * p
                            last = nc.tensor.matmul(F[:, at:at + P], lhsT=low[:, p, 0:P], rhs=X[g][:, p, :],
                                                    start=True, stop=True)
                        last.then_inc(p_mm, 1)
                    for g, (d, par) in enumerate(groups):
                        pe.wait_ge(p_cp, s * (4 * L) + (4 * n + g + 1))
                        for p in range(CT):
                            at = 512 * g + P * p
                            if n < L - 1 or d == 1:
                                last = nc.tensor.matmul(F[:, 2048 + at:2048 + at + P], lhsT=Z[g][:, p, :],
                                                        rhs=P1[g][:, p, :], start=True, stop=True)
                            if n < L - 1 or d == 0:
                                last = nc.tensor.matmul(F[:, at:at + P], lhsT=P1[g][:, p, :], rhs=Z[g][:, p, :],
                                                        start=True, stop=True)
                        last.then_inc(x_mm, 1)
                pe.wait_ge(x_cp, s * (4 * L) + 4 * L)
                pe.wait_ge(zero, 4)
                if not first:
                    pe.wait_ge(s_cp, s * 2)
                pairs = [(d, p) for d in range(2) for p in range(CT)]
                for d, p in pairs:
                    r = F[:, 2048 + 512 * d + P * p:2048 + 512 * d + P * (p + 1)]
                    nc.tensor.matmul(r, lhsT=inp[:, d, p, 0, :], rhs=sm[:, 3 * d + p, :], start=True, stop=False)
                    for par in range(2):
                        last = nc.tensor.matmul(r, lhsT=KM[2 * d + par][:, p, 0:P], rhs=v[:, d, p, par, :],
                                                start=False, stop=par == 1)
                    if p == CT - 1:
                        last.then_inc(r_mm, 1)
                for w in range(2):
                    for dp in range(6):
                        at = (6 * w + dp) * P
                        last = nc.tensor.transpose(F[:, at:at + P], inp[:, dp // 3, dp % 3, 2 + w, :], M.c("ident"))
                last.then_inc(t_mm, 1)
                for d, p in pairs:
                    if p == 0:
                        pe.wait_ge(r_cp, s * 2 + (d + 1))
                    inv_t = X if d else Z
                    u = F[:, 3072 + 512 * d + P * p:3072 + 512 * d + P * (p + 1)]
                    for par in range(2):
                        last = nc.tensor.matmul(u, lhsT=inv_t[2 * d + par][:, p, :], rhs=R0[:, d, p, par, :],
                                                start=par == 0, stop=par == 1)
                    if p == CT - 1:
                        last.then_inc(u_mm, 1)
                def begin_y(d, p):
                    y = F[:, 2048 + 512 * d + P * p:2048 + 512 * d + P * (p + 1)]
                    nc.tensor.matmul(y, lhsT=sm[:, 3 * d + p, :], rhs=inp[:, d, p, 1, :], start=True, stop=False)
                    nc.tensor.matmul(y, lhsT=v[:, d, p, 0, :], rhs=KM[2 * d][:, p, P:2 * P], start=False, stop=False)
                    return y

                begun = {d: begin_y(d, 0) for d in range(2)}
                pe.wait_ge(t_cp, s + 1)
                for d, p in pairs:
                    if p == 0:
                        pe.wait_ge(u_cp, s * 2 + (d + 1))
                    y = begin_y(d, p) if p else begun[d]
                    for par in range(2):
                        o, h = 64 * par, 64 * (2 * p + par)
                        nc.tensor.matmul(y[o:o + 64, :], lhsT=U[:, d, h:h + 64],
                                         rhs=BM[2 * d + par][:, p, P:2 * P], start=False, stop=False,
                                         skip_group_check=True)
                    last = nc.tensor.matmul(y, lhsT=v[:, d, p, 1, :], rhs=KM[2 * d + 1][:, p, P:2 * P],
                                            start=False, stop=True)
                last.then_inc(y_mm, 1)
                for d, p in pairs:
                    ds = F[:, 3072 + 512 * d + P * p:3072 + 512 * d + P * (p + 1)]
                    nc.tensor.matmul(ds, lhsT=TOK[:, 3 * d + p, :], rhs=U[:, d, P * p:P * (p + 1)],
                                     start=True, stop=False)
                    for par in range(2):
                        last = nc.tensor.matmul(ds, lhsT=TOK[:, 6 + 3 * d + p, :], rhs=v[:, d, p, par, :],
                                                start=False, stop=par == 1)
                last.then_inc(s_mm, 1)

            run(pe, body)

        @block.scalar
        def _(act):
            def body(i, c, first):
                s = i * 2 + c
                if first:
                    act.wait_ge(zero, 4)
                for d in range(2):
                    act.wait_ge(r_mm, s * 2 + (d + 1))
                    src = F[:, 2048 + 512 * d:2048 + 512 * d + 384].rearrange("p (a e n) -> p a e n", a=CT, e=2)
                    for par in range(2):
                        last = nc.scalar.activation(R0[:, d, :, par, 64 * par:64 * par + 64], src[:, :, par, :],
                                                    ACT.Copy, scale=-1.0)
                    last.then_inc(r_cp, 1)
                act.wait_ge(t_mm, s + 1)
                if not first:
                    act.wait_ge(s_mm, s)
                nc.scalar.activation(TOK.rearrange("p a n -> p (a n)"), F[:, 0:12 * P], ACT.Copy).then_inc(t_cp, 1)
            run(act, body)

        @block.gpsimd
        def _(pool):
            def body(i, c, first):
                s = i * 2 + c
                for g, (d, par) in enumerate(groups[:3]):
                    pool.wait_ge(a_cp, s * 4 + (g + 1))
                    if not first:
                        pool.wait_ge(u_mm, s * 2)
                    src = (LL[g], BM[g][:, :, 0:P]) if d == 0 else (BM[g][:, :, 0:P], LL[g])
                    nc.gpsimd.tensor_tensor(X[g], src[0], b3(pair[:, 0:P]), ALU.mult).then_inc(initp, 1)
                    nc.gpsimd.tensor_tensor(Z[g], src[1], b3(pair[:, P:2 * P]), ALU.mult).then_inc(initp, 1)
                    pool.wait_ge(initp, s * 9 + (3 * g + 2))
                    nc.gpsimd.tensor_tensor(X[g], X[g], b3(M.c("ident")), ALU.add).then_inc(initp, 1)
                    nc.gpsimd.tensor_tensor(Z[g], Z[g], b3(M.c("ident")), ALU.add).then_inc(init, 1)
                    pool.wait_ge(initp, s * 9 + (3 * g + 3))

            pool.wait_ge(m_in, 16)
            run(pool, body)

        @block.vector
        def _(dve):
            tt = nc.vector.tensor_tensor

            def body(i, c, first):
                s = i * 2 + c
                sm, new = SM[c], SM[1 - c]
                for g, (d, par) in enumerate(groups):
                    base = 2048 * par
                    dve.wait_ge(a_mm, s * 4 + (g + 1))
                    if not first:
                        dve.wait_ge(y_mm, s)
                        dve.wait_ge(init, s * 3)
                    m = 640 * d
                    tt(BM[g], F[:, base:base + 768].rearrange("p (a n) -> p a n", a=CT), b3(rwm[:, m:m + 256]), ALU.mult)
                    tt(KM[g], F[:, base + 768:base + 1536].rearrange("p (a n) -> p a n", a=CT),
                       b3(rwm[:, m + 256:m + 512]), ALU.mult)
                    tt(LL[g], F[:, base + 1536:base + 1920].rearrange("p (a n) -> p a n", a=CT),
                       b3(rwm[:, m + 512:m + 640]), ALU.mult).then_inc(a_cp, 1)
                dve.wait_ge(a_cp, s * 4 + 4)
                if not first:
                    dve.wait_ge(u_mm, s * 2)
                tt(X[3], BM[3][:, :, 0:P], b3(pair[:, 0:P]), ALU.mult).then_inc(init_last, 1)
                tt(Z[3], LL[3], b3(pair[:, P:2 * P]), ALU.mult).then_inc(init_last, 1)
                dve.wait_ge(init_last, s * 4 + 2)
                tt(X[3], X[3], b3(M.c("ident")), ALU.add).then_inc(init_last, 1)
                tt(Z[3], Z[3], b3(M.c("ident")), ALU.add).then_inc(init_last, 1)
                for n, b in enumerate(JOINS):
                    for g, (d, par) in enumerate(groups):
                        dve.wait_ge(p_mm, s * (4 * L) + (4 * n + g + 1))
                        m = mask("join_mask")[:, P * n:P * (n + 1)]
                        tt(P1[g], F[:, 512 * g:512 * g + 384].rearrange("p (a n) -> p a n", a=CT), b3(m),
                           ALU.mult).then_inc(p_cp, 1)
                    for g, (d, par) in enumerate(groups):
                        dve.wait_ge(x_mm, s * (4 * L) + (4 * n + g + 1))
                        for k, dst in enumerate((X[g], Z[g])):
                            if n == L - 1 and k == d:
                                continue
                            at = 2048 * (1 - k) + 512 * g
                            last = tt(dst, dst, F[:, at:at + 384].rearrange("p (a n) -> p a n", a=CT), ALU.add)
                        last.then_inc(x_cp, 1)
                if not first:
                    dve.wait_ge(y_mm, s)
                for d in range(2):
                    dve.wait_ge(u_mm, s * 2 + (d + 1))
                    nc.vector.tensor_copy(U[:, d, :], F[:, 3072 + 512 * d:3072 + 512 * d + 384]).then_inc(u_cp, 1)
                dve.wait_ge(s_mm, s + 1)
                car = M.carry[:, bass.ds(s, 1), :].rearrange("p o n -> p (o n)")
                for o in (0, 64):
                    r, q = slice(o, o + 64), slice(o, o + 64)
                    for d in range(2):
                        ds = F[r, 3072 + 512 * d:3072 + 512 * d + 384].rearrange("p (a n) -> p a n", a=CT)
                        last = tt(new[r, 3 * d:3 * d + 3, q], sm[r, 3 * d:3 * d + 3, q], ds[:, :, q], ALU.add)
                    last.then_inc(s_ad, 1)
                for j, o in enumerate((0, 64)):
                    r, q = slice(o, o + 64), slice(o, o + 64)
                    dve.wait_ge(s_ad, s * 2 + (j + 1))
                    tt(new[r, :, q], new[r, :, q], car[r].unsqueeze(2).to_broadcast([64, 6, 64]),
                       ALU.mult).then_inc(s_cp, 1)
                dve.wait_ge(y_mm, s + 1)
                for d, ch in enumerate((s, -s + (TT - 1))):
                    y = Y[:, :, bass.ds(ch * P, P)]
                    last = tt(y, y, F[:, 2048 + 512 * d:2048 + 512 * d + 384].rearrange("p (a n) -> p a n", a=CT),
                              ALU.add)
                last.then_inc(y_cp, 1)
                dve.wait_ge(y_cp, s + 1)

            for v in V:
                nc.vector.memset(v, 0.0).then_inc(cleared, 1)
            for place in (SM[0], SM[1], Y, R0):
                nc.vector.memset(place, 0.0).then_inc(zero, 1)
            dve.wait_ge(zero, 4)
            dve.wait_ge(m_in, 16)
            run(dve, body)


def rwkv_finish(nc, M, bonus_dram, g_dram):
    sem = M.semaphore
    ins, m_mm, cen, sqd, v_mm, root, step, fin = (
        sem(f"rf_{x}") for x in ("in", "mean", "centred", "squared", "var", "root", "step", "done"))
    c = Cut(M.scr[:, :])
    bonus, gate, sq = (c(CT * T, CT) for _ in range(3))
    Y = M.ht[:, 5:8, :]
    eps = M.small[:, 60:61]

    def head_sum(unit, x):
        for half in range(2):
            last = nc.tensor.matmul(M.ps[:, unit, half * 512:(half + 1) * 512], lhsT=M.c("blocks64"),
                                    rhs=x[:, half * 512:(half + 1) * 512], start=True, stop=True)
        return last

    with nc.Block() as block:
        @block.sync
        def _(sp):
            for a in range(CT):
                sp.dma_start(bonus[:, a, :], bonus_dram[a]).then_inc(ins, 16)
                sp.dma_start(gate[:, a, :], g_dram[a]).then_inc(ins, 16)

        @block.tensor
        def _(pe):
            for a in range(CT):
                head_sum(a, Y[:, a, :]).then_inc(m_mm, 1)
            for a in range(CT):
                pe.wait_ge(sqd, a + 1)
                head_sum((a + 3) % 4, sq[:, a, :]).then_inc(v_mm, 1)

        @block.scalar
        def _(act):
            for a in range(CT):
                act.wait_ge(cen, a + 1)
                nc.scalar.activation(sq[:, a, :], Y[:, a, :], ACT.Square).then_inc(sqd, 1)
            act.wait_ge(step, 1)
            for a in range(CT):
                act.wait_ge(v_mm, a + 1)
                nc.scalar.activation(sq[:, a, :], M.ps[:, (a + 3) % 4, :], ACT.Ln, scale=1.0 / 64,
                                     bias=eps).then_inc(root, 1)
            for a in range(CT):
                act.wait_ge(root, a + 1)
                nc.scalar.activation(sq[:, a, :], sq[:, a, :], ACT.Exp, scale=-0.5).then_inc(root, 1)

        @block.vector
        def _(dve):
            tt, stt = nc.vector.tensor_tensor, nc.vector.scalar_tensor_tensor
            link = Link(dve, step)
            link(nc.vector.memset(eps, 64e-5))
            for a in range(CT):
                dve.wait_ge(m_mm, a + 1)
                stt(Y[:, a, :], M.ps[:, a, :], -1.0 / 64, Y[:, a, :], ALU.mult, ALU.add).then_inc(cen, 1)
            dve.wait_ge(ins, 16 * 2 * CT)
            for a in range(CT):
                y = Y[:, a, :]
                dve.wait_ge(root, CT + a + 1)
                link(stt(y, y, M.p("lnx_g")[:, a:a + 1], sq[:, a, :], ALU.mult, ALU.mult))
                link(stt(y, y, M.p("lnx_b")[:, a:a + 1], bonus[:, a, :], ALU.add, ALU.add))
                link(tt(y, y, gate[:, a, :], ALU.mult))


class ExpertMemory:

    def __init__(self, nc, M):
        z = Cut(zt_flat(M))
        self.w = {"gate": [M.ring[:, 0, :], M.ring[:, 1, :]],
                  "up": [z(CHUNK_W), z(CHUNK_W)], "down": [z(CHUNK_W), z(CHUNK_W)]}
        self.loaded = {k: [nc.alloc_semaphore(f"expert_{k}_loaded_{j}") for j in range(2)] for k in self.w}
        self.gates = M.par[:, 0:NE]
        self.idx = M.par[:, NE:2 * NE].bitcast(U32)

    def first(self, w):
        return [(self.w[k][j], w[k][0, j], self.loaded[k][j]) for k in ("gate", "up", "down") for j in range(2)]


def route(nc, M, E, hf_out, raw_out):
    sem = M.semaphore
    l_mm, ce, ex, step, a_mm, i_mm = (
        sem(f"rt_{x}") for x in ("logits", "centred", "exp", "step", "affinity_turned", "picks_turned"))
    c = Cut(M.scr[:, 0:TT * D])
    aff = c(TT * NE, TT)
    rows = [c(T)[0:NE, :] for _ in range(2)]
    best = c(CAP)[0:NE, :]
    where = c(CAP)[0:NE, :].bitcast(U32)
    where_f = c(CAP)[0:NE, :]
    router = M.p("router").rearrange("p (k n) -> p k n", k=KD)
    LG = M.ps[:, 3, 0:TT * NE].rearrange("p (a n) -> p a n", a=TT)
    AX = mybir.AxisListType.X
    with nc.Block() as block:
        @block.sync
        def _(sp):
            sp.wait_ge(hf_out, 16 * TT)
            sp.wait_ge(raw_out, 16 * TT)

        @block.tensor
        def _(pe):
            for t in range(TT):
                for k in range(KD):
                    last = nc.tensor.matmul(LG[:, t, :], lhsT=M.ht[:, k, t * P:(t + 1) * P], rhs=router[:, k, :],
                                            start=k == 0, stop=k == KD - 1)
            last.then_inc(l_mm, 1)
            pe.wait_ge(ce, 2)
            for t in range(TT):
                last = nc.tensor.transpose(M.ps[0:NE, 0, t * P:(t + 1) * P], aff[:, t, :], M.c("ident"))
            last.then_inc(a_mm, 1)
            pe.wait_ge(i_mm, 1)
            nc.tensor.transpose(M.ps[:, 1, 0:NE], best, M.c("ident")[0:NE, 0:NE])
            nc.tensor.transpose(M.ps[:, 1, NE:2 * NE], where_f, M.c("ident")[0:NE, 0:NE]).then_inc(i_mm, 1)

        @block.scalar
        def _(act):
            act.wait_ge(ce, 1)
            nc.scalar.activation(aff, aff, ACT.Exp).then_inc(ex, 1)

        @block.vector
        def _(dve):
            link = Link(dve, step)
            stat = M.small[:, 0:TT]
            dve.wait_ge(l_mm, 1)
            dve.wait_ge(raw_out, 16 * TT)
            link(nc.vector.reduce_max(stat, LG, AX))
            nc.vector.tensor_tensor(aff, LG, stat.unsqueeze(2).to_broadcast([P, TT, NE]), ALU.subtract).then_inc(ce, 1)
            dve.wait_ge(ex, 1)
            link(nc.vector.reduce_sum(stat, aff, AX))
            link(nc.vector.reciprocal(stat, stat))
            nc.vector.tensor_tensor(aff, aff, stat.unsqueeze(2).to_broadcast([P, TT, NE]), ALU.mult).then_inc(ce, 1)
            dve.wait_ge(a_mm, 1)
            link(nc.vector.tensor_copy(rows[0], M.ps[0:NE, 0, :]))
            for r in range(CAP // 8):
                src, dst = rows[r % 2], rows[1 - r % 2]
                eight = best[:, 8 * r:8 * r + 8]
                link(nc.vector.max(eight, src))
                nc.vector.max_index(where[:, 8 * r:8 * r + 8], eight, src)
                link(nc.vector.match_replace(dst, eight, src, -1.0))
            link(nc.vector.tensor_copy(where_f, where))
            dve.sem_inc(i_mm, 1)
            dve.wait_ge(i_mm, 2)
            link(nc.vector.tensor_copy(E.gates, M.ps[:, 1, 0:NE]))
            link(nc.vector.tensor_copy(E.idx, M.ps[:, 1, NE:2 * NE]))


def experts(nc, M, E, w, hf_dram, acc_dram):
    sem = M.semaphore
    xe_in, xt_mm, xt_cp, g_mm, g_cp, u_mm, h_ok, th_mm, th_cp, d_mm, ye_ok, out = (
        sem(f"ex_{x}") for x in ("rows_in", "rows_turned", "turned_copied", "gate_summed", "gate_done", "up_summed",
                                 "hidden", "hidden_turned", "hidden_copied", "down_summed", "rows_out", "added"))
    c = Cut(M.scr[:, :])
    XE, XT, GA, H, HT, YE = c(D), c(D, KD), c(D), c(D), c(D, KD), c(D)

    def half(kind, j):
        return E.w[kind][j].rearrange("p (k n) -> p k n", k=KD)

    with nc.Block() as block:
        @block.sync
        def _(sp):
            def load(kind, j, e):
                src = w[kind][bass.ds(e, 1), j, :, :].rearrange("o p n -> (o p) n")
                sp.dma_start(E.w[kind][j], src).then_inc(E.loaded[kind][j], 16)

            with sp.Fori(0, NE - 1) as e:
                for kind, used in (("gate", g_mm), ("up", u_mm), ("down", d_mm)):
                    for j in range(2):
                        sp.wait_ge(used, e * 2 + (j + 1))
                        load(kind, j, e + 1)

        @block.gpsimd
        def _(pool):
            def gather(e):
                if e:
                    pool.wait_ge(xt_mm, 2 * e)
                pool.indirect_dma_start(XE, None, hf_dram, bass.IndirectOffsetOnAxis(E.idx[:, e:e + 1], 0)
                                        ).then_inc(xe_in, 16)
            gather(0)
            gather(1)
            for e in range(NE):
                if e + 2 < NE:
                    gather(e + 2)
                pool.wait_ge(ye_ok, e + 1)
                pool.indirect_dma_start(acc_dram, bass.IndirectOffsetOnAxis(E.idx[:, e:e + 1], 0), YE, None,
                                        compute_op=ALU.add).then_inc(out, 16)
                pool.wait_ge(out, 16 * (e + 1))

        @block.tensor
        def _(pe):
            def turn(src, half):
                for k in range(4 * half, 4 * half + 4):
                    last = nc.tensor.transpose(M.ps[:, 3, k * P:(k + 1) * P], src[:, k * P:(k + 1) * P], M.c("ident"))
                return last

            def turn_hidden(e):
                pe.wait_ge(h_ok, e + 1)
                turn(H, 0)
                turn(H, 1).then_inc(th_mm, 1)

            def product(unit, kind, e, lhs, done, before=lambda j, k: None):
                for j in range(2):
                    pe.wait_ge(E.loaded[kind][j], e * 16 + 16)
                    ww = half(kind, j)
                    for k in range(KD):
                        before(j, k)
                        last = nc.tensor.matmul(M.ps[:, unit, j * 512:(j + 1) * 512], lhsT=lhs[:, k, :],
                                                rhs=ww[:, k, :], start=k == 0, stop=k == KD - 1)
                    last.then_inc(done, 1)

            def gate(e, first=False, second=False):
                pe.wait_ge(xe_in, e * 16 + 16)
                if not first and not second:
                    pe.wait_ge(th_cp, e - 1)
                turn(XE, 0).then_inc(xt_mm, 1)
                turn(XE, 1).then_inc(xt_mm, 1)
                if not first:
                    pe.wait_ge(g_cp, e)

                def before(j, k):
                    if j == 0 and k % 4 == 0:
                        pe.wait_ge(xt_cp, e * 2 + (1 + k // 4))
                    if (j, k) == (1, 0) and not first:
                        turn_hidden(e - 1)
                product(0, "gate", e, XT, g_mm, before)

            def down(e, first=False):
                pe.wait_ge(th_cp, e + 1)
                if not first:
                    pe.wait_ge(ye_ok, e)
                product(2, "down", e, HT, d_mm)

            def up(e, first=False):
                if not first:
                    pe.wait_ge(h_ok, e)
                product(1, "up", e, XT, u_mm)

            gate(0, True)
            up(0, True)
            gate(1, second=True)
            down(0, True)
            up(1)
            with pe.Fori(2, NE) as e:
                gate(e)
                down(e - 1)
                up(e)
            turn_hidden(NE - 1)
            down(NE - 1)

        @block.scalar
        def _(act):
            def turned(e, first=False):
                for j in range(2):
                    act.wait_ge(xt_mm, e * 2 + (1 + j))
                    if not first and j == 0:
                        act.wait_ge(u_mm, e * 2)
                    nc.scalar.activation(XT[:, 4 * j:4 * j + 4, :].rearrange("p k n -> p (k n)"),
                                         M.ps[:, 3, 512 * j:512 * (j + 1)], ACT.Copy).then_inc(xt_cp, 1)

            def silu(e, first=False):
                act.wait_ge(g_mm, e * 2 + 2)
                if not first:
                    act.wait_ge(h_ok, e)
                nc.scalar.activation(GA, M.ps[:, 0, :], ACT.Silu).then_inc(g_cp, 1)

            def hidden(e, first=False):
                act.wait_ge(th_mm, e + 1)
                if not first:
                    act.wait_ge(d_mm, e * 2)
                nc.scalar.activation(HT.rearrange("p k n -> p (k n)"), M.ps[:, 3, :], ACT.Copy).then_inc(th_cp, 1)

            turned(0, True)
            silu(0, True)
            turned(1)
            hidden(0, True)
            silu(1)
            with act.Fori(2, NE) as e:
                turned(e)
                hidden(e - 1)
                silu(e)
            hidden(NE - 1)

        @block.vector
        def _(dve):
            def hid(e, first=False):
                dve.wait_ge(u_mm, e * 2 + 2)
                dve.wait_ge(g_cp, e + 1)
                if not first:
                    dve.wait_ge(th_mm, e)
                nc.vector.tensor_tensor(H, GA, M.ps[:, 1, :], ALU.mult).then_inc(h_ok, 1)

            def rows(e, first=False):
                dve.wait_ge(d_mm, e * 2 + 2)
                if not first:
                    dve.wait_ge(out, e * 16)
                nc.vector.tensor_scalar(YE, M.ps[:, 2, :], E.gates[:, bass.ds(e, 1)], None,
                                        ALU.mult).then_inc(ye_ok, 1)

            hid(0, True)
            rows(0, True)
            hid(1)
            with dve.Fori(2, NE) as e:
                rows(e - 1)
                hid(e)
            rows(NE - 1)


def program(nc, A, out):
    def scratch(name, shape):
        return nc.dram_tensor(name, shape, F32, kind="Internal").ap()

    M, W = Memory(nc), Weights(nc)
    h1, x2, hf, acc = (scratch(n, [T, D]) for n in ("h1_rows", "x2_rows", "ffn_rows", "acc_rows"))
    rw, vt = scratch("rwkv_operands", [2, TT, P, CT * 4 * P]), scratch("rwkv_values", [TT, P, CT * P])
    gate, bonus = scratch("rwkv_gate", [CT, P, T]), scratch("rwkv_bonus", [CT, P, T])

    setup(nc, M, A["par"], A["con"], A["bytes"])
    M.stage_end()
    lower_bounds(nc, M)
    M.stage_end()
    n = 0
    pool_in = [A["pool_in"][g + 4 * j] for g in range(G) for j in range(2)]
    stages = (pool_in, [A["pool_out"][c] for c in range(4)], [A["hgrn_gate"][c] for c in range(4)],
              [A["hgrn_heads"][h] for h in range(HEADS)], [A["hgrn_out"][c] for c in range(4)],
              [A["mem_kv"][0]], [A["mix_in"][c] for c in range(5)], [A["mix_out"][c] for c in range(2)])
    chunks = [c for s in stages for c in s]
    starts = [sum(len(s) for s in stages[:j]) for j in range(len(stages))]

    def ahead(n):
        return [(m, chunks[m]) for m in (n, n + 1) if m < len(chunks) and m not in M.sent]

    norm_transpose(nc, M, W, "norm0", M.p("norm0"), load=A["x"], prefetch=ahead(starts[0]))
    M.stage_end()
    M.sent = {0, 1}
    pool_layer(nc, M, W, starts[0], A["pool_in"], A["pool_grp"], prefetch=ahead(starts[1]))
    M.stage_end()
    M.sent = {starts[1], starts[1] + 1}
    out_projection(nc, M, W, "pool_out", starts[1], M.zt, KI, A["pool_out"], A["x"], prefetch=ahead(starts[2]))
    M.stage_end()
    M.sent = {starts[2], starts[2] + 1}
    norm_transpose(nc, M, W, "norm1", M.p("norm1"), store=h1, squared=True)
    M.stage_end()
    hgrn_gates(nc, M, W, starts[2], A["hgrn_gate"], prefetch=ahead(starts[3]))
    M.stage_end()
    M.sent = {starts[3], starts[3] + 1}
    hgrn_heads(nc, M, W, starts[3], A["hgrn_heads"], prefetch=ahead(starts[4]))
    M.stage_end()
    M.sent = {starts[4], starts[4] + 1}
    out_projection(nc, M, W, "hgrn_out", starts[4], M.zt, KI, A["hgrn_out"], h1, prefetch=ahead(starts[5]))
    M.stage_end()
    M.sent = {starts[5], starts[5] + 1}
    norm_transpose(nc, M, W, "norm_mix", M.p("norm_mix"), squared=True, final=(A["final_g"], x2))
    M.stage_end()
    mix_memory(M)
    memory_keys(nc, M, W, starts[5], A["mem"], A["mem_kv"][0], prefetch=[(starts[6] + 1, chunks[starts[6] + 1])])
    M.stage_end()
    M.sent = {starts[6], starts[6] + 1}
    mixer_projections(nc, M, W, starts[6], A["mix_in"], prefetch=ahead(starts[7]))
    M.stage_end()
    M.sent = {starts[7], starts[7] + 1}
    attention(nc, M)
    M.stage_end()
    conv_norm(nc, M)
    M.stage_end()
    rwkv_common(nc, M, A["rwkv_small"], vt, gate)
    M.stage_end()
    rwkv_directions(nc, M, rw, bonus)
    M.stage_end()
    rwkv_steps(nc, M, rw, vt, A["rwkv_masks"])
    M.stage_end()
    rwkv_finish(nc, M, bonus, gate)
    M.stage_end()
    out_projection(nc, M, W, "mix_out", starts[7], M.ht, KD, A["mix_out"], x2)
    M.stage_end()
    E = ExpertMemory(nc, M)
    w = {k: A["expert_" + k] for k in E.w}
    hf_out, raw_out = nc.alloc_semaphore("ffn_rows_out"), nc.alloc_semaphore("acc_rows_out")
    row_norm(nc, M, "norm_ffn", A["norm_ffn_g"], hf, hf_out, raw=acc, raw_out=raw_out, turn=True,
             prefetch=E.first(w))
    M.stage_end()
    route(nc, M, E, hf_out, raw_out)
    M.stage_end()
    experts(nc, M, E, w, hf, acc)
    M.stage_end()
    result_out = nc.alloc_semaphore("result_out")
    row_norm(nc, M, "final2", A["final_norm_g"], out, result_out, load=acc)
    nc.sync.wait_ge(result_out, 16 * TT)
    M.stage_end()


def by_feature(v):
    return v.reshape(-1, P).T


def by_chunk(w, cols):
    k = w.shape[0] // P
    return np.ascontiguousarray(w.reshape(k, P, -1, cols).transpose(2, 1, 0, 3)).reshape(-1, P, k * cols)


def layout(x):
    f32 = np.float32
    par = np.zeros((P, PAR_N), f32)
    second = {k[:-2]: v for k, v in x.items() if k.endswith("_2")}
    features = {
        "norm0": x["norm_g"][0], "norm1": x["norm_g"][1], "pool_scale": x["pool_scale"],
        "lb0": x["hgrn_lower_bounds"][0], "lb1": x["hgrn_lower_bounds"][1], "hgrn_g": x["hgrn_norm_g"],
        "norm_mix": second["norm_mix_g"], "norm_mem": second["norm_mem_g"], "conv_b": second["conv_b"],
        "conv_g": second["conv_ln_g"], "conv_beta": second["conv_ln_b"], "mu_prev": second["shift_mu"][0, 0],
        "mu_next": second["shift_mu"][0, 1], "w0": second["decay_w0"], "a0": second["iclr_a0"],
        "k_k": second["k_k"], "k_a": second["k_a"], "r_k": second["r_k"], "lnx_g": second["lnx_g"],
        "lnx_b": second["lnx_b"],
    }
    for name, v in features.items():
        at, n = PAR[name]
        par[:, at:at + n] = by_feature(v)
    at, n = PAR["conv_w"]
    par[:, at:at + n] = second["conv_w"][0].reshape(CONV_K, CT, P).transpose(2, 1, 0).reshape(P, n)
    at, n = PAR["router"]
    par[:, at:at + n] = second["w_router"][0].reshape(KD, P, NE).transpose(1, 0, 2).reshape(P, n)
    w = x["hgrn_w_in"][0]
    heads = w[:, 0:3 * DI].reshape(KD, P, 3, HEADS, P).transpose(3, 1, 0, 2, 4)
    arrays = {
        "x": x["x"][0], "mem": second["mem"][0], "par": par, "con": constants(), "bytes": level_masks(),
        "rwkv_masks": rwkv_masks(),
        "pool_in": by_chunk(x["pool_w_in"][0], 512),
        "pool_grp": np.concatenate([by_chunk(g, 512) for g in x["pool_w_grp"][0]]),
        "pool_out": by_chunk(x["pool_w_out"][0], 256),
        "hgrn_gate": by_chunk(w[:, 3 * DI:], 512),
        "hgrn_heads": np.ascontiguousarray(heads).reshape(HEADS, P, KD * 3 * P),
        "hgrn_out": by_chunk(x["hgrn_w_out"][0], 256),
        "mem_kv": by_chunk(np.concatenate([second["w_mk"][0], second["w_mv"][0]], 1), 512),
        "mix_in": by_chunk(second["w_in"][0], 512),
        "mix_out": by_chunk(second["w_out"][0], 512),
        "rwkv_small": np.concatenate([second["decay_up"][0].reshape(P, CT * P),
                                      second["iclr_up"][0].reshape(P, CT * P), second["gate_up"][0]], 1),
        "final_g": x["final_g"].reshape(1, D), "norm_ffn_g": second["norm_ffn_g"].reshape(1, D),
        "final_norm_g": second["final_norm_g"].reshape(1, D),
    }
    for kind in ("gate", "up", "down"):
        e = second["w_e_" + kind][0].reshape(NE, KD, P, 2, 512).transpose(0, 3, 2, 1, 4)
        arrays["expert_" + kind] = np.ascontiguousarray(e).reshape(NE, 2, P, KD * 512)
    return arrays


def kernel(**inputs):
    import concourse.bacc as bacc
    from concourse.bass_utils import run_bass_kernel_spmd

    nc = bacc.Bacc("TRN2", target_bir_lowering=False, num_devices=1)
    arrays = layout({k: np.asarray(v) for k, v in inputs.items()})
    arrays = {f"in_{k}": np.ascontiguousarray(v) for k, v in arrays.items()}
    aps = {k[3:]: nc.dram_tensor(k, v.shape, mybir.dt.from_np(v.dtype), kind="ExternalInput").ap()
           for k, v in arrays.items()}
    out = nc.dram_tensor("out_rows", [T, D], F32, kind="ExternalOutput").ap()
    program(nc, aps, out)
    r = run_bass_kernel_spmd(nc, [arrays], core_ids=[0])
    return np.asarray(r.results[0]["out_rows"]).reshape(1, T, D)
```
